# Optimizing a Trainium2 kernel written in Bass

```python
import jax, jax.numpy as jnp
from jax import lax
import numpy as np

D_MODEL = 1024
BATCH = 1
SEQ = 256
DEPTH = 1

NSA_HEADS = 8
NSA_KV_GROUPS = 2
NSA_HEADS_PER_GROUP = NSA_HEADS // NSA_KV_GROUPS
NSA_HEAD_DIM = 64
CMP_BLOCK = 32
CMP_STRIDE = 16
CMP_RATIO = CMP_BLOCK // CMP_STRIDE
CMP_HIDDEN = 256
SLC_BLOCK = 64
SLC_TOPK = 16
WINDOW = 512
Q_BLOCK = 128
GLA_HEADS = 4
GLA_KEY_DIM = 64
GLA_VAL_DIM = 128
GLA_RANK = 16
GLA_TAU = 16.0
GLA_CHUNK = 64
MOE_GROUPS = 4
MOE_EXPERTS_PER_GROUP = 8
MOE_N_EXPERTS = MOE_GROUPS * MOE_EXPERTS_PER_GROUP
MOE_TOPK = 2
MOE_D_FF = 512

ROPE_THETA = 10000.0
EPS = 1e-6
NEG_INF = -1e30
FORCED_SCORE = 1e4

NSA_Q_W = NSA_HEADS * NSA_HEAD_DIM
NSA_KV_W = NSA_KV_GROUPS * NSA_HEAD_DIM
GLA_QK_W = GLA_HEADS * GLA_KEY_DIM
GLA_V_W = GLA_HEADS * GLA_VAL_DIM
IN_SPLITS = (NSA_Q_W,) + (NSA_KV_W,) * 6 + (3 * NSA_HEADS, GLA_QK_W, GLA_QK_W, GLA_V_W, GLA_RANK, GLA_V_W, D_MODEL, D_MODEL)
IN_WIDTH = sum(IN_SPLITS)


def rms_norm(x, g):
    xf = x.astype(jnp.float32)
    y = xf * lax.rsqrt(jnp.mean(xf * xf, axis=-1, keepdims=True) + EPS)
    return (y * g.astype(jnp.float32)).astype(x.dtype)

def rope(x, pos):
    half = x.shape[-1] // 2
    inv = 1.0 / (ROPE_THETA ** (jnp.arange(half, dtype=jnp.float32) / half))
    ang = pos.astype(jnp.float32)[..., None] * inv
    cos, sin = jnp.cos(ang), jnp.sin(ang)
    x1 = x[..., :half].astype(jnp.float32)
    x2 = x[..., half:].astype(jnp.float32)
    return jnp.concatenate([x1 * cos - x2 * sin, x2 * cos + x1 * sin], axis=-1).astype(x.dtype)

def _heads(t, n, dh):
    b, s, _ = t.shape
    return t.reshape(b, s, n, dh).transpose(0, 2, 1, 3)

def compress_blocks(t, pos_emb, w1, b1, w2, b2):
    bsz, g, seq, dh = t.shape
    chunks = t.reshape(bsz, g, seq // CMP_STRIDE, CMP_STRIDE, dh)
    n_cmp = seq // CMP_STRIDE - CMP_RATIO + 1
    blocks = jnp.concatenate([chunks[:, :, m:m + n_cmp] for m in range(CMP_RATIO)], axis=3)
    blocks = blocks + pos_emb
    flat = blocks.reshape(bsz, g, n_cmp, CMP_BLOCK * dh)
    return jax.nn.gelu(flat @ w1 + b1) @ w2 + b2

def cmp_to_slc_overlap(n_cmp, n_slc):
    c0 = CMP_STRIDE * jnp.arange(n_cmp)[:, None]
    s0 = SLC_BLOCK * jnp.arange(n_slc)[None, :]
    ov = jnp.clip(jnp.minimum(c0 + CMP_BLOCK, s0 + SLC_BLOCK) - jnp.maximum(c0, s0), 0, None)
    return ov.astype(jnp.float32) / CMP_BLOCK

def nsa_attention(q, k_c, v_c, k_s, v_s, k_w, v_w, gate_logits, positions,
                  cmp_pos_k, cmp_w1_k, cmp_b1_k, cmp_w2_k, cmp_b2_k,
                  cmp_pos_v, cmp_w1_v, cmp_b1_v, cmp_w2_v, cmp_b2_v):
    f32 = jnp.float32
    bsz, seq, _ = q.shape
    G, hpg, dh = NSA_KV_GROUPS, NSA_HEADS_PER_GROUP, NSA_HEAD_DIM
    pos_h = positions[:, None, :]
    q = (rope(_heads(q, NSA_HEADS, dh), pos_h) * dh ** -0.5).reshape(bsz, G, hpg, seq, dh)
    k_cmp = compress_blocks(_heads(k_c, G, dh), cmp_pos_k, cmp_w1_k, cmp_b1_k, cmp_w2_k, cmp_b2_k)
    v_cmp = compress_blocks(_heads(v_c, G, dh), cmp_pos_v, cmp_w1_v, cmp_b1_v, cmp_w2_v, cmp_b2_v)
    n_cmp = k_cmp.shape[2]
    cmp_end = CMP_STRIDE * jnp.arange(n_cmp) + CMP_BLOCK - 1
    k_cmp = rope(k_cmp, jnp.take(positions, cmp_end, axis=1)[:, None, :])
    n_slc = seq // SLC_BLOCK
    top_n = min(SLC_TOPK, n_slc)
    overlap = cmp_to_slc_overlap(n_cmp, n_slc)
    k_blocks = rope(_heads(k_s, G, dh), pos_h).reshape(bsz, G, n_slc, SLC_BLOCK, dh)
    v_blocks = _heads(v_s, G, dh).reshape(bsz, G, n_slc, SLC_BLOCK, dh)
    pad = ((0, 0), (0, 0), (WINDOW, 0), (0, 0))
    k_win = jnp.pad(rope(_heads(k_w, G, dh), pos_h), pad)
    v_win = jnp.pad(_heads(v_w, G, dh), pad)
    gates = jax.nn.sigmoid(gate_logits.astype(f32)).reshape(bsz, seq, NSA_HEADS, 3)
    gates = gates.transpose(0, 2, 1, 3).reshape(bsz, G, hpg, seq, 3)
    b_idx = jnp.arange(bsz)[:, None, None, None]
    g_idx = jnp.arange(G)[None, :, None, None]
    blk_ids = jnp.arange(n_slc)

    def query_block(c):
        q0 = c * Q_BLOCK
        t_idx = q0 + jnp.arange(Q_BLOCK)
        qc = lax.dynamic_slice_in_dim(q, q0, Q_BLOCK, axis=3)
        gc = lax.dynamic_slice_in_dim(gates, q0, Q_BLOCK, axis=3)
        s = jnp.einsum('bghqd,bgnd->bghqn', qc, k_cmp).astype(f32)
        cmp_ok = cmp_end[None, :] <= t_idx[:, None]
        p_cmp = jax.nn.softmax(jnp.where(cmp_ok, s, NEG_INF), axis=-1) * cmp_ok
        o_cmp = jnp.einsum('bghqn,bgnd->bghqd', p_cmp.astype(v_cmp.dtype), v_cmp)
        imp = jnp.einsum('bghqn,nj->bgqj', p_cmp, overlap)
        cur = t_idx // SLC_BLOCK
        forced = (blk_ids[None, :] == 0) | (blk_ids[None, :] == cur[:, None]) | (blk_ids[None, :] == cur[:, None] - 1)
        imp = jnp.where(forced, FORCED_SCORE, imp)
        imp = jnp.where(blk_ids[None, :] <= cur[:, None], imp, NEG_INF)
        _, sel = lax.top_k(imp, top_n)
        k_sel = k_blocks[b_idx, g_idx, sel].reshape(bsz, G, Q_BLOCK, top_n * SLC_BLOCK, dh)
        v_sel = v_blocks[b_idx, g_idx, sel].reshape(bsz, G, Q_BLOCK, top_n * SLC_BLOCK, dh)
        key_pos = (sel[..., None] * SLC_BLOCK + jnp.arange(SLC_BLOCK)).reshape(bsz, G, Q_BLOCK, top_n * SLC_BLOCK)
        sel_ok = (key_pos <= t_idx[:, None])[:, :, None]
        s = jnp.einsum('bghqd,bgqkd->bghqk', qc, k_sel).astype(f32)
        p = jax.nn.softmax(jnp.where(sel_ok, s, NEG_INF), axis=-1)
        o_slc = jnp.einsum('bghqk,bgqkd->bghqd', p.astype(v_sel.dtype), v_sel)
        kw = lax.dynamic_slice_in_dim(k_win, q0, Q_BLOCK + WINDOW, axis=2)
        vw = lax.dynamic_slice_in_dim(v_win, q0, Q_BLOCK + WINDOW, axis=2)
        kpos = q0 - WINDOW + jnp.arange(Q_BLOCK + WINDOW)
        win_ok = (kpos[None, :] >= 0) & (kpos[None, :] <= t_idx[:, None]) & (kpos[None, :] > t_idx[:, None] - WINDOW)
        s = jnp.einsum('bghqd,bgkd->bghqk', qc, kw).astype(f32)
        p = jax.nn.softmax(jnp.where(win_ok, s, NEG_INF), axis=-1)
        o_win = jnp.einsum('bghqk,bgkd->bghqd', p.astype(vw.dtype), vw)
        o = gc[..., 0:1] * o_cmp + gc[..., 1:2] * o_slc + gc[..., 2:3] * o_win
        return o.astype(q.dtype)

    out = lax.map(query_block, jnp.arange(seq // Q_BLOCK))
    return out.transpose(1, 0, 4, 2, 3, 5).reshape(bsz, seq, NSA_HEADS * dh)

def gla_attention(q, k, v, a_low, r, w_a2, b_a, norm_g):
    f32 = jnp.float32
    bsz, seq, _ = q.shape
    H, dk, dv, C = GLA_HEADS, GLA_KEY_DIM, GLA_VAL_DIM, GLA_CHUNK
    q = _heads(q, H, dk).astype(f32) * dk ** -0.5
    k = _heads(k, H, dk).astype(f32)
    v = _heads(v, H, dv).astype(f32)
    log_a = _heads(jax.nn.log_sigmoid((a_low @ w_a2 + b_a).astype(f32)) / GLA_TAU, H, dk)
    nc = seq // C

    def to_chunks(t):
        return t.reshape(bsz, H, nc, C, t.shape[-1]).transpose(2, 0, 1, 3, 4)

    causal = jnp.tril(jnp.ones((C, C), dtype=bool))[:, :, None]

    def step(state, xs):
        qc, kc, vc, lac = xs
        b = jnp.cumsum(lac, axis=2)
        o_inter = jnp.einsum('bhtd,bhde->bhte', qc * jnp.exp(b), state)
        diff = b[:, :, :, None, :] - b[:, :, None, :, :]
        decay = jnp.where(causal, jnp.exp(jnp.where(causal, diff, 0.0)), 0.0)
        attn = jnp.einsum('bhtd,bhsd,bhtsd->bhts', qc, kc, decay)
        o_intra = jnp.einsum('bhts,bhse->bhte', attn, vc)
        b_last = b[:, :, -1, :]
        k_dec = kc * jnp.exp(b_last[:, :, None, :] - b)
        state = jnp.exp(b_last)[..., None] * state + jnp.einsum('bhsd,bhse->bhde', k_dec, vc)
        return state, o_inter + o_intra

    state0 = jnp.zeros((bsz, H, dk, dv), f32)
    _, o = lax.scan(step, state0, (to_chunks(q), to_chunks(k), to_chunks(v), to_chunks(log_a)))
    o = o.transpose(1, 2, 0, 3, 4).reshape(bsz, H, seq, dv)
    o = o * lax.rsqrt(jnp.mean(o * o, axis=-1, keepdims=True) + EPS)
    o = o.transpose(0, 2, 1, 3).reshape(bsz, seq, H * dv) * norm_g.astype(f32)
    return (o * jax.nn.silu(r.astype(f32))).astype(r.dtype)

def hybrid_mixer(u, positions, w_in,
                 cmp_pos_k, cmp_w1_k, cmp_b1_k, cmp_w2_k, cmp_b2_k,
                 cmp_pos_v, cmp_w1_v, cmp_b1_v, cmp_w2_v, cmp_b2_v,
                 gla_w_a2, gla_b_a, gla_norm_g, w_proj_nsa, w_proj_gla, w_out):
    z = u @ w_in
    (nsa_q, k_c, v_c, k_s, v_s, k_w, v_w, nsa_g,
     g_q, g_k, g_v, g_a, g_r, m_a, m_b) = jnp.split(z, np.cumsum(IN_SPLITS)[:-1].tolist(), axis=-1)
    y_a = nsa_attention(nsa_q, k_c, v_c, k_s, v_s, k_w, v_w, nsa_g, positions,
                        cmp_pos_k, cmp_w1_k, cmp_b1_k, cmp_w2_k, cmp_b2_k,
                        cmp_pos_v, cmp_w1_v, cmp_b1_v, cmp_w2_v, cmp_b2_v) @ w_proj_nsa
    y_b = gla_attention(g_q, g_k, g_v, g_a, g_r, gla_w_a2, gla_b_a, gla_norm_g) @ w_proj_gla
    mixed = jax.nn.sigmoid(m_a) * y_a + jax.nn.sigmoid(m_b) * y_b
    return mixed @ w_out

def hier_moe(v, w_grp, b_grp, w_exp, b_exp, w_gate, w_up, w_down):
    f32 = jnp.float32
    bsz, seq, d = v.shape
    vt = v.reshape(-1, d)
    grp_prob = jax.nn.softmax((vt @ w_grp + b_grp).astype(f32), axis=-1)
    p_grp, g_sel = lax.top_k(grp_prob, 1)
    exp_logits = (vt @ w_exp + b_exp).astype(f32).reshape(-1, MOE_GROUPS, MOE_EXPERTS_PER_GROUP)
    in_grp = jnp.take_along_axis(exp_logits, g_sel[:, :, None], axis=1)[:, 0]
    p_in, e_sel = lax.top_k(jax.nn.softmax(in_grp, axis=-1), MOE_TOPK)
    w = p_grp * p_in / jnp.sum(p_in, axis=-1, keepdims=True)
    expert_id = g_sel * MOE_EXPERTS_PER_GROUP + e_sel
    combine = jnp.einsum('tk,tke->te', w, jax.nn.one_hot(expert_id, MOE_N_EXPERTS, dtype=f32))
    y = jnp.zeros(vt.shape, f32)
    for e in range(MOE_N_EXPERTS):
        hdn = jax.nn.silu(vt @ w_gate[e]) * (vt @ w_up[e])
        y = y + (combine[:, e:e + 1].astype(hdn.dtype) * hdn) @ w_down[e]
    return y.reshape(bsz, seq, d).astype(v.dtype)

def first_inputs(seed: int = 0) -> dict:
    key = jax.random.key(seed)
    ks = jax.random.split(key, 32)
    f32 = jnp.float32
    L, D, dh = DEPTH, D_MODEL, NSA_HEAD_DIM

    def nrm(k, shape, scale):
        return jax.random.normal(k, shape, f32) * scale

    start = jax.random.randint(ks[1], (BATCH,), 0, 1024)
    positions = (start[:, None] + jnp.arange(SEQ)[None, :]).astype(jnp.int32)
    return {
        "x": nrm(ks[0], (BATCH, SEQ, D), 1.0),
        "positions": positions,
        "g_mix": 1.0 + nrm(ks[2], (L, D), 0.02),
        "w_in": nrm(ks[3], (L, D, IN_WIDTH), D ** -0.5),
        "cmp_pos_k": nrm(ks[4], (L, CMP_BLOCK, dh), 0.02),
        "cmp_w1_k": nrm(ks[5], (L, CMP_BLOCK * dh, CMP_HIDDEN), (CMP_BLOCK * dh) ** -0.5),
        "cmp_b1_k": nrm(ks[6], (L, CMP_HIDDEN), 0.01),
        "cmp_w2_k": nrm(ks[7], (L, CMP_HIDDEN, dh), CMP_HIDDEN ** -0.5),
        "cmp_b2_k": nrm(ks[8], (L, dh), 0.01),
        "cmp_pos_v": nrm(ks[9], (L, CMP_BLOCK, dh), 0.02),
        "cmp_w1_v": nrm(ks[10], (L, CMP_BLOCK * dh, CMP_HIDDEN), (CMP_BLOCK * dh) ** -0.5),
        "cmp_b1_v": nrm(ks[11], (L, CMP_HIDDEN), 0.01),
        "cmp_w2_v": nrm(ks[12], (L, CMP_HIDDEN, dh), CMP_HIDDEN ** -0.5),
        "cmp_b2_v": nrm(ks[13], (L, dh), 0.01),
        "gla_w_a2": nrm(ks[14], (L, GLA_RANK, GLA_QK_W), GLA_RANK ** -0.5),
        "gla_b_a": nrm(ks[15], (L, GLA_QK_W), 0.1),
        "gla_norm_g": 1.0 + nrm(ks[16], (L, GLA_V_W), 0.02),
        "w_proj_nsa": nrm(ks[17], (L, NSA_Q_W, D), NSA_Q_W ** -0.5),
        "w_proj_gla": nrm(ks[18], (L, GLA_V_W, D), GLA_V_W ** -0.5),
        "w_out": nrm(ks[19], (L, D, D), D ** -0.5),
        "g_ffn": 1.0 + nrm(ks[20], (L, D), 0.02),
        "w_grp": nrm(ks[21], (L, D, MOE_GROUPS), D ** -0.5),
        "b_grp": nrm(ks[22], (L, MOE_GROUPS), 0.01),
        "w_exp": nrm(ks[23], (L, D, MOE_N_EXPERTS), D ** -0.5),
        "b_exp": nrm(ks[24], (L, MOE_N_EXPERTS), 0.01),
        "w_gate": nrm(ks[25], (L, MOE_N_EXPERTS, D, MOE_D_FF), D ** -0.5),
        "w_up": nrm(ks[26], (L, MOE_N_EXPERTS, D, MOE_D_FF), D ** -0.5),
        "w_down": nrm(ks[27], (L, MOE_N_EXPERTS, MOE_D_FF, D), MOE_D_FF ** -0.5),
        "g_final": 1.0 + nrm(ks[28], (D,), 0.02),
    }

def first_block(x, positions, g_mix, w_in,
              cmp_pos_k, cmp_w1_k, cmp_b1_k, cmp_w2_k, cmp_b2_k,
              cmp_pos_v, cmp_w1_v, cmp_b1_v, cmp_w2_v, cmp_b2_v,
              gla_w_a2, gla_b_a, gla_norm_g, w_proj_nsa, w_proj_gla, w_out,
              g_ffn, w_grp, b_grp, w_exp, b_exp, w_gate, w_up, w_down, g_final):
    h = x
    for layer in range(DEPTH):
        u = rms_norm(h, g_mix[layer])
        h = h + hybrid_mixer(u, positions, w_in[layer],
                             cmp_pos_k[layer], cmp_w1_k[layer], cmp_b1_k[layer], cmp_w2_k[layer], cmp_b2_k[layer],
                             cmp_pos_v[layer], cmp_w1_v[layer], cmp_b1_v[layer], cmp_w2_v[layer], cmp_b2_v[layer],
                             gla_w_a2[layer], gla_b_a[layer], gla_norm_g[layer],
                             w_proj_nsa[layer], w_proj_gla[layer], w_out[layer])
        h = h + hier_moe(rms_norm(h, g_ffn[layer]), w_grp[layer], b_grp[layer], w_exp[layer], b_exp[layer],
                         w_gate[layer], w_up[layer], w_down[layer])
    return rms_norm(h, g_final)


DEPTH_2 = 2

GRID_W = 64
CTX_LEN = 256
NORM_EPS = 1e-6
HEAD_DIM = 64

A_HEADS = 8
A_KV_HEADS = 2
A_WINDOW = 128
A_BLOCK = 128
B_HEADS = 8
B_Q_LORA = 384
B_KV_LORA = 256
B_NOPE = 64
B_ROPE = 32
B_V = 64
B_BLOCK = 128
C_HEADS = 16
C_KH = 8
C_KW = 16

A_WIDTH = A_HEADS * HEAD_DIM
A_KV_WIDTH = A_KV_HEADS * HEAD_DIM
B_WIDTH = B_HEADS * B_V
AB_MIX = A_WIDTH + B_WIDTH
AB_SPLITS = (
    A_WIDTH,
    A_WIDTH + A_KV_WIDTH,
    A_WIDTH + 2 * A_KV_WIDTH,
    2 * A_WIDTH + 2 * A_KV_WIDTH,
    2 * A_WIDTH + 2 * A_KV_WIDTH + B_Q_LORA,
    2 * A_WIDTH + 2 * A_KV_WIDTH + B_Q_LORA + B_KV_LORA,
    2 * A_WIDTH + 2 * A_KV_WIDTH + B_Q_LORA + B_KV_LORA + B_ROPE,
)
AB_IN = 2 * A_WIDTH + 2 * A_KV_WIDTH + B_Q_LORA + B_KV_LORA + B_ROPE + B_WIDTH
C_WIDTH = C_HEADS * HEAD_DIM
C_IN = 4 * C_WIDTH
N_EVEN = (DEPTH_2 + 1) // 2
N_ODD = DEPTH_2 // 2


def rms_norm_2(x, g):
    xf = x.astype(jnp.float32)
    y = xf * lax.rsqrt(jnp.mean(xf * xf, axis=-1, keepdims=True) + NORM_EPS)
    return (y * g.astype(jnp.float32)).astype(x.dtype)

def axial_rope_angles(n_tokens, rot_dim):
    t = jnp.arange(n_tokens, dtype=jnp.int32)
    row = (t // GRID_W).astype(jnp.float32)
    col = (t % GRID_W).astype(jnp.float32)
    pairs_per_axis = rot_dim // 4
    inv = ROPE_THETA ** (-jnp.arange(pairs_per_axis, dtype=jnp.float32) / pairs_per_axis)
    ang = jnp.concatenate([row[:, None] * inv, col[:, None] * inv], axis=-1)
    return jnp.cos(ang), jnp.sin(ang)

def apply_rope(x, cos, sin):
    d = x.shape[-1]
    xr = x.reshape(x.shape[:-1] + (d // 2, 2)).astype(jnp.float32)
    x1, x2 = xr[..., 0], xr[..., 1]
    out = jnp.stack([x1 * cos - x2 * sin, x1 * sin + x2 * cos], axis=-1)
    return out.reshape(x.shape).astype(x.dtype)

def gqa_sink_dense(q, k, v, sink):
    bn, n, _, d = q.shape
    grp = A_HEADS // A_KV_HEADS
    qg = q.reshape(bn, n, A_KV_HEADS, grp, d)
    s = jnp.einsum('bqhgd,bkhd->bhgqk', qg, k).astype(jnp.float32) * (d ** -0.5)
    s_sink = jnp.broadcast_to(sink.astype(jnp.float32).reshape(A_KV_HEADS, grp)[None, :, :, None, None], s.shape[:-1] + (1,))
    p = jax.nn.softmax(jnp.concatenate([s, s_sink], axis=-1), axis=-1)[..., :-1].astype(v.dtype)
    return jnp.einsum('bhgqk,bkhd->bqhgd', p, v).reshape(bn, n, A_HEADS * d)

def window_gqa_latent(q, k, v, kc, vc, sink):
    bn, s_len, _, d = q.shape
    nb = s_len // A_BLOCK
    grp = A_HEADS // A_KV_HEADS
    scale = d ** -0.5
    pad = [(0, 0), (A_BLOCK, A_BLOCK), (0, 0), (0, 0)]

    def band(t):
        tb = jnp.pad(t, pad).reshape(bn, nb + 2, A_BLOCK, A_KV_HEADS, d)
        w = jnp.concatenate([tb[:, :-2], tb[:, 1:-1], tb[:, 2:]], axis=2)
        return jnp.moveaxis(w, 1, 0)

    kw, vw = band(k), band(v)
    qb = jnp.moveaxis(q.reshape(bn, nb, A_BLOCK, A_KV_HEADS, grp, d), 1, 0)
    qi = jnp.arange(A_BLOCK)[:, None]
    kj = jnp.arange(3 * A_BLOCK)[None, :] - A_BLOCK
    band_ok = jnp.abs(kj - qi) <= A_WINDOW
    sink_g = sink.astype(jnp.float32).reshape(A_KV_HEADS, grp)[None, :, :, None, None]

    def block(args):
        n, qn, kn, vn = args
        kpos = n * A_BLOCK + kj
        mask = band_ok & (kpos >= 0) & (kpos < s_len)
        s_loc = jnp.einsum('bqhgd,bkhd->bhgqk', qn, kn).astype(jnp.float32) * scale
        s_loc = jnp.where(mask, s_loc, -jnp.inf)
        s_ctx = jnp.einsum('bqhgd,blhd->bhgql', qn, kc).astype(jnp.float32) * scale
        s_sink = jnp.broadcast_to(sink_g, s_loc.shape[:-1] + (1,))
        p = jax.nn.softmax(jnp.concatenate([s_loc, s_ctx, s_sink], axis=-1), axis=-1)
        p_loc = p[..., :3 * A_BLOCK].astype(vn.dtype)
        p_ctx = p[..., 3 * A_BLOCK:-1].astype(vc.dtype)
        return (jnp.einsum('bhgqk,bkhd->bqhgd', p_loc, vn)
                + jnp.einsum('bhgql,blhd->bqhgd', p_ctx, vc))

    o = lax.map(block, (jnp.arange(nb), qb, kw, vw))
    return jnp.moveaxis(o, 0, 1).reshape(bn, s_len, A_HEADS * d)

def mla_dense(qn, qr, kn, kr, v):
    scale = (B_NOPE + B_ROPE) ** -0.5
    s = (jnp.einsum('bqhd,bkhd->bhqk', qn, kn) + jnp.einsum('bqhr,bkr->bhqk', qr, kr)).astype(jnp.float32) * scale
    p = jax.nn.softmax(s, axis=-1).astype(v.dtype)
    return jnp.einsum('bhqk,bkhd->bqhd', p, v)

def mla_latent(qn, qr, kn, kr, v, kn_c, kr_c, v_c):
    bn, s_len = qn.shape[0], qn.shape[1]
    nb = s_len // B_BLOCK
    k_n = jnp.concatenate([kn_c, kn], axis=1)
    k_r = jnp.concatenate([kr_c, kr], axis=1)
    v_all = jnp.concatenate([v_c, v], axis=1)
    qn_b = jnp.moveaxis(qn.reshape(bn, nb, B_BLOCK, B_HEADS, B_NOPE), 1, 0)
    qr_b = jnp.moveaxis(qr.reshape(bn, nb, B_BLOCK, B_HEADS, B_ROPE), 1, 0)
    o = lax.map(lambda a: mla_dense(a[0], a[1], k_n, k_r, v_all), (qn_b, qr_b))
    return jnp.moveaxis(o, 0, 1).reshape(bn, s_len, B_HEADS * B_V)

def ab_project(u, in_w, qn_g, w_uq, kvn_g, w_ukv):
    bn, n, _ = u.shape
    p = u @ in_w
    qa, ka, va, za, cq, ckv, kr, zb = jnp.split(p, AB_SPLITS, axis=-1)
    qa = qa.reshape(bn, n, A_HEADS, HEAD_DIM)
    ka = ka.reshape(bn, n, A_KV_HEADS, HEAD_DIM)
    va = va.reshape(bn, n, A_KV_HEADS, HEAD_DIM)
    qb = (rms_norm_2(cq, qn_g) @ w_uq).reshape(bn, n, B_HEADS, B_NOPE + B_ROPE)
    kvb = (rms_norm_2(ckv, kvn_g) @ w_ukv).reshape(bn, n, B_HEADS, B_NOPE + B_V)
    return (qa, ka, va, za, qb[..., :B_NOPE], qb[..., B_NOPE:],
            kvb[..., :B_NOPE], kr, kvb[..., B_NOPE:], zb)

def ab_mixer(u, uc, in_w, out_w, sink, qn_g, w_uq, kvn_g, w_ukv, rope_a, rope_b, need_ctx):
    qa, ka, va, za, qbn, qbr, kbn, kbr, vb, zb = ab_project(u, in_w, qn_g, w_uq, kvn_g, w_ukv)
    qa_c, ka_c, va_c, za_c, qbn_c, qbr_c, kbn_c, kbr_c, vb_c, zb_c = ab_project(uc, in_w, qn_g, w_uq, kvn_g, w_ukv)
    cos_a, sin_a = rope_a
    cos_b, sin_b = rope_b
    qa = apply_rope(qa, cos_a[:, None, :], sin_a[:, None, :])
    ka = apply_rope(ka, cos_a[:, None, :], sin_a[:, None, :])
    qbr = apply_rope(qbr, cos_b[:, None, :], sin_b[:, None, :])
    kbr = apply_rope(kbr, cos_b, sin_b)
    oa = window_gqa_latent(qa, ka, va, ka_c, va_c, sink)
    ob = mla_latent(qbn, qbr, kbn, kbr, vb, kbn_c, kbr_c, vb_c)
    y = jnp.concatenate([oa * jax.nn.silu(za), ob * jax.nn.silu(zb)], axis=-1) @ out_w
    if not need_ctx:
        return y, None
    bn, n = uc.shape[0], uc.shape[1]
    oa_c = gqa_sink_dense(qa_c, ka_c, va_c, sink)
    ob_c = mla_dense(qbn_c, qbr_c, kbn_c, kbr_c, vb_c).reshape(bn, n, B_WIDTH)
    yc = jnp.concatenate([oa_c * jax.nn.silu(za_c), ob_c * jax.nn.silu(zb_c)], axis=-1) @ out_w
    return y, yc

def mha_dense(q, k, v):
    bn, n, h, d = q.shape
    s = jnp.einsum('bqhd,bkhd->bhqk', q, k).astype(jnp.float32) * (d ** -0.5)
    p = jax.nn.softmax(s, axis=-1).astype(v.dtype)
    return jnp.einsum('bhqk,bkhd->bqhd', p, v).reshape(bn, n, h * d)

def neighbourhood_latent(q, k, v, kc, vc, rpb):
    bn, s_len, h, d = q.shape
    rows = s_len // GRID_W
    kh = min(C_KH, rows)
    scale = d ** -0.5
    qg = jnp.moveaxis(q.reshape(bn, rows, GRID_W, h, d), 1, 0)
    kg = k.reshape(bn, rows, GRID_W, h, d)
    vg = v.reshape(bn, rows, GRID_W, h, d)
    col = jnp.arange(GRID_W)
    cs = jnp.clip(col - C_KW // 2, 0, GRID_W - C_KW)
    col_ok = (col[None, :] >= cs[:, None]) & (col[None, :] < cs[:, None] + C_KW)
    col_idx = jnp.clip(col[None, :] - col[:, None] + (C_KW - 1), 0, 2 * C_KW - 2)
    rpb_col = rpb[:, :, col_idx]
    mask = jnp.broadcast_to(col_ok[:, None, :], (GRID_W, kh, GRID_W)).reshape(GRID_W, kh * GRID_W)

    def row_block(args):
        r, qr = args
        rs = jnp.clip(r - kh // 2, 0, rows - kh)
        kr = lax.dynamic_slice_in_dim(kg, rs, kh, axis=1).reshape(bn, kh * GRID_W, h, d)
        vr = lax.dynamic_slice_in_dim(vg, rs, kh, axis=1).reshape(bn, kh * GRID_W, h, d)
        row_idx = rs + jnp.arange(kh) - r + (C_KH - 1)
        bias = jnp.take(rpb_col, row_idx, axis=1)
        bias = jnp.transpose(bias, (0, 2, 1, 3)).reshape(h, GRID_W, kh * GRID_W)
        s_loc = jnp.einsum('bqhd,bkhd->bhqk', qr, kr).astype(jnp.float32) * scale + bias.astype(jnp.float32)
        s_loc = jnp.where(mask, s_loc, -jnp.inf)
        s_ctx = jnp.einsum('bqhd,blhd->bhql', qr, kc).astype(jnp.float32) * scale
        p = jax.nn.softmax(jnp.concatenate([s_loc, s_ctx], axis=-1), axis=-1)
        p_loc = p[..., :kh * GRID_W].astype(vr.dtype)
        p_ctx = p[..., kh * GRID_W:].astype(vc.dtype)
        return jnp.einsum('bhqk,bkhd->bqhd', p_loc, vr) + jnp.einsum('bhql,blhd->bqhd', p_ctx, vc)

    o = lax.map(row_block, (jnp.arange(rows), qg))
    return jnp.moveaxis(o, 0, 1).reshape(bn, s_len, h * d)

def c_mixer(u, uc, in_w, out_w, rpb, need_ctx):
    def proj(t):
        bn, n, _ = t.shape
        q, k, v, z = jnp.split(t @ in_w, 4, axis=-1)
        shp = (bn, n, C_HEADS, HEAD_DIM)
        return q.reshape(shp), k.reshape(shp), v.reshape(shp), z
    q, k, v, z = proj(u)
    q_c, k_c, v_c, z_c = proj(uc)
    o = neighbourhood_latent(q, k, v, k_c, v_c, rpb)
    y = (o * jax.nn.silu(z)) @ out_w
    if not need_ctx:
        return y, None
    yc = (mha_dense(q_c, k_c, v_c) * jax.nn.silu(z_c)) @ out_w
    return y, yc

def second_inputs(seed: int = 0) -> dict:
    key = jax.random.key(seed)
    ks = jax.random.split(key, 20)
    f32 = jnp.float32

    def w(k, shape, fan_in, gain=1.0):
        return jax.random.normal(k, shape, f32) * (gain * fan_in ** -0.5)

    def gain(k, shape):
        return 1.0 + 0.05 * jax.random.normal(k, shape, f32)

    return {
        "x": jax.random.normal(ks[0], (BATCH, SEQ, D_MODEL), f32),
        "c": jax.random.normal(ks[1], (BATCH, D_MODEL), f32),
        "ctx": jax.random.normal(ks[2], (BATCH, CTX_LEN, D_MODEL), f32),
        "c_ctx": jax.random.normal(ks[3], (D_MODEL,), f32),
        "ada_w": w(ks[4], (DEPTH_2, D_MODEL, 3 * D_MODEL), D_MODEL, 0.5),
        "ada_b": 0.02 * jax.random.normal(ks[5], (DEPTH_2, 3 * D_MODEL), f32),
        "norm_g": gain(ks[6], (DEPTH_2, D_MODEL)),
        "ab_in_w": w(ks[7], (N_EVEN, D_MODEL, AB_IN), D_MODEL),
        "ab_out_w": w(ks[8], (N_EVEN, AB_MIX, D_MODEL), AB_MIX),
        "a_sink": jax.random.normal(ks[9], (N_EVEN, A_HEADS), f32),
        "b_q_norm_g": gain(ks[10], (N_EVEN, B_Q_LORA)),
        "b_w_uq": w(ks[11], (N_EVEN, B_Q_LORA, B_HEADS * (B_NOPE + B_ROPE)), B_Q_LORA),
        "b_kv_norm_g": gain(ks[12], (N_EVEN, B_KV_LORA)),
        "b_w_ukv": w(ks[13], (N_EVEN, B_KV_LORA, B_HEADS * (B_NOPE + B_V)), B_KV_LORA),
        "c_in_w": w(ks[14], (N_ODD, D_MODEL, C_IN), D_MODEL),
        "c_out_w": w(ks[15], (N_ODD, C_WIDTH, D_MODEL), C_WIDTH),
        "c_rpb": 0.5 * jax.random.normal(ks[16], (N_ODD, C_HEADS, 2 * C_KH - 1, 2 * C_KW - 1), f32),
        "final_g": gain(ks[17], (D_MODEL,)),
    }

def second_block(x, c, ctx, c_ctx, ada_w, ada_b, norm_g, ab_in_w, ab_out_w, a_sink,
              b_q_norm_g, b_w_uq, b_kv_norm_g, b_w_ukv, c_in_w, c_out_w, c_rpb, final_g):
    n_lat = x.shape[1]
    rope_a = axial_rope_angles(n_lat, HEAD_DIM)
    rope_b = axial_rope_angles(n_lat, B_ROPE)
    sc = jax.nn.silu(c)
    sc_ctx = jax.nn.silu(c_ctx)
    h, hc = x, ctx
    for layer in range(DEPTH_2):
        last = layer == DEPTH_2 - 1
        mod = sc @ ada_w[layer] + ada_b[layer]
        shift, scale, gate = jnp.split(mod[:, None, :], 3, axis=-1)
        mod_c = sc_ctx @ ada_w[layer] + ada_b[layer]
        shift_c, scale_c, gate_c = jnp.split(mod_c, 3, axis=-1)
        u = rms_norm_2(h, norm_g[layer]) * (1 + scale) + shift
        uc = rms_norm_2(hc, norm_g[layer]) * (1 + scale_c) + shift_c
        if layer % 2 == 0:
            i = layer // 2
            y, yc = ab_mixer(u, uc, ab_in_w[i], ab_out_w[i], a_sink[i], b_q_norm_g[i], b_w_uq[i],
                             b_kv_norm_g[i], b_w_ukv[i], rope_a, rope_b, not last)
        else:
            i = layer // 2
            y, yc = c_mixer(u, uc, c_in_w[i], c_out_w[i], c_rpb[i], not last)
        h = h + gate * y
        if not last:
            hc = hc + gate_c * yc
    return rms_norm_2(h, final_g)


def setup_inputs(seed=0):
    out = dict(first_inputs(seed))
    for name, value in second_inputs(seed + 1).items():
        if name != "x":
            out[name + "_2"] = value
    return out


def reference(
    x, positions, g_mix, w_in, cmp_pos_k, cmp_w1_k, cmp_b1_k, cmp_w2_k, cmp_b2_k, cmp_pos_v,
    cmp_w1_v, cmp_b1_v, cmp_w2_v, cmp_b2_v, gla_w_a2, gla_b_a, gla_norm_g, w_proj_nsa,
    w_proj_gla, w_out, g_ffn, w_grp, b_grp, w_exp, b_exp, w_gate, w_up, w_down, g_final, c_2,
    ctx_2, c_ctx_2, ada_w_2, ada_b_2, norm_g_2, ab_in_w_2, ab_out_w_2, a_sink_2, b_q_norm_g_2,
    b_w_uq_2, b_kv_norm_g_2, b_w_ukv_2, c_in_w_2, c_out_w_2, c_rpb_2, final_g_2,
):
    x = first_block(
        x, positions, g_mix, w_in, cmp_pos_k, cmp_w1_k, cmp_b1_k, cmp_w2_k, cmp_b2_k, cmp_pos_v,
        cmp_w1_v, cmp_b1_v, cmp_w2_v, cmp_b2_v, gla_w_a2, gla_b_a, gla_norm_g, w_proj_nsa,
        w_proj_gla, w_out, g_ffn, w_grp, b_grp, w_exp, b_exp, w_gate, w_up, w_down, g_final,
    )
    return second_block(
        x, c_2, ctx_2, c_ctx_2, ada_w_2, ada_b_2, norm_g_2, ab_in_w_2, ab_out_w_2, a_sink_2,
        b_q_norm_g_2, b_w_uq_2, b_kv_norm_g_2, b_w_ukv_2, c_in_w_2, c_out_w_2, c_rpb_2,
        final_g_2,
    )


_drawn_inputs = setup_inputs


def setup_inputs(seed=0):
    import zlib

    import numpy as np

    out = dict(_drawn_inputs(seed))
    spreads = {}
    factors = {'cmp_pos_k': 8.0,
     'cmp_b1_k': 8.0,
     'cmp_b2_k': 8.0,
     'cmp_pos_v': 3.959,
     'cmp_b1_v': 8.0,
     'cmp_b2_v': 5.321,
     'gla_norm_g': 3.635,
     'b_grp': 3.368,
     'b_exp': 6.514,
     'g_final': 2.736,
     'ada_b_2': 7.038,
     'norm_g_2': 8.0,
     'a_sink_2': 8.0,
     'b_q_norm_g_2': 8.0,
     'b_w_uq_2': 4.258,
     'b_kv_norm_g_2': 8.0,
     'c_rpb_2': 8.0}
    for name, (base, spread) in spreads.items():
        noise = np.random.default_rng([zlib.crc32(name.encode()), seed]).standard_normal(out[name].shape)
        drawn = base * np.exp(spread * noise) if base else spread * noise
        out[name] = __import__('jax').numpy.asarray(drawn.astype(out[name].dtype))
    for name, factor in factors.items():
        out[name] = (out[name] * factor).astype(out[name].dtype)
    return out
```

```python
from contextlib import ExitStack

import numpy as np

import concourse.bass as bass
from concourse import mybir
from concourse.alu_op_type import AluOpType as ALU

F32 = mybir.dt.float32
I32 = mybir.dt.int32
U32 = mybir.dt.uint32
ACT = mybir.ActivationFunctionType
X = mybir.AxisListType.X
EPS = 1e-6
NEG = -1e30
NSLOT = 4
SLOT = 4096
LEVELS = (64, 32, 16, 8, 4, 2, 1)

SMALL = [("gmix", 8), ("gffn", 8), ("gfin", 8), ("ng0", 8), ("ng1", 8), ("fin2", 8), ("qng", 3),
         ("kvng", 2), ("glang", 4), ("b1k", 2), ("b1v", 2), ("glaba", 2), ("cc", 16), ("adab", 48),
         ("posk", 16), ("posv", 16), ("w2k", 128), ("w2v", 128), ("wr", 288), ("wa2", 256),
         ("b2k", 64), ("b2v", 64), ("brout", 36), ("sink", 8)]
CONST = [("ident", 128), ("inv", 32), ("causal", 128), ("cmpadd", 30), ("cmpok", 30), ("amask", 1024),
         ("lev", 128 * (len(LEVELS) + 1)), ("colmask", 64), ("cosa", 128), ("sina", 128), ("cosb", 64),
         ("sinb", 64), ("desc", 8), ("nhalf", 16)]


def offsets(fields):
    out, at = {}, 0
    for name, w in fields:
        out[name] = (at, w)
        at += w
    return out, at


class Bank:
    def __init__(self, t):
        self.t = t
        self.readers = []


class Prog:

    ENGINES = ("pe", "act", "dve", "pool", "sp")

    def __init__(self, nc, ctx):
        self.nc = nc
        self.ctx = ctx
        self.q = {e: [] for e in self.ENGINES}
        self.sem = {e: ctx.enter_context(nc.semaphore("s_" + e)) for e in self.ENGINES}
        self.n = {e: 0 for e in self.ENGINES}
        self.seen = {e: {} for e in self.ENGINES}
        self.flip = 0
        self.banks = [Bank(ctx.enter_context(nc.psum_tensor(f"ps{i}", [128, 512], F32))) for i in range(8)]
        self.ring = self.banks
        self.at = 0

    def wait(self, eng, toks):
        for t in toks:
            if t is None:
                continue
            if isinstance(t, (list, tuple)) and not (t and isinstance(t[0], str)):
                self.wait(eng, t)
                continue
            key, sem, v = t
            if self.seen[eng].get(key, 0) < v:
                self.seen[eng][key] = v
                self.q[eng].append(lambda e, s=sem, v=v: e.wait_ge(s, v))

    def last(self, eng):
        return (eng, self.sem[eng], self.n[eng]) if self.n[eng] else None

    def op(self, eng, fn, *after, inc=True):
        if eng != "pe":
            self.wait(eng, [self.last(eng)])
        self.wait(eng, after)
        if not inc:
            self.q[eng].append(fn)
            return None
        self.n[eng] += 1
        self.q[eng].append(lambda e, s=self.sem[eng]: fn(e).then_inc(s, 1))
        return (eng, self.sem[eng], self.n[eng])

    def dma(self, eng, out, in_, name, sem, count, *after):
        self.wait(eng, after)
        self.q[eng].append(lambda e: e.dma_start(out, in_).then_inc(sem, 16))
        return (name, sem, count)

    def barrier(self):
        for e in ("pe", "act", "dve", "pool"):
            self.wait(e, [self.last(o) for o in ("pe", "act", "dve", "pool") if o != e])

    def bank(self):
        b = self.ring[self.at % len(self.ring)]
        self.at += 1
        assert b.readers is not None
        r, b.readers = b.readers, None
        return b, r

    def mm(self, out, pairs, *after, start=True, stop=True, skip=False):
        self.wait("pe", after)
        for i, (l, r) in enumerate(pairs):
            t = self.op("pe", lambda e, l=l, r=r, i=i: e.matmul(
                out, l, r, start=start and i == 0, stop=stop and i == len(pairs) - 1, skip_group_check=skip),
                inc=i == len(pairs) - 1)
        return t

    def tr(self, out, in_, ident, *after, inc=True):
        return self.op("pe", lambda e: e.transpose(out, in_, ident), *after, inc=inc)

    def tt(self, out, a, b, op, *after, eng="dve"):
        return self.op(eng, lambda e: e.tensor_tensor(out, a, b, op), *after)

    def ts(self, out, a, s1, s2, op0, op1, *after, eng="dve"):
        if op1 is None:
            return self.op(eng, lambda e: e.tensor_scalar(out, a, s1, None, op0), *after)
        return self.op(eng, lambda e: e.tensor_scalar(out, a, s1, s2, op0, op1), *after)

    def stt(self, out, a, s, b, op0, op1, *after):
        return self.op("dve", lambda e: e.scalar_tensor_tensor(out=out, in0=a, scalar=s, in1=b, op0=op0, op1=op1),
                       *after)

    def red(self, out, a, op, *after):
        return self.op("dve", lambda e: e.tensor_reduce(out, a, X, op), *after)

    def ttr(self, out, a, b, init, op0, op1, acc, *after):
        return self.op("dve", lambda e: e.tensor_tensor_reduce(out, a, b, 1.0, init, op0, op1, acc), *after)

    def recip(self, out, a, *after):
        return self.op("dve", lambda e: e.reciprocal(out, a), *after)

    def act(self, out, in_, f, *after, bias=None, scale=1.0, acc=None):
        kw = {"scale": scale}
        if bias is not None:
            kw["bias"] = bias
        if acc is not None:
            kw["accum_out"] = acc
        return self.op("act", lambda e: e.activation(out, in_, f, **kw), *after)

    def copy(self, out, in_, *after, eng=None):
        if eng is None:
            self.flip ^= 1
            eng = "act" if self.flip else "dve"
        if eng == "act":
            return self.act(out, in_, ACT.Copy, *after)
        return self.op("dve", lambda e: e.tensor_copy(out, in_), *after)

    def sb(self, scope, name, shape, dt=F32):
        return scope.enter_context(self.nc.sbuf_tensor(name, shape, dt))


def bc(ap, axis, n):
    a = ap.unsqueeze(axis)
    shape = list(a.shape)
    shape[axis] = n
    return a.to_broadcast(shape)


def build(nc, d, out):
    with ExitStack() as ctx:
        P = Prog(nc, ctx)
        s_load = ctx.enter_context(nc.semaphore("s_load"))
        s_out = ctx.enter_context(nc.semaphore("s_out"))
        ring = P.sb(ctx, "wring", [128, NSLOT, SLOT])
        s_w = [ctx.enter_context(nc.semaphore(f"s_w{i}")) for i in range(NSLOT)]
        slot_n = [0] * NSLOT
        slot_reader = [None] * NSLOT
        at = [0]
        class W:

            def __init__(self, src):
                self.i = i = at[0] % NSLOT
                at[0] += 1
                n = 1
                for s in src.shape[1:]:
                    n *= s
                v = ring[0:src.shape[0], i, 0:n]
                assert slot_reader[i] != "held"
                if len(src.shape) == 3:
                    v = v.rearrange("p (a b) -> p a b", a=src.shape[1])
                elif len(src.shape) == 4:
                    v = v.rearrange("p (a b c) -> p a b c", a=src.shape[1], b=src.shape[2])
                slot_n[i] += 16
                self.v = v
                self.tok = P.dma("sp", v, src, f"w{i}", s_w[i], slot_n[i], slot_reader[i])
                slot_reader[i] = "held"

            def done(self, *toks):
                slot_reader[self.i] = list(toks)

        const_o, const_n = offsets(CONST)
        small_o, small_n = offsets(SMALL)
        cst = P.sb(ctx, "cst", [128, const_n])
        sml = P.sb(ctx, "sml", [128, small_n])
        post = P.sb(ctx, "post", [128, 3], I32)
        h = P.sb(ctx, "h", [128, 4, 1024])
        ld = [0]

        def load(o, i):
            ld[0] += 16
            P.dma("sp", o, i, "load", s_load, ld[0])

        load(cst[:, :], d["const"])
        load(sml[:, :], d["small"])
        load(post[:, :], d["pos"])
        load(h[:, 0:2, :], d["x"].rearrange("o (t p) d -> p (o t) d", p=128))
        load(h[:, 2:4, :], d["ctx"].rearrange("o (t p) d -> p (o t) d", p=128))
        T0 = ("load", s_load, ld[0])
        for e in ("pe", "act", "dve", "pool"):
            P.wait(e, [T0])

        def C(name, k=None):
            a, w = const_o[name]
            return cst[:, a:a + w]

        def S(name):
            a, w = small_o[name]
            return sml[:, a:a + w]

        ident = C("ident")
        NB = 3
        bS = P.sb(ctx, "bS", [128, NB, 512])
        bP = P.sb(ctx, "bP", [128, NB, 512])
        bT = P.sb(ctx, "bT", [128, NB, 512])
        st = P.sb(ctx, "st", [128, 4, 8])
        ss = P.sb(ctx, "ss", [128, 8])
        rs = P.sb(ctx, "rs", [128, 8])
        xs = P.sb(ctx, "xs", [128, 2, 1024])
        grow = P.sb(ctx, "grow", [128, 2, 1024])
        rt = P.sb(ctx, "rt", [128, 4, 256])
        scT = P.sb(ctx, "scT", [128, 8, 2])
        mod = P.sb(ctx, "mod", [128, 2, 24, 2])
        Amod = P.sb(ctx, "Amod", [128, 2, 2, 8])

        def rstd(rows, width, n, *after, c0=0):
            for i, r in enumerate(rows):
                P.ttr(xs[:, 0, 0:width], r, r, 0.0, ALU.mult, ALU.add, ss[:, c0 + i:c0 + i + 1], *after)
            s = ss[:, c0:c0 + n]
            t = P.ts(s, s, 1.0 / width, EPS, ALU.mult, ALU.add)
            return P.tt(rs[:, c0:c0 + n], s, C("nhalf")[:, 0:n], ALU.pow, t, eng="pool")

        def to_T(cols, nk, put, *after):
            for k0 in range(0, nk, 4):
                n = min(4, nk - k0)
                b, free = P.bank()
                P.wait("pe", [after, free])
                for k in range(n):
                    t = P.tr(b.t[:, k * 128:k * 128 + 128], cols(k0 + k), ident, inc=k == n - 1)
                b.readers = [put(k0, n, b.t[:, 0:n * 128].rearrange("p (k t) -> p k t", k=n), t)]
            return t

        def norm_T(tiles, outT, A, B=None):
            t0 = rstd([r for r in tiles], 1024, len(tiles), P.last("pe"))
            last = None
            xsfree = [None, None]
            for i, r in enumerate(tiles):
                tx = P.ts(xs[:, i % 2, :], r, rs[:, i:i + 1], None, ALU.mult, None, t0, xsfree[i % 2])
                xv = xs[:, i % 2, :].rearrange("p (d k) -> p k d", k=8)
                a, b2 = A(i), (B(i) if B else None)

                def put(k0, n, ps, t, i=i, a=a, b2=b2):
                    o = outT[:, k0:k0 + n, i * 128:(i + 1) * 128]
                    t = P.tt(o, ps, bc(a[:, k0:k0 + n], 2, 128), ALU.mult, t)
                    if b2 is not None:
                        P.tt(o, o, bc(b2[:, k0:k0 + n], 2, 128), ALU.add)
                    return t
                xsfree[i % 2] = to_T(lambda k: xv[:, k, :], 8, put, tx)
            return P.last("dve")

        def lin(xT, w, cols, tiles, put, *after, nk=8):
            for i in tiles:
                b, free = P.bank()
                t = P.mm(b.t[:, 0:cols], [(xT[:, k, i * 128:(i + 1) * 128], w.v[:, k, 0:cols]) for k in range(nk)],
                         w.tok, free, after)
                b.readers = [put(i, b.t[:, 0:cols], t)]
            w.done(t)

        def linT(xT, w, mtiles, n, put, *after, nk=8):
            for j, (c0, m) in enumerate(mtiles):
                b, free = P.bank()
                t = P.mm(b.t[0:m, 0:n], [(w.v[:, k, c0:c0 + m], xT[:, k, 0:n]) for k in range(nk)], w.tok, free, after)
                b.readers = [put(j, b.t[0:m, 0:n], t)]
            w.done(t)

        def lin2(xT, ws, tiles, put, *after):
            for i in tiles:
                for c in range(2):
                    b, free = P.bank()
                    t = P.mm(b.t[:, :], [(xT[:, k, i * 128:(i + 1) * 128], ws[k // 4].v[:, k % 4, c * 512:c * 512 + 512])
                                         for k in range(8)], ws[0].tok, ws[1].tok, free, after)
                    b.readers = [put(i, c, b.t[:, :], t)]
            for w in ws:
                w.done(t)

        pfree = [None] * NB
        tfree = [None] * NB

        def attend(units):
            n = len(units)
            live = {}

            def scores(i):
                u = units[i]
                b, free = P.bank()
                P.wait("pe", [free, u["after"]])
                for col, w, l, r in u["qk"]:
                    t = P.mm(b.t[:, col:col + w], [(l, r)])
                live[i] = {"b": b, "t": t}

            def soft(i):
                u, L = units[i], live[i]
                x = L["b"].t[:, 0:u["nk"]]
                m = st[:, i % 4, :]
                src, readers = u["peak"](x, bS[:, i % NB, 0:u["nk"]], m[:, 0:1], L["t"])
                sc = u["scale"]
                if u.get("sink") is not None:
                    P.ts(m[:, 1:2], m[:, 0:1], sc, u["sink"], ALU.mult, ALU.max)
                    t = P.ts(m[:, 1:2], m[:, 1:2], -1.0, None, ALU.mult, None)
                else:
                    t = P.ts(m[:, 1:2], m[:, 0:1], -sc, None, ALU.mult, None)
                p = bP[:, i % NB, 0:u["nk"]]
                te = P.act(p, src, ACT.Exp, t, pfree[i % NB], bias=m[:, 1:2], scale=sc, acc=m[:, 2:3])
                L["b"].readers = readers + [te]
                if u.get("sink") is not None:
                    te = P.act(m[:, 3:4], u["sink"], ACT.Exp, bias=m[:, 1:2])
                    P.tt(m[:, 2:3], m[:, 2:3], m[:, 3:4], ALU.add, te)
                if u.get("ok") is not None:
                    te = P.tt(p, p, u["ok"], ALU.mult, te)
                L["r"] = P.recip(m[:, 4:5], m[:, 2:3], te)
                L["p"] = te

            def turn(i):
                u, L = units[i], live[i]
                b, free = P.bank()
                P.wait("pe", [free, L["p"]])
                nk = u["nk"]
                blocks = [(c, min(128, nk - c)) for c in range(0, nk, 128)]
                for j, (c, w) in enumerate(blocks):
                    t = P.tr(b.t[0:w, j * 128:(j + 1) * 128], bP[:, i % NB, c:c + w], ident, inc=j == len(blocks) - 1)
                pfree[i % NB] = t
                w = blocks[0][1]
                t = P.copy(bT[0:w, i % NB, 0:128 * len(blocks)], b.t[0:w, 0:128 * len(blocks)], t, tfree[i % NB])
                b.readers = [t]
                L["pt"] = t

            def mix(i):
                u, L = units[i], live.pop(i)
                b, free = P.bank()
                t = P.mm(b.t[:, 0:64], [(bT[0:v.shape[0], i % NB, j * 128:(j + 1) * 128], v) for j, v in enumerate(u["v"])],
                         free, L["pt"])
                tfree[i % NB] = t
                b.readers = [u["put"](b.t[:, 0:64], st[:, i % 4, 4:5], t, L["r"])]

            for s in range(n + 3):
                if s < n:
                    scores(s)
                if 0 <= s - 1 < n:
                    soft(s - 1)
                if 0 <= s - 2 < n:
                    turn(s - 2)
                if 0 <= s - 3 < n:
                    mix(s - 3)

        def peak(x, s, m, t):
            return x, [P.red(m, x, ALU.max, t)]

        def peak_masked(mask):
            def f(x, s, m, t):
                t = P.ttr(s, x, mask, -3e38, ALU.add, ALU.max, m, t)
                return s, [t]
            return f

        with ExitStack() as sc:
            uT = P.sb(sc, "uT", [128, 8, 256])
            tu = norm_T([h[:, 0, :], h[:, 1, :]], uT, lambda i: S("gmix"))

            ang = P.sb(sc, "ang", [128, 3, 32])
            rr = P.sb(sc, "rr", [128, 3, 32])
            cos = P.sb(sc, "cos", [128, 3, 32])
            sin = P.sb(sc, "sin", [128, 3, 32])
            posf = P.sb(sc, "posf", [128, 3])
            P.op("dve", lambda e: e.tensor_copy(posf[:, :], post[:, :]))
            P.tt(ang[:, :, :], bc(C("inv"), 1, 3), bc(posf[:, :], 2, 32), ALU.mult)
            twopi = 2.0 * np.pi
            hi = float(np.float32(np.round(twopi * 128) / 128))
            mid = float(np.float32(np.round((twopi - hi) * 2.0 ** 19) / 2.0 ** 19))
            lo = float(np.float32(twopi - hi - mid))
            magic = 12582912.0
            P.ts(rr[:, :, :], ang[:, :, :], 1.0 / twopi, magic, ALU.mult, ALU.add)
            P.ts(rr[:, :, :], rr[:, :, :], -magic, None, ALU.add, None)
            for c in (hi, mid, lo):
                P.stt(ang[:, :, :], rr[:, :, :], -c, ang[:, :, :], ALU.mult, ALU.add)
            t = P.ts(ang[:, :, :], ang[:, :, :], 3.1415925, -3.1415925, ALU.min, ALU.max)
            P.act(sin[:, :, :], ang[:, :, :], ACT.Sin, t)
            t = P.act(rr[:, :, :], ang[:, :, :], ACT.Sin, scale=0.5)
            P.tt(rr[:, :, :], rr[:, :, :], rr[:, :, :], ALU.mult, t)
            P.ts(cos[:, :, :], rr[:, :, :], -2.0, 1.0, ALU.mult, ALU.add)

            qk = P.sb(sc, "qk", [128, 4, 256])
            w = W(d["w_gqk"])

            def put(j, ps, t):
                return P.ts(qk[:, j, :], ps, 0.125 if j < 2 else 1.0, None, ALU.mult, None, t)
            linT(uT, w, [(j * 128, 128) for j in range(4)], 256, put, tu)

            gate = P.sb(sc, "gate", [128, 2, 24])
            alow = P.sb(sc, "alow", [16, 256])
            w = W(d["w_sm"])
            for i in range(2):
                b, free = P.bank()
                t = P.mm(b.t[:, 0:24], [(uT[:, k, i * 128:(i + 1) * 128], w.v[:, k, 0:24]) for k in range(8)], w.tok, free)
                b.readers = [P.act(gate[:, i, :], b.t[:, 0:24], ACT.Sigmoid, t)]
            linT(uT, w, [(24, 16)], 256, lambda j, ps, t: P.copy(alow[:, :], ps, t))
            ta = P.last("act"), P.last("dve")
            gv = P.sb(sc, "gv", [128, 2, 512])
            lin(uT, W(d["w_gv"]), 512, range(2), lambda i, ps, t: P.copy(gv[:, i, :], ps, t))

            q = P.sb(sc, "q", [128, 2, 512])
            kv = P.sb(sc, "kv", [128, 2, 512])
            lin(uT, W(d["w_q"]), 512, range(2), lambda i, ps, t: P.copy(q[:, i, :], ps, t, eng="act"))
            lin(uT, W(d["w_kv"]), 512, range(2), lambda i, ps, t: P.copy(kv[:, i, :], ps, t, eng="act"))

            la = P.sb(sc, "la", [128, 2, 256])
            cum = P.sb(sc, "cum", [128, 2, 256])
            tmp = P.sb(sc, "tmp", [128, 2, 256])
            ones = P.sb(sc, "ones", [128, 256])
            tones = P.op("pool", lambda e: e.memset(ones[:, :], 1.0))
            b, free = P.bank()
            P.wait("pe", [ta, free])
            for j in range(2):
                t = P.mm(b.t[:, j * 256:(j + 1) * 256], [(S("wa2")[0:16, j * 128:(j + 1) * 128], alow[:, :])])
            for j in range(2):
                t = P.ts(la[:, j, :], b.t[:, j * 256:(j + 1) * 256], S("glaba")[:, j:j + 1], None, ALU.add, None, t)
            b.readers = [t]
            t = P.stt(tmp[:, :, :], la[:, :, :], -1.0, la[:, :, :], ALU.mult, ALU.max)
            P.act(tmp[:, :, :], tmp[:, :, :], ACT.Exp, t, scale=-1.0)
            t = P.act(tmp[:, :, :], tmp[:, :, :], ACT.Ln, tones, bias=ones[:, 0:1])
            P.stt(la[:, :, :], la[:, :, :], 0.0, tmp[:, :, :], ALU.min, ALU.subtract, t)
            P.ts(la[:, :, :], la[:, :, :], 1.0 / 16.0, None, ALU.mult, None)
            for j in range(2):
                P.op("dve", lambda e, j=j: e.tensor_tensor_scan(cum[:, j, :], ones[:, :], la[:, j, :], 0.0, ALU.mult, ALU.add),
                     tones)

            def rope_half(dst1, dst2, x1, x2, co, si, tmps):
                a, b_, c_, d_ = tmps
                P.tt(a, x1, co, ALU.mult)
                P.tt(b_, x2, si, ALU.mult)
                P.tt(c_, x2, co, ALU.mult)
                P.tt(d_, x1, si, ALU.mult)
                P.tt(dst1, a, b_, ALU.subtract)
                return P.tt(dst2, c_, d_, ALU.add)

            kr = P.sb(sc, "kr", [128, 2, 4, 2, 64])
            for i in range(2):
                qv = q[:, i, :].rearrange("p (h a r) -> p h a r", h=8, a=2)
                tm = [rt[:, n, :].rearrange("p (h r) -> p h r", h=8) for n in range(4)]
                P.wait("dve", [P.last("act")])
                rope_half(qv[:, :, 0, :], qv[:, :, 1, :], qv[:, :, 0, :], qv[:, :, 1, :],
                          bc(cos[:, i, :], 1, 8), bc(sin[:, i, :], 1, 8), tm)
                kw = kv[:, i, 0:256].rearrange("p (h a r) -> p h a r", h=4, a=2)
                tm = [rt[:, n, 0:128].rearrange("p (h r) -> p h r", h=4) for n in range(4)]
                ko = kr[:, i, :, 0, :].rearrange("p h (a r) -> p h a r", a=2)
                rope_half(ko[:, :, 0, :], ko[:, :, 1, :], kw[:, :, 0, :], kw[:, :, 1, :],
                          bc(cos[:, i, :], 1, 4), bc(sin[:, i, :], 1, 4), tm)
                tk = P.op("dve", lambda e, i=i: e.tensor_copy(kr[:, i, :, 1, :], kr[:, i, :, 0, :]))
            qT = P.sb(sc, "qT", [128, 4, 256])
            kT = P.sb(sc, "kT", [128, 4, 256])
            for i in range(2):
                to_T(lambda k: q[:, i, k * 128:(k + 1) * 128], 4,
                     lambda k0, n, ps, t: P.copy(qT[:, :, i * 128:(i + 1) * 128], ps, t), tk)
                to_T(lambda k: kr[:, i, k, :, :].rearrange("p a r -> p (a r)"), 4,
                     lambda k0, n, ps, t: P.copy(kT[:, :, i * 128:(i + 1) * 128], ps, t), tk)

            Bt = P.sb(sc, "Bt", [128, 2, 16, 30])
            hid = P.sb(sc, "hid", [128, 2, 2, 30])
            kcr = P.sb(sc, "kcr", [16, 2, 2, 64])
            kcT = P.sb(sc, "kcT", [128, 2, 16])
            vc = P.sb(sc, "vc", [16, 2, 64])
            w = W(d["w_kvc"])

            def put(j, ps, t):
                m, g = j // 2, j % 2
                for jp in range(2):
                    p0 = 64 * jp
                    src = ps[p0:p0 + 64, :].rearrange("p (n s) -> p s n", s=16)
                    pos = S("posk" if m == 0 else "posv")
                    for half in range(2):
                        t = P.tt(Bt[p0:p0 + 64, m, 8 * half:8 * half + 8, 15 * g:15 * g + 15],
                                 src[:, jp:16:2, half:half + 15],
                                 bc(pos[p0:p0 + 64, 8 * half:8 * half + 8], 2, 15), ALU.add, t)
                return t
            linT(uT, w, [(j * 128, 128) for j in range(4)], 256, put)
            tb = P.last("dve")
            for m in range(2):
                w = W(d["w1k" if m == 0 else "w1v"])
                b1 = S("b1k" if m == 0 else "b1v")
                for c in range(2):
                    b, free = P.bank()
                    t = P.mm(b.t[:, 0:30], [(w.v[:, j, c * 128:(c + 1) * 128], Bt[:, m, j, :]) for j in range(16)],
                             w.tok, free, tb)
                    b.readers = [P.act(hid[:, m, c, :], b.t[:, 0:30], ACT.Gelu_apprx_tanh, t, bias=b1[:, c:c + 1])]
                w.done(t)
            th = P.last("act")
            for m in range(2):
                w2 = S("w2k" if m == 0 else "w2v").rearrange("p (c n) -> p c n", c=2)
                b2 = S("b2k" if m == 0 else "b2v")[0:15, :]
                b, free = P.bank()
                P.wait("pe", [free, th])
                for g in range(2):
                    t = P.mm(b.t[0:15, g * 64:g * 64 + 64],
                             [(hid[:, m, c, 15 * g:15 * g + 15], w2[:, c, :]) for c in range(2)])
                ps = b.t[0:15, 0:128].rearrange("p (g n) -> p g n", g=2)
                if m == 1:
                    b.readers = [P.tt(vc[0:15, :, :], ps, bc(b2, 1, 2), ALU.add, t)]
                    continue
                t = P.tt(kcr[0:15, :, 0, :], ps, bc(b2, 1, 2), ALU.add, t)
                b.readers = [t]
                kk = kcr[0:15, :, 0, :].rearrange("p g (a r) -> p g a r", a=2)
                tm = [rt[0:15, n, 0:64].rearrange("p (h r) -> p h r", h=2) for n in range(4)]
                rope_half(kk[:, :, 0, :], kk[:, :, 1, :], kk[:, :, 0, :], kk[:, :, 1, :],
                          bc(cos[0:15, 2, :], 1, 2), bc(sin[0:15, 2, :], 1, 2), tm)
                t = P.op("dve", lambda e: e.tensor_copy(kcr[0:15, :, 1, :], kcr[0:15, :, 0, :]))
                b, free = P.bank()
                for g in range(2):
                    t = P.tr(b.t[:, g * 16:g * 16 + 15], kcr[0:15, g, :, :].rearrange("p a r -> p (a r)"),
                             ident[0:15, 0:15], free, t)
                for g in range(2):
                    t = P.copy(kcT[:, g, 0:15], b.t[:, g * 16:g * 16 + 15], t, eng="dve")
                b.readers = [t]

            gr = P.sb(sc, "gr", [128, 2, 512])
            lin(uT, W(d["w_gr"]), 512, range(2), lambda i, ps, t: P.act(gr[:, i, :], ps, ACT.Silu, t))

            yn = P.sb(sc, "yn", [128, 2, 512])
            cf = P.sb(sc, "cf", [128, 4])
            cfn = [0]

            def nsa_put(kind, hh, i):
                def f(ps, r, t, tr):
                    cfn[0] += 1
                    c = cf[:, cfn[0] % 4:cfn[0] % 4 + 1]
                    P.tt(c, r, gate[:, i, 3 * hh + kind:3 * hh + kind + 1], ALU.mult, tr)
                    o = yn[:, i, hh * 64:hh * 64 + 64]
                    if kind == 0:
                        return P.ts(o, ps, c, None, ALU.mult, None, t)
                    return P.stt(o, ps, c, o, ALU.mult, ALU.add, t)
                return f

            def peak_causal(i):
                def f(x, s, m, t):
                    if i == 1:
                        P.copy(s[:, 0:128], x[:, 0:128], t, eng="dve")
                    t = P.tt(s[:, i * 128:i * 128 + 128], x[:, i * 128:i * 128 + 128], C("causal"), ALU.add, t)
                    P.red(m, s, ALU.max)
                    return s, [t]
                return f

            units = []
            te = [P.last("act"), P.last("dve")]
            for kind in range(3):
                for i in range(2):
                    for hh in range(8):
                        g, p0 = hh // 4, 64 * (hh % 2)
                        ql = qT[p0:p0 + 64, hh // 2, i * 128:(i + 1) * 128]
                        u = {"after": te, "scale": 0.125, "put": nsa_put(kind, hh, i)}
                        if kind == 0:
                            u.update(nk=15, qk=[(0, 15, ql, kcT[p0:p0 + 64, g, 0:15])],
                                     peak=peak_masked(C("cmpadd")[:, 15 * i:15 * i + 15]),
                                     ok=C("cmpok")[:, 15 * i:15 * i + 15], v=[vc[0:15, g, :]])
                        else:
                            n = 128 * (i + 1)
                            c = 256 + (kind - 1) * 128 + g * 64
                            u.update(nk=n, qk=[(0, n, ql, kT[p0:p0 + 64, 2 * (kind - 1) + g, 0:n])],
                                     peak=peak_causal(i), v=[kv[:, j, c:c + 64] for j in range(i + 1)])
                        units.append(u)
            attend(units)


            Am = P.sb(sc, "Am", [128, 4, 3, 128])
            Q = P.sb(sc, "Q", [128, 2, 256])
            K = P.sb(sc, "K", [128, 2, 256])
            E = P.sb(sc, "E", [128, 2, 256])
            P.op("dve", lambda e: e.memset(Am[:, :, :, :], 0.0))
            P.op("dve", lambda e: e.memset(Q[:, :, :], 0.0))
            P.op("dve", lambda e: e.memset(K[:, :, :], 0.0))
            tq = None

            def place(hp, ps, li, *after):
                a0 = const_o["lev"][0] + 128 * li
                mk = bc(bc(cst[:, a0:a0 + 128].bitcast(U32), 1, 2), 1, 2)
                return P.op("dve", lambda e: e.copy_predicated(Am[:, hp:4:2, 0:2, :], mk, ps), *after)

            for m in (128,) + LEVELS:
                nb = 128 // m
                for j in range(2):
                    v = cum[:, j, :].rearrange("p (n a m) -> p n a m", a=2, m=m)
                    ev = E[:, j, :].rearrange("p (n a m) -> p n a m", a=2, m=m)
                    mid_ = v[:, :, 0, m - 1:m].to_broadcast([128, nb, m])
                    P.tt(ev[:, :, 1, :], v[:, :, 1, :], mid_, ALU.subtract)
                    t = P.tt(ev[:, :, 0, :], mid_, v[:, :, 0, :], ALU.subtract)
                t = P.act(E[:, :, :], E[:, :, :], ACT.Exp, t)
                for j in range(2):
                    def part(x, a):
                        return x.rearrange("p (n a m) -> p n a m", a=2, m=m)[:, :, a, :]
                    P.tt(part(Q[:, j, :], 1), part(qk[:, j, :], 1), part(E[:, j, :], 1), ALU.mult, t, tq)
                    t = P.tt(part(K[:, j, :], 0), part(qk[:, 2 + j, :], 0), part(E[:, j, :], 0), ALU.mult)
                for hp in range(2):
                    p0 = 64 * hp
                    b, free = P.bank()
                    P.wait("pe", [t, free])
                    for pr in range(2):
                        for bl in range(1 if m == 128 else 2):
                            ks = K[p0:p0 + 64, pr, bl * 128:bl * 128 + 128]
                            qs = Q[p0:p0 + 64, pr, 128:256] if m == 128 else Q[p0:p0 + 64, pr, bl * 128:bl * 128 + 128]
                            tq = P.mm(b.t[:, (2 * pr + bl) * 128:(2 * pr + bl) * 128 + 128], [(ks, qs)])
                    ps = b.t[:, :].rearrange("p (h b t) -> p h b t", h=2, b=2)
                    if m == 128:
                        b.readers = [P.copy(Am[:, hp:4:2, 2, :], ps[:, :, 0, :], tq, eng="dve")]
                    else:
                        b.readers = [place(hp, ps, LEVELS.index(m), tq)]
            for hp in range(2):
                p0 = 64 * hp
                b, free = P.bank()
                P.wait("pe", [free])
                for pr in range(2):
                    for bl in range(2):
                        tq = P.mm(b.t[:, (2 * pr + bl) * 128:(2 * pr + bl) * 128 + 128],
                                  [(qk[p0:p0 + 64, 2 + pr, bl * 128:bl * 128 + 128], qk[p0:p0 + 64, pr, bl * 128:bl * 128 + 128])])
                ps = b.t[:, :].rearrange("p (h b t) -> p h b t", h=2, b=2)
                b.readers = [place(hp, ps, len(LEVELS), tq)]
            tA = P.last("dve")
            go = q
            for i in range(2):
                b, free = P.bank()
                P.wait("pe", [free, tA])
                for hh in range(4):
                    pairs = [(Am[:, hh, i, :], gv[:, i, hh * 128:hh * 128 + 128])]
                    if i == 1:
                        pairs.insert(0, (Am[:, hh, 2, :], gv[:, 0, hh * 128:hh * 128 + 128]))
                    t = P.mm(b.t[:, hh * 128:hh * 128 + 128], pairs)
                b.readers = [P.copy(go[:, i, :], b.t[:, :], t, eng="dve")]
                P.tt(xs[:, 0, 0:512], go[:, i, :], go[:, i, :], ALU.mult)
                P.red(ss[:, 4 * i:4 * i + 4], xs[:, 0, 0:512].rearrange("p (h e) -> p h e", h=4), ALU.add)
            t = P.ts(ss[:, :], ss[:, :], 1.0 / 128, EPS, ALU.mult, ALU.add)
            t = P.tt(rs[:, :], ss[:, :], C("nhalf")[:, 0:8], ALU.pow, t, eng="pool")
            for i in range(2):
                gov = go[:, i, :].rearrange("p (h e) -> p h e", h=4)
                P.tt(gov, gov, bc(rs[:, 4 * i:4 * i + 4], 2, 128), ALU.mult, t)
                tg = P.tt(go[:, i, :], go[:, i, :], gr[:, i, :], ALU.mult)

            ynT, ogT = qT, kT
            for i in range(2):
                to_T(lambda k: yn[:, i, :].rearrange("p (d k) -> p k d", k=4)[:, k, :], 4,
                     lambda k0, n, ps, t: P.copy(ynT[:, :, i * 128:(i + 1) * 128], ps, t), tg)
                to_T(lambda k: go[:, i, :].rearrange("p (d k) -> p k d", k=4)[:, k, :], 4,
                     lambda k0, n, ps, t: P.tt(ogT[:, :, i * 128:(i + 1) * 128], ps, bc(S("glang"), 2, 128), ALU.mult, t))
            te = [P.last("act"), P.last("dve")]
            mx = grow
            sm = xs[:, :, :].rearrange("p i (m n) -> p i m n", m=2)
            for c in range(2):
                for m in range(2):
                    lin(uT, W(d["w_m"][2 * m + c]), 512, range(2),
                        lambda i, ps, t: P.act(sm[:, i, m, :], ps, ACT.Sigmoid, t, P.last("dve")))
                wa, wb = (W(d[n].rearrange("(p k) n -> p k n", k=4)[:, :, c * 512:c * 512 + 512])
                          for n in ("w_proj_nsa", "w_proj_gla"))
                for i in range(2):
                    o = mx[:, i, c * 512:c * 512 + 512]
                    b, free = P.bank()
                    t = P.mm(b.t[:, :], [(ynT[:, k, i * 128:(i + 1) * 128], wa.v[:, k, :]) for k in range(4)],
                             wa.tok, free, te)
                    b.readers = [P.tt(o, b.t[:, :], sm[:, i, 0, :], ALU.mult, t, P.last("act"))]
                    b, free = P.bank()
                    t = P.mm(b.t[:, :], [(ogT[:, k, i * 128:(i + 1) * 128], wb.v[:, k, :]) for k in range(4)],
                             wb.tok, free)
                    b.readers = [P.tt(bS[:, 0, :], b.t[:, :], sm[:, i, 1, :], ALU.mult, t)]
                    tm_ = P.tt(o, o, bS[:, 0, :], ALU.add)
                wa.done(t)
                wb.done(t)
            mxT = uT
            for i in range(2):
                to_T(lambda k: mx[:, i, :].rearrange("p (d k) -> p k d", k=8)[:, k, :], 8,
                     lambda k0, n, ps, t: P.copy(mxT[:, k0:k0 + n, i * 128:(i + 1) * 128], ps, t), tm_)
            te = [P.last("act"), P.last("dve")]
            wo = d["w_out"].rearrange("(p k) n -> p k n", k=8)

            def put(i, c, ps, t):
                o = h[:, i, c * 512:c * 512 + 512]
                return P.tt(o, o, ps, ALU.add, t)
            lin2(mxT, [W(wo[:, 0:4, :]), W(wo[:, 4:8, :])], range(2), put, te)
            P.barrier()

        with ExitStack() as sc:
            vT = P.sb(sc, "vT", [128, 8, 256])
            tv = norm_T([h[:, 0, :], h[:, 1, :]], vT, lambda i: S("gffn"))
            lg = P.sb(sc, "lg", [128, 2, 36])
            wr = S("wr").rearrange("p (k n) -> p k n", k=8)
            for i in range(2):
                b, free = P.bank()
                t = P.mm(b.t[:, 0:36], [(vT[:, k, i * 128:(i + 1) * 128], wr[:, k, :]) for k in range(8)], free, tv)
                b.readers = [P.tt(lg[:, i, :], b.t[:, 0:36], S("brout"), ALU.add, t)]
            R = P.sb(sc, "R", [128, 2, 128])
            comb = P.sb(sc, "comb", [128, 2, 32])
            g4, e32 = lg[:, :, 0:4], lg[:, :, 4:36].rearrange("p i (g e) -> p i g e", g=4)
            m1, eg, sg, oh4 = R[:, :, 0:1], R[:, :, 1:5], R[:, :, 5:6], R[:, :, 6:10]
            w4, in8, oh8, oh8b, t8 = R[:, :, 10:14], R[:, :, 16:24], R[:, :, 24:32], R[:, :, 32:40], R[:, :, 40:48]
            ma, mb, e2, dn, c1, c2 = (R[:, :, 48 + n:49 + n] for n in range(6))
            tb_ = R[:, :, 64:96]

            def first(oh, x, mx_, n):
                P.tt(oh, x, mx_.to_broadcast([128, 2, n]), ALU.is_equal)
                P.tt(oh, oh, bc(C("desc")[:, 8 - n:8], 1, 2), ALU.mult)
                P.red(dn[:, :, 0], oh, ALU.max)
                return P.tt(oh, oh, dn.to_broadcast([128, 2, n]), ALU.is_equal)

            P.red(m1[:, :, 0], g4, ALU.max)
            t = P.tt(eg, g4, m1.to_broadcast([128, 2, 4]), ALU.subtract)
            t = P.act(eg, eg, ACT.Exp, t)
            P.red(sg[:, :, 0], eg, ALU.add, t)
            first(oh4, g4, m1, 4)
            pe_ = tb_.rearrange("p i (g e) -> p i g e", g=4)
            for i in range(2):
                P.tt(pe_[:, i], e32[:, i], bc(oh4[:, i], 2, 8), ALU.mult)
                P.red(in8[:, i], pe_[:, i].rearrange("p g e -> p e g"), ALU.add)
            P.red(ma[:, :, 0], in8, ALU.max)
            first(oh8, in8, ma, 8)
            P.stt(t8, oh8, NEG, in8, ALU.mult, ALU.add)
            P.red(mb[:, :, 0], t8, ALU.max)
            first(oh8b, t8, mb, 8)
            t = P.tt(e2, mb, ma, ALU.subtract)
            t = P.act(e2, e2, ACT.Exp, t)
            P.ts(dn, e2, 1.0, None, ALU.add, None, t)
            P.tt(dn, dn, sg, ALU.mult)
            P.recip(c1, dn)
            P.tt(c2, c1, e2, ALU.mult)
            P.tt(oh8, oh8, c1.to_broadcast([128, 2, 8]), ALU.mult)
            P.tt(oh8b, oh8b, c2.to_broadcast([128, 2, 8]), ALU.mult)
            P.tt(oh8, oh8, oh8b, ALU.add)
            cv = comb[:, :, :].rearrange("p i (g e) -> p i g e", g=4)
            for i in range(2):
                t = P.tt(cv[:, i], bc(oh8[:, i], 1, 4), bc(oh4[:, i], 2, 8), ALU.mult)
            combT = P.sb(sc, "combT", [32, 256])
            b, free = P.bank()
            P.wait("pe", [free, t])
            for i in range(2):
                t = P.tr(b.t[0:32, i * 128:(i + 1) * 128], comb[:, i, :], ident)
            tc = P.copy(combT[:, :], b.t[0:32, 0:256], t)
            b.readers = [tc]

            hT = P.sb(sc, "hT", [128, 2, 4, 256])
            sl = P.sb(sc, "sl", [128, 2, 256])
            cb = P.sb(sc, "cb", [128, 2, 256])
            P.barrier()
            Y = P.banks[0:4]
            yfree = [P.last("act"), P.last("dve")]
            P.ring = P.banks[4:8]
            hfree = [None, None]
            hready = [None, None]
            held = {}

            def up(e):
                wg = W(d["w_gate"][e].rearrange("(p k) f -> p k f", k=8))
                wu = W(d["w_up"][e].rearrange("(p k) f -> p k f", k=8))
                b, free = P.bank()
                t = P.mm(b.t[:, 0:256], [(ident[0:32, e:e + 1].to_broadcast([32, 128]), combT[:, :])], free, tc)
                tcb = P.copy(cb[:, e % 2, :], b.t[:, 0:256], t, P.last("dve"), eng="act")
                b.readers = [tcb]
                for f in range(4):
                    b, free = P.bank()
                    t1 = P.mm(b.t[:, 0:256], [(wg.v[:, k, f * 128:(f + 1) * 128], vT[:, k, :]) for k in range(8)], free, wg.tok)
                    t2 = P.mm(b.t[:, 256:512], [(wu.v[:, k, f * 128:(f + 1) * 128], vT[:, k, :]) for k in range(8)], wu.tok)
                    t = P.act(sl[:, f % 2, :], b.t[:, 0:256], ACT.Silu, t2, P.last("dve"))
                    o = hT[:, e % 2, f, :]
                    t3 = P.tt(o, b.t[:, 256:512], cb[:, e % 2, :], ALU.mult, tcb, t, hfree[e % 2])
                    b.readers = [t, t3]
                    hready[e % 2] = P.tt(o, o, sl[:, f % 2, :], ALU.mult, t)
                wg.done(t2)
                wu.done(t2)

            def down(e):
                wd = W(d["w_down"][e].rearrange("(j p) n -> p j n", p=128))
                P.wait("pe", [wd.tok, hready[e % 2], yfree])
                for i in range(2):
                    for c in range(2):
                        t = P.mm(Y[2 * i + c].t[:, :],
                                 [(hT[:, e % 2, f, i * 128:(i + 1) * 128], wd.v[:, f, c * 512:c * 512 + 512]) for f in range(4)],
                                 start=e == 0, stop=e == 31)
                hfree[e % 2] = t
                wd.done(t)
                return t

            for e in range(33):
                if e < 32:
                    up(e)
                if e > 0:
                    ty = down(e - 1)
            for i in range(2):
                for c in range(2):
                    o = h[:, i, c * 512:c * 512 + 512]
                    t = P.tt(o, o, Y[2 * i + c].t[:, :], ALU.add, ty)
                    Y[2 * i + c].readers = [t]
            P.ring = P.banks
            P.at = 0
            P.barrier()

        def row_bcast(dst, col, *after):
            dv = dst.rearrange("p (n k) -> p k n", k=8)
            for k0 in (0, 4):
                b, free = P.bank()
                P.wait("pe", [free, after])
                for k in range(4):
                    t = P.mm(b.t[:, k * 128:(k + 1) * 128], [(col(k0 + k).to_broadcast([128, 128]), ident)])
                b.readers = [P.copy(dv[:, k0:k0 + 4, :], b.t[:, :].rearrange("p (k n) -> p k n", k=4), t, eng="dve")]

        def final_norm(g, dst):
            row_bcast(grow[:, 0, :], lambda k: S(g)[:, k:k + 1])
            t = rstd([h[:, 0, :], h[:, 1, :]], 1024, 2)
            for i in range(2):
                t = P.stt(dst(i), h[:, i, :], rs[:, i:i + 1], grow[:, 0, :], ALU.mult, ALU.mult, t)
            return t

        final_norm("gfin", lambda i: h[:, i, :])

        t = P.act(scT[:, :, :], S("cc").rearrange("p (k w) -> p k w", w=2), ACT.Silu)
        for l in range(2):
            b, free = P.bank()
            P.wait("pe", [free, t])
            for c in range(6):
                w = W(d["w_ada"][l, c])
                P.wait("pe", [w.tok])
                for j in range(4):
                    o = 2 * (4 * c + j)
                    tm_ = P.mm(b.t[:, o:o + 2], [(w.v[:, k, j * 128:(j + 1) * 128], scT[:, k, :]) for k in range(8)])
                w.done(tm_)
            b.readers = [P.tt(mod[:, l], b.t[:, 0:48].rearrange("p (c w) -> p c w", w=2),
                              bc(S("adab")[:, 24 * l:24 * l + 24], 2, 2), ALU.add, tm_)]
            for wh in range(2):
                P.stt(Amod[:, l, wh, :], mod[:, l, 8:16, wh], 1.0, S("ng0" if l == 0 else "ng1"), ALU.add, ALU.mult)

        def modulated(UT, l):
            return norm_T([h[:, i, :] for i in range(4)], UT, lambda i: Amod[:, l, i // 2, :],
                          lambda i: mod[:, l, 0:8, i // 2])

        def residual(i, c, ps, t):
            o = h[:, i, c * 512:c * 512 + 512]
            t = P.tt(bS[:, 0, :], ps, grow[:, i // 2, c * 512:c * 512 + 512], ALU.mult, t)
            P.tt(o, o, bS[:, 0, :], ALU.add)
            return t

        with ExitStack() as sc:
            UT = P.sb(sc, "UT", [128, 8, 512])
            tu = modulated(UT, 0)
            for wh in range(2):
                row_bcast(grow[:, wh, :], lambda k: mod[:, 0, 16 + k, wh:wh + 1], P.last("dve"))
            ZO = P.sb(sc, "ZO", [128, 4, 1024])
            va = P.sb(sc, "va", [128, 4, 128])
            with ExitStack() as sa:
                cq = P.sb(sa, "cq", [128, 4, 416])
                vb = P.sb(sa, "vb", [128, 4, 8, 64])
                vbf = vb[:, :, :, :].rearrange("p i h r -> p (i h r)")
                ck = vbf[:, 0:1024].rearrange("p (i n) -> p i n", i=4)
                kaT = vbf[:, 1024:2048].rearrange("p (g t) -> p g t", g=2)
                qq = P.sb(sa, "qq", [128, 8, 512])
                qa, qaT, kbT = qq[:, 0:4, :], qq[:, 4:8, :], qq[0:96, :, :]
                ka = P.sb(sa, "ka", [128, 4, 128])
                kd = P.sb(sa, "kd", [128, 2, 2, 64])
                T4 = range(4)
                lin(UT, W(d["w_qa"]), 512, T4, lambda i, ps, t: P.copy(qa[:, i, :], ps, t), tu)

                def put(i, ps, t):
                    P.copy(ka[:, i, :], ps[:, 0:128], t, eng="dve")
                    P.copy(va[:, i, :], ps[:, 128:256], t, eng="dve")
                    return P.copy(ck[:, i, :], ps[:, 256:512], t, eng="dve")
                lin(UT, W(d["w_kva"]), 512, T4, put)
                lin(UT, W(d["w_za"]), 512, T4, lambda i, ps, t: P.act(ZO[:, i, 0:512], ps, ACT.Silu, t))
                lin(UT, W(d["w_zb"]), 512, T4, lambda i, ps, t: P.act(ZO[:, i, 512:1024], ps, ACT.Silu, t))
                lin(UT, W(d["w_cq"]), 416, T4, lambda i, ps, t: P.copy(cq[:, i, :], ps, t))
                P.wait("dve", [P.last("act")])

                def rope_pairs(x1, x2, i, ca, sa_, n, r, dst1=None, dst2=None):
                    co = bc(C(ca).rearrange("p (i r) -> p i r", i=4)[:, i, :], 1, n)
                    si = bc(C(sa_).rearrange("p (i r) -> p i r", i=4)[:, i, :], 1, n)
                    tm = [rt[:, m_, 0:n * r].rearrange("p (h r) -> p h r", h=n) for m_ in range(4)]
                    P.tt(tm[0], x1, co, ALU.mult)
                    P.tt(tm[1], x2, si, ALU.mult)
                    P.tt(tm[2], x1, si, ALU.mult)
                    P.tt(tm[3], x2, co, ALU.mult)
                    P.tt(x1 if dst1 is None else dst1, tm[0], tm[1], ALU.subtract)
                    return P.tt(x2 if dst2 is None else dst2, tm[2], tm[3], ALU.add)

                tkd = None
                for i in range(4):
                    v = qa[:, i, :].rearrange("p (h r a) -> p h r a", h=8, a=2)
                    rope_pairs(v[:, :, :, 0], v[:, :, :, 1], i, "cosa", "sina", 8, 32)
                    v = ka[:, i, :].rearrange("p (h r a) -> p h r a", h=2, a=2)
                    rope_pairs(v[:, :, :, 0], v[:, :, :, 1], i, "cosa", "sina", 2, 32)
                    for a in range(2):
                        t = P.op("dve", lambda e, a=a, i=i: e.tensor_copy(
                            kd[:, :, a, :], ka[:, i, :].rearrange("p (g r) -> p g r", g=2)), tkd)
                    to_T(lambda k: qa[:, i, k * 128:(k + 1) * 128], 4,
                         lambda k0, n, ps, t: P.copy(qaT[:, :, i * 128:(i + 1) * 128], ps, t), t)
                    tkd = to_T(lambda k: kd[:, k, :, :].rearrange("p a r -> p (a r)"), 2,
                               lambda k0, n, ps, t: P.copy(kaT[:, :, i * 128:(i + 1) * 128], ps, t), t)
                te = [P.last("act"), P.last("dve")]

                def gated(i, c0):
                    def f(ps, r, t, tr):
                        o = ZO[:, i, c0:c0 + 64]
                        return P.stt(o, ps, r, o, ALU.mult, ALU.mult, t, tr)
                    return f

                units = []
                for i in range(4):
                    for hh in range(8):
                        g, p0 = hh // 4, 64 * (hh % 2)
                        ql = qaT[p0:p0 + 64, hh // 2, i * 128:(i + 1) * 128]
                        k0, nk = (0, 512) if i < 2 else (256, 256)
                        units.append({
                            "after": te, "scale": 0.125, "put": gated(i, hh * 64), "nk": nk,
                            "qk": [(0, nk, ql, kaT[p0:p0 + 64, g, k0:k0 + nk])], "sink": S("sink")[:, hh:hh + 1],
                            "peak": peak_masked(C("amask")[:, i * 512:(i + 1) * 512]) if i < 2 else peak,
                            "v": [va[:, j, g * 64:g * 64 + 64] for j in range(k0 // 128, 4)]})
                attend(units)

                cqT = xs[:, :, :].rearrange("p a b -> p (a b)")[:, 0:1536].rearrange("p (k t) -> p k t", k=3)
                ckT = P.sb(sa, "ckT", [128, 2, 512])
                rstd([cq[:, i, 0:384] for i in range(4)], 384, 4, P.last("pe"))
                t = rstd([ck[:, i, :] for i in range(4)], 256, 4, P.last("pe"), c0=4)
                for i in range(4):
                    t = P.ts(cq[:, i, 0:384], cq[:, i, 0:384], rs[:, i:i + 1], None, ALU.mult, None, t)
                    to_T(lambda k: cq[:, i, 0:384].rearrange("p (d k) -> p k d", k=3)[:, k, :], 3,
                         lambda k0, n, ps, t: P.tt(cqT[:, :, i * 128:(i + 1) * 128], ps, bc(S("qng"), 2, 128), ALU.mult, t), t)
                for i in range(4):
                    t = P.ts(ck[:, i, :], ck[:, i, :], rs[:, 4 + i:5 + i], None, ALU.mult, None, t)
                    to_T(lambda k: ck[:, i, :].rearrange("p (d k) -> p k d", k=2)[:, k, :], 2,
                         lambda k0, n, ps, t: P.tt(ckT[:, :, i * 128:(i + 1) * 128], ps, bc(S("kvng"), 2, 128), ALU.mult, t), t)
                krp = P.sb(sa, "krp", [128, 4, 32])
                P.op("dve", lambda e: e.tensor_copy(krp[:, :, :], cq[:, :, 384:416]))
                rows = cq[:, :, :].rearrange("p i n -> p (i n)")[:, 0:1536].rearrange("p (i h r) -> p i h r", i=4, h=4)
                qbT = UT[0:96, :, :]

                def head_T(dst, c, *after):
                    for hh in range(4):
                        b, free = P.bank()
                        P.wait("pe", [free, after])
                        for i in range(4):
                            t = P.tr(b.t[0:96, i * 128:(i + 1) * 128], rows[:, i, hh, :], ident, inc=i == 3)
                        b.readers = [P.copy(dst[0:96, 4 * c + hh, :], b.t[0:96, :], t)]
                    return t

                P.wait("pe", [P.last("dve")])
                w = W(d["b_w_uq"].rearrange("(p k) n -> p k n", k=3))
                trow = None
                for c in range(2):
                    for i in range(4):
                        b, free = P.bank()
                        t = P.mm(b.t[:, 0:384], [(cqT[:, k, i * 128:(i + 1) * 128], w.v[:, k, c * 384:c * 384 + 384]) for k in range(3)],
                                 w.tok, free)
                        b.readers = [P.copy(rows[:, i, :, :], b.t[:, 0:384].rearrange("p (h r) -> p h r", h=4), t, trow, eng="dve")]
                        v = rows[:, i, :, 64:96].rearrange("p h (r a) -> p h r a", a=2)
                        tr_ = rope_pairs(v[:, :, :, 0], v[:, :, :, 1], i, "cosb", "sinb", 4, 16)
                    trow = head_T(qbT, c, tr_)
                w.done(t)
                w = W(d["b_w_ukv"].rearrange("(p k) n -> p k n", k=2))
                for i in range(4):
                    v = krp[:, i:i + 1, :].rearrange("p h (r a) -> p h r a", a=2)
                    rope_pairs(v[:, :, :, 0], v[:, :, :, 1], i, "cosb", "sinb", 1, 16)
                for c in range(2):
                    for i in range(4):
                        b, free = P.bank()
                        t = P.mm(b.t[:, :], [(ckT[:, k, i * 128:(i + 1) * 128], w.v[:, k, c * 512:c * 512 + 512]) for k in range(2)],
                                 w.tok, free)
                        ps = b.t[:, :].rearrange("p (h a r) -> p h a r", h=4, a=2)
                        P.copy(rows[:, i, :, 0:64], ps[:, :, 0, :], t, trow, eng="dve")
                        b.readers = [P.copy(vb[:, i, 4 * c:4 * c + 4, :], ps[:, :, 1, :], t, eng="dve")]
                        tr_ = P.op("dve", lambda e, i=i: e.tensor_copy(rows[:, i, :, 64:96], bc(krp[:, i, :], 1, 4)))
                    trow = head_T(kbT, c, tr_)
                w.done(t)
                te = [P.last("act"), P.last("dve")]
                units = []
                for i in range(4):
                    for hh in range(8):
                        k0, nk = (0, 512) if i < 2 else (256, 256)
                        units.append({
                            "after": te, "scale": 96.0 ** -0.5, "put": gated(i, 512 + hh * 64), "nk": nk,
                            "qk": [(0, nk, qbT[0:96, hh, i * 128:(i + 1) * 128], kbT[0:96, hh, k0:k0 + nk])],
                            "peak": peak, "v": [vb[:, j, hh, :] for j in range(k0 // 128, 4)]})
                attend(units)
                P.barrier()

            def rows_T(dst, n, *after):
                for i in range(n):
                    to_T(lambda k: ZO[:, i, :].rearrange("p (d k) -> p k d", k=8)[:, k, :], 8,
                         lambda k0, m, ps, t: P.copy(dst[:, k0:k0 + m, i * 128:(i + 1) * 128], ps, t), *after)
                return [P.last("act"), P.last("dve")]
            te = rows_T(UT, 4, P.last("dve"))
            wo = d["ab_out_w"].rearrange("(p k) n -> p k n", k=8)
            lin2(UT, [W(wo[:, 0:4, :]), W(wo[:, 4:8, :])], range(4), residual, te)
            P.barrier()

        with ExitStack() as sc:
            UT = P.sb(sc, "UT1", [128, 8, 512])
            tu = modulated(UT, 1)
            row_bcast(grow[:, 0, :], lambda k: mod[:, 1, 16 + k, 0:1], P.last("dve"))
            qcT = P.sb(sc, "qcT", [128, 8, 256])
            kcT2 = P.sb(sc, "kcT2", [128, 8, 512])
            vcr = P.sb(sc, "vcr", [128, 4, 1024])
            ZO = P.sb(sc, "ZO1", [128, 2, 1024])
            M4 = [(j * 128, 128) for j in range(4)]
            for c in range(2):
                linT(UT, W(d["w_c"][c]), M4, 256, lambda j, ps, t: P.copy(qcT[:, 4 * c + j, :], ps, t), tu)
            for c in range(2):
                linT(UT, W(d["w_c"][2 + c]), M4, 512, lambda j, ps, t: P.copy(kcT2[:, 4 * c + j, :], ps, t))
            for c in range(2):
                lin(UT, W(d["w_c"][4 + c]), 512, range(4), lambda i, ps, t: P.copy(vcr[:, i, c * 512:c * 512 + 512], ps, t))
            for c in range(2):
                lin(UT, W(d["w_c"][6 + c]), 512, range(2), lambda i, ps, t: P.act(ZO[:, i, c * 512:c * 512 + 512], ps, ACT.Silu, t))
            te = [P.last("act"), P.last("dve")]

            def gated(i, c0):
                def f(ps, r, t, tr):
                    o = ZO[:, i, c0:c0 + 64]
                    return P.stt(o, ps, r, o, ALU.mult, ALU.mult, t, tr)
                return f

            def peak_biased(bias, tb):
                def f(x, s, m, t):
                    P.stt(s[:, 0:256], x[:, 0:256], 0.125, bias, ALU.mult, ALU.add, t, tb)
                    t = P.ts(s[:, 256:512], x[:, 256:512], 0.125, None, ALU.mult, None)
                    P.red(m, s, ALU.max)
                    return s, [t]
                return f

            for c in range(2):
                w = W(d["bias"][c])
                v = w.v.rearrange("p h (r k) -> p (h r) k", k=64)
                tb = P.tt(v, v, bc(C("colmask"), 1, 64), ALU.add, w.tok, eng="pool")
                units = []
                for hh in range(8 * c, 8 * c + 8):
                    for i in range(2):
                        p0 = 64 * (hh % 2)
                        units.append({
                            "after": te, "scale": 1.0, "put": gated(i, hh * 64), "nk": 512,
                            "qk": [(0, 512, qcT[p0:p0 + 64, hh // 2, i * 128:(i + 1) * 128], kcT2[p0:p0 + 64, hh // 2, :])],
                            "peak": peak_biased(w.v[:, hh % 8, i * 256:(i + 1) * 256], tb),
                            "v": [vcr[:, j, hh * 64:hh * 64 + 64] for j in range(4)]})
                attend(units)
                w.done(P.last("dve"))
            for i in range(2):
                to_T(lambda k: ZO[:, i, :].rearrange("p (d k) -> p k d", k=8)[:, k, :], 8,
                     lambda k0, n, ps, t: P.copy(qcT[:, k0:k0 + n, i * 128:(i + 1) * 128], ps, t), P.last("dve"))
            te = [P.last("act"), P.last("dve")]
            wo = d["c_out_w"].rearrange("(p k) n -> p k n", k=8)
            lin2(qcT, [W(wo[:, 0:4, :]), W(wo[:, 4:8, :])], range(2), residual, te)
            t = final_norm("fin2", lambda i: xs[:, i, :])
            o = out.rearrange("o (t p) d -> p (o t) d", p=128)
            tf = P.dma("sp", o, xs[:, :, :], "out", s_out, 16, t)
            P.wait("sp", [tf])
            P.barrier()

        block = ctx.enter_context(nc.Block())

        @block.tensor
        def _(e):
            for f in P.q["pe"]:
                f(e)

        @block.scalar
        def _(e):
            for f in P.q["act"]:
                f(e)

        @block.vector
        def _(e):
            for f in P.q["dve"]:
                f(e)

        @block.gpsimd
        def _(e):
            for f in P.q["pool"]:
                f(e)

        @block.sync
        def _(e):
            for f in P.q["sp"]:
                f(e)


def constants():
    f = np.float32
    p = np.arange(128)
    o = {"ident": np.eye(128)}
    o["inv"] = np.tile((f(1.0) / (f(10000.0) ** (np.arange(32, dtype=f) / f(32)))).astype(f), (128, 1))
    o["causal"] = np.where(p[None, :] <= p[:, None], 0.0, NEG)
    t = p[:, None, None] + 128 * np.arange(2)[None, :, None]
    ok = (16 * np.arange(15) + 31)[None, None, :] <= t
    o["cmpadd"] = np.where(ok, 0.0, NEG)
    o["cmpok"] = ok * 1.0
    k = np.arange(512)[None, None, :]
    o["amask"] = np.where((np.abs(k - t) <= 128) | (k >= 256), 0.0, NEG)
    lev = []
    s, q = p[:, None], p[None, :]
    for m in LEVELS:
        lev.append((s // (2 * m) == q // (2 * m)) & (s // m % 2 == 0) & (q // m % 2 == 1))
    lev.append(s == q)
    o["lev"] = np.stack(lev, 1) * 1.0
    qc, kc = (p % 64)[:, None], np.arange(64)[None, :]
    cs = np.clip(qc - 8, 0, 48)
    o["colmask"] = np.where((kc >= cs) & (kc < cs + 16), 0.0, NEG)
    tok = p[:, None] + 128 * np.arange(2)[None, :]
    for name, d in (("a", 64), ("b", 32)):
        n = d // 4
        inv = (f(10000.0) ** (-np.arange(n, dtype=f) / f(n))).astype(f)
        row, col = (tok // 64).astype(f), (tok % 64).astype(f)
        ang = np.concatenate([row[..., None] * inv, col[..., None] * inv], -1).astype(f)
        one = np.zeros((128, 2, 2 * n), f)
        o["cos" + name] = np.concatenate([np.cos(ang), one + 1], 1)
        o["sin" + name] = np.concatenate([np.sin(ang), one], 1)
    o["desc"] = np.tile(np.arange(8, 0, -1), (128, 1))
    o["nhalf"] = np.full((128, 16), -0.5)
    return np.concatenate([np.asarray(o[n], f).reshape(128, w) for n, w in CONST], 1)


def tiles(w, k, *cols):
    w = w.reshape(128, k, w.shape[1])
    return np.ascontiguousarray(np.concatenate([w[:, :, c] for c in cols], 2))


def kernel(**inputs):
    import concourse.bacc as _bacc
    from concourse import mybir as _mybir
    from concourse.bass_utils import run_bass_kernel_spmd as _run

    a = {k: np.asarray(v) for k, v in inputs.items()}
    f = np.float32
    w_in = a["w_in"][0]
    c = np.cumsum([0, 512, 128, 128, 128, 128, 128, 128, 24, 256, 256, 512, 16, 512, 1024, 1024])
    col = [slice(c[i], c[i + 1]) for i in range(15)]
    ab = a["ab_in_w_2"][0]
    cin = a["c_in_w_2"][0]

    def kmaj(v, k):
        return v.reshape(128, k)

    def tmaj(v, k):
        return v.reshape(k, 128).T

    def rep(v):
        return np.broadcast_to(v.reshape(1, -1), (128, v.size))

    def pairs(pos):
        return pos.reshape(16, 128).T

    def half(s, n):
        return slice(s.start + n * 64, s.start + n * 64 + 64)

    wr = np.concatenate([a["w_grp"][0], a["w_exp"][0]], 1).reshape(128, 288)
    wa2 = np.zeros((128, 256), f)
    wa2[0:16] = a["gla_w_a2"][0]
    small = {
        "gmix": kmaj(a["g_mix"][0], 8), "gffn": kmaj(a["g_ffn"][0], 8), "gfin": kmaj(a["g_final"], 8),
        "ng0": kmaj(a["norm_g_2"][0], 8), "ng1": kmaj(a["norm_g_2"][1], 8), "fin2": kmaj(a["final_g_2"], 8),
        "qng": kmaj(a["b_q_norm_g_2"][0], 3), "kvng": kmaj(a["b_kv_norm_g_2"][0], 2),
        "glang": kmaj(a["gla_norm_g"][0], 4), "b1k": tmaj(a["cmp_b1_k"][0], 2), "b1v": tmaj(a["cmp_b1_v"][0], 2),
        "glaba": tmaj(a["gla_b_a"][0], 2),
        "cc": np.stack([kmaj(a["c_2"][0], 8), kmaj(a["c_ctx_2"], 8)], 2).reshape(128, 16),
        "adab": a["ada_b_2"].reshape(2, 3, 128, 8).transpose(2, 0, 1, 3).reshape(128, 48),
        "posk": pairs(a["cmp_pos_k"][0]), "posv": pairs(a["cmp_pos_v"][0]),
        "w2k": a["cmp_w2_k"][0].reshape(2, 128, 64).transpose(1, 0, 2).reshape(128, 128),
        "w2v": a["cmp_w2_v"][0].reshape(2, 128, 64).transpose(1, 0, 2).reshape(128, 128),
        "wr": wr, "wa2": wa2, "b2k": rep(a["cmp_b2_k"][0]), "b2v": rep(a["cmp_b2_v"][0]),
        "brout": np.concatenate([rep(a["b_grp"][0]), rep(a["b_exp"][0])], 1), "sink": rep(a["a_sink_2"][0]),
    }
    pos = a["positions"][0]
    ends = np.zeros(128, np.int64)
    ends[0:15] = 16 * np.arange(15) + 31
    t = np.arange(256)
    dr = t[None, :] // 64 - t[:, None] // 64 + 7
    dc = np.clip(t[None, :] % 64 - t[:, None] % 64 + 15, 0, 30)
    bias = a["c_rpb_2"][0][:, dr, dc].reshape(2, 8, 2, 128, 256).transpose(0, 3, 1, 2, 4).reshape(2, 128, 8, 512)

    def pos_tile(w):
        return np.ascontiguousarray(w.reshape(16, 128, 256).transpose(1, 0, 2))

    ada = a["ada_w_2"].reshape(2, 128, 8, 3, 128, 8).transpose(0, 3, 5, 1, 2, 4)
    ada = ada.reshape(2, 6, 4, 128, 8, 128).transpose(0, 1, 3, 4, 2, 5).reshape(2, 6, 128, 8, 512)
    send = {
        "const": constants(),
        "small": np.concatenate([np.asarray(small[n]).reshape(128, w) for n, w in SMALL], 1),
        "pos": np.stack([pos[0:128], pos[128:256], pos[ends]], 1),
        "x": a["x"], "ctx": a["ctx_2"],
        "w_gqk": tiles(w_in, 8, col[8], col[9]), "w_sm": tiles(w_in, 8, col[7], col[11]),
        "w_gv": tiles(w_in, 8, col[10]), "w_q": tiles(w_in, 8, col[0]),
        "w_kv": tiles(w_in, 8, col[3], col[5], col[4], col[6]),
        "w_kvc": tiles(w_in, 8, *[half(col[m], g) for m in (1, 2) for g in (0, 0, 1, 1)]),
        "w1k": pos_tile(a["cmp_w1_k"][0]), "w1v": pos_tile(a["cmp_w1_v"][0]),
        "w_gr": tiles(w_in, 8, col[12]),
        "w_m": np.stack([tiles(w_in, 8, slice(c[13] + 512 * j, c[13] + 512 * j + 512)) for j in range(4)]),
        "w_proj_nsa": a["w_proj_nsa"][0], "w_proj_gla": a["w_proj_gla"][0], "w_out": a["w_out"][0],
        "w_gate": a["w_gate"][0], "w_up": a["w_up"][0], "w_down": a["w_down"][0],
        "w_ada": np.ascontiguousarray(ada),
        "w_qa": tiles(ab, 8, slice(0, 512)),
        "w_kva": tiles(ab, 8, slice(512, 768), slice(1664, 1920)),
        "w_za": tiles(ab, 8, slice(768, 1280)), "w_zb": tiles(ab, 8, slice(1952, 2464)),
        "w_cq": tiles(ab, 8, slice(1280, 1664), slice(1920, 1952)),
        "b_w_uq": a["b_w_uq_2"][0], "b_w_ukv": a["b_w_ukv_2"][0], "ab_out_w": a["ab_out_w_2"][0],
        "w_c": np.stack([tiles(cin, 8, slice(512 * j, 512 * j + 512)) for j in range(8)]),
        "bias": np.ascontiguousarray(bias), "c_out_w": a["c_out_w_2"][0],
    }
    nc = _bacc.Bacc("TRN2", target_bir_lowering=False, num_devices=1)
    arrays, d = {}, {}
    for name, v in send.items():
        v = np.ascontiguousarray(v)
        arrays[f"in_{name}"] = v
        d[name] = nc.dram_tensor(f"in_{name}", v.shape, _mybir.dt.from_np(v.dtype), kind="ExternalInput").ap()
    out = nc.dram_tensor("out_0", (1, 256, 1024), _mybir.dt.float32, kind="ExternalOutput").ap()
    build(nc, d, out)
    r = _run(nc, [arrays], core_ids=[0])
    return r.results[0]["out_0"]
```

```python
from contextlib import ExitStack

import numpy as np

import concourse.bass as bass
from concourse import mybir
from concourse.alu_op_type import AluOpType as ALU

F32 = mybir.dt.float32
I32 = mybir.dt.int32
U32 = mybir.dt.uint32
ACT = mybir.ActivationFunctionType
X = mybir.AxisListType.X
EPS = 1e-6
NEG = -1e30
NSLOT = 4
XSLOT = 2
CAP = 64
SLOT = 4096
LEVELS = (64, 32, 16, 8, 4, 2, 1)

SMALL = [("gmix", 8), ("gffn", 8), ("gfin", 8), ("ng0", 8), ("ng1", 8), ("fin2", 8), ("qng", 3),
         ("kvng", 2), ("glang", 4), ("b1k", 2), ("b1v", 2), ("glaba", 2), ("cc", 16), ("adab", 48),
         ("posk", 16), ("posv", 16), ("w2k", 128), ("w2v", 128), ("wr", 288), ("wa2", 256),
         ("b2k", 64), ("b2v", 64), ("brout", 36), ("sink", 8)]
CONST = [("ident", 128), ("inv", 32), ("causal", 256), ("cmpadd", 30), ("cmpok", 30), ("amask", 1024),
         ("lev", 128 * (len(LEVELS) + 1)), ("colmask", 64), ("cosa", 128), ("sina", 128), ("cosb", 64),
         ("sinb", 64), ("desc", 8), ("nhalf", 16),
         ("before", 128), ("ones", 128), ("iota", 64), ("pick", 2)]


def offsets(fields):
    out, at = {}, 0
    for name, w in fields:
        out[name] = (at, w)
        at += w
    return out, at


class Bank:
    def __init__(self, t):
        self.t = t
        self.readers = []


class Prog:

    ENGINES = ("pe", "act", "dve", "pool", "sp")

    def __init__(self, nc, ctx):
        self.nc = nc
        self.ctx = ctx
        self.q = {e: [] for e in self.ENGINES}
        self.sem = {e: ctx.enter_context(nc.semaphore("s_" + e)) for e in self.ENGINES}
        self.n = {e: 0 for e in self.ENGINES}
        self.seen = {e: {} for e in self.ENGINES}
        self.flip = 0
        self.banks = [Bank(ctx.enter_context(nc.psum_tensor(f"ps{i}", [128, 512], F32))) for i in range(8)]
        self.ring = self.banks
        self.at = 0

    def wait(self, eng, toks):
        for t in toks:
            if t is None:
                continue
            if isinstance(t, (list, tuple)) and not (t and isinstance(t[0], str)):
                self.wait(eng, t)
                continue
            key, sem, v = t
            if self.seen[eng].get(key, 0) < v:
                self.seen[eng][key] = v
                self.q[eng].append(lambda e, s=sem, v=v: e.wait_ge(s, v))

    def last(self, eng):
        return (eng, self.sem[eng], self.n[eng]) if self.n[eng] else None

    def op(self, eng, fn, *after, inc=True):
        if eng != "pe":
            self.wait(eng, [self.last(eng)])
        self.wait(eng, after)
        if not inc:
            self.q[eng].append(fn)
            return None
        self.n[eng] += 1
        self.q[eng].append(lambda e, s=self.sem[eng]: fn(e).then_inc(s, 1))
        return (eng, self.sem[eng], self.n[eng])

    def dma(self, eng, out, in_, name, sem, count, *after):
        self.wait(eng, after)
        self.q[eng].append(lambda e: e.dma_start(out, in_).then_inc(sem, 16))
        return (name, sem, count)

    def barrier(self):
        for e in ("pe", "act", "dve", "pool"):
            self.wait(e, [self.last(o) for o in ("pe", "act", "dve", "pool") if o != e])

    def branch(self, flag, least, many, few, *after):
        for e in self.ENGINES:
            self.wait(e, after)
        outer, n0 = self.q, dict(self.n)
        seen0 = {e: dict(v) for e, v in self.seen.items()}
        sides = []
        for f in (many, few):
            self.q = {e: [] for e in self.ENGINES}
            self.n = dict(n0)
            self.seen = {e: dict(v) for e, v in seen0.items()}
            f()
            sides.append((self.q, self.n))
        self.n = {e: max(n[e] for _, n in sides) for e in self.ENGINES}
        for q, n in sides:
            for e in self.ENGINES:
                if n[e] < self.n[e]:
                    q[e].append(lambda g, s=self.sem[e], k=self.n[e] - n[e]: g.drain().then_inc(s, k))
        self.q = outer
        self.seen = seen0
        for e in self.ENGINES:
            self.q[e].append((flag, least, sides[0][0][e], sides[1][0][e]))

    def emit(self, eng, items):
        for f in items:
            if not isinstance(f, tuple):
                f(eng)
                continue
            flag, least, many, few = f
            v = eng.value_load(flag)
            with eng.If(v > least):
                self.emit(eng, many)
            with eng.Else():
                self.emit(eng, few)

    def bank(self):
        b = self.ring[self.at % len(self.ring)]
        self.at += 1
        assert b.readers is not None
        r, b.readers = b.readers, None
        return b, r

    def mm(self, out, pairs, *after, start=True, stop=True, skip=False):
        self.wait("pe", after)
        for i, (l, r) in enumerate(pairs):
            t = self.op("pe", lambda e, l=l, r=r, i=i: e.matmul(
                out, l, r, start=start and i == 0, stop=stop and i == len(pairs) - 1, skip_group_check=skip),
                inc=i == len(pairs) - 1)
        return t

    def tr(self, out, in_, ident, *after, inc=True):
        return self.op("pe", lambda e: e.transpose(out, in_, ident), *after, inc=inc)

    def tt(self, out, a, b, op, *after, eng="dve"):
        return self.op(eng, lambda e: e.tensor_tensor(out, a, b, op), *after)

    def ts(self, out, a, s1, s2, op0, op1, *after, eng="dve"):
        if op1 is None:
            return self.op(eng, lambda e: e.tensor_scalar(out, a, s1, None, op0), *after)
        return self.op(eng, lambda e: e.tensor_scalar(out, a, s1, s2, op0, op1), *after)

    def stt(self, out, a, s, b, op0, op1, *after):
        return self.op("dve", lambda e: e.scalar_tensor_tensor(out=out, in0=a, scalar=s, in1=b, op0=op0, op1=op1),
                       *after)

    def red(self, out, a, op, *after):
        return self.op("dve", lambda e: e.tensor_reduce(out, a, X, op), *after)

    def ttr(self, out, a, b, init, op0, op1, acc, *after):
        return self.op("dve", lambda e: e.tensor_tensor_reduce(out, a, b, 1.0, init, op0, op1, acc), *after)

    def recip(self, out, a, *after):
        return self.op("dve", lambda e: e.reciprocal(out, a), *after)

    def act(self, out, in_, f, *after, bias=None, scale=1.0, acc=None):
        kw = {"scale": scale}
        if bias is not None:
            kw["bias"] = bias
        if acc is not None:
            kw["accum_out"] = acc
        return self.op("act", lambda e: e.activation(out, in_, f, **kw), *after)

    def copy(self, out, in_, *after, eng=None):
        if eng is None:
            self.flip ^= 1
            eng = "act" if self.flip else "dve"
        if eng == "act":
            return self.act(out, in_, ACT.Copy, *after)
        return self.op("dve", lambda e: e.tensor_copy(out, in_), *after)

    def sb(self, scope, name, shape, dt=F32):
        return scope.enter_context(self.nc.sbuf_tensor(name, shape, dt))


def bc(ap, axis, n):
    a = ap.unsqueeze(axis)
    shape = list(a.shape)
    shape[axis] = n
    return a.to_broadcast(shape)


def build(nc, d, out):
    with ExitStack() as ctx:
        P = Prog(nc, ctx)
        s_load = ctx.enter_context(nc.semaphore("s_load"))
        s_out = ctx.enter_context(nc.semaphore("s_out"))
        ring = P.sb(ctx, "wring", [128, NSLOT, SLOT])
        s_w = [ctx.enter_context(nc.semaphore(f"s_w{i}")) for i in range(NSLOT + XSLOT)]
        slots = list(range(NSLOT))
        views = [ring[:, i, :] for i in range(NSLOT)] + [None] * XSLOT
        slot_n = [0] * (NSLOT + XSLOT)
        slot_reader = [None] * (NSLOT + XSLOT)
        at = [0]
        class W:

            def __init__(self, src):
                self.i = i = slots[at[0] % len(slots)]
                at[0] += 1
                n = 1
                for s in src.shape[1:]:
                    n *= s
                v = views[i][0:src.shape[0], 0:n]
                assert slot_reader[i] != "held"
                if len(src.shape) == 3:
                    v = v.rearrange("p (a b) -> p a b", a=src.shape[1])
                elif len(src.shape) == 4:
                    v = v.rearrange("p (a b c) -> p a b c", a=src.shape[1], b=src.shape[2])
                slot_n[i] += 16
                self.v = v
                self.tok = P.dma("sp", v, src, f"w{i}", s_w[i], slot_n[i], slot_reader[i])
                slot_reader[i] = "held"

            def done(self, *toks):
                slot_reader[self.i] = list(toks)

        const_o, const_n = offsets(CONST)
        small_o, small_n = offsets(SMALL)
        cst = P.sb(ctx, "cst", [128, const_n])
        sml = P.sb(ctx, "sml", [128, small_n])
        post = P.sb(ctx, "post", [128, 3], I32)
        h = P.sb(ctx, "h", [128, 4, 1024])
        ld = [0]

        def load(o, i):
            ld[0] += 16
            P.dma("sp", o, i, "load", s_load, ld[0])

        load(cst[:, :], d["const"])
        load(sml[:, :], d["small"])
        load(post[:, :], d["pos"])
        load(h[:, 0:2, :], d["x"].rearrange("o (t p) d -> p (o t) d", p=128))
        load(h[:, 2:4, :], d["ctx"].rearrange("o (t p) d -> p (o t) d", p=128))
        T0 = ("load", s_load, ld[0])
        for e in ("pe", "act", "dve", "pool"):
            P.wait(e, [T0])

        def C(name, k=None):
            a, w = const_o[name]
            return cst[:, a:a + w]

        def S(name):
            a, w = small_o[name]
            return sml[:, a:a + w]

        ident = C("ident")
        NB = 3
        bS = P.sb(ctx, "bS", [128, 2, 512])
        bP = P.sb(ctx, "bP", [128, NB, 512])
        bT = P.sb(ctx, "bT", [128, NB, 512])
        st = P.sb(ctx, "st", [128, 4, 8])
        ss = P.sb(ctx, "ss", [128, 8])
        rs = P.sb(ctx, "rs", [128, 8])
        xs = P.sb(ctx, "xs", [128, 2, 1024])
        grow = P.sb(ctx, "grow", [128, 2, 1024])
        rt = P.sb(ctx, "rt", [128, 4, 256])
        scT = grow[:, 0, 0:256].rearrange("p (k w) -> p k w", k=8)
        mod = P.sb(ctx, "mod", [128, 2, 24, 2])
        Amod = P.sb(ctx, "Amod", [128, 2, 2, 8])

        def rstd(rows, width, n, *after, c0=0):
            for i, r in enumerate(rows):
                P.ttr(xs[:, 0, 0:width], r, r, 0.0, ALU.mult, ALU.add, ss[:, c0 + i:c0 + i + 1], *after)
            s = ss[:, c0:c0 + n]
            t = P.ts(s, s, 1.0 / width, EPS, ALU.mult, ALU.add)
            return P.tt(rs[:, c0:c0 + n], s, C("nhalf")[:, 0:n], ALU.pow, t, eng="pool")

        def to_T(cols, nk, put, *after):
            for k0 in range(0, nk, 4):
                n = min(4, nk - k0)
                b, free = P.bank()
                P.wait("pe", [after, free])
                for k in range(n):
                    t = P.tr(b.t[:, k * 128:k * 128 + 128], cols(k0 + k), ident, inc=k == n - 1)
                b.readers = [put(k0, n, b.t[:, 0:n * 128].rearrange("p (k t) -> p k t", k=n), t)]
            return t

        def norm_T(tiles, outT, A, B=None):
            t0 = rstd([r for r in tiles], 1024, len(tiles), P.last("pe"))
            last = None
            xsfree = [None, None]
            for i, r in enumerate(tiles):
                xv = xs[:, i % 2, :].rearrange("p (k d) -> p k d", k=8)
                tx = P.ts(xv, r.rearrange("p (d k) -> p k d", k=8), rs[:, i:i + 1], None, ALU.mult, None, t0, xsfree[i % 2])
                a, b2 = A(i), (B(i) if B else None)

                def put(k0, n, ps, t, i=i, a=a, b2=b2):
                    o = outT[:, k0:k0 + n, i * 128:(i + 1) * 128]
                    t = P.tt(o, ps, bc(a[:, k0:k0 + n], 2, 128), ALU.mult, t)
                    if b2 is not None:
                        P.tt(o, o, bc(b2[:, k0:k0 + n], 2, 128), ALU.add)
                    return t
                xsfree[i % 2] = to_T(lambda k, xv=xv: xv[:, k, :], 8, put, tx)
            return P.last("dve")

        def lin(xT, w, cols, tiles, put, *after, nk=8):
            for i in tiles:
                b, free = P.bank()
                t = P.mm(b.t[:, 0:cols], [(xT[:, k, i * 128:(i + 1) * 128], w.v[:, k, 0:cols]) for k in range(nk)],
                         w.tok, free, after)
                b.readers = [put(i, b.t[:, 0:cols], t)]
            w.done(t)

        def linT(xT, w, mtiles, n, put, *after, nk=8):
            for j, (c0, m) in enumerate(mtiles):
                b, free = P.bank()
                t = P.mm(b.t[0:m, 0:n], [(w.v[:, k, c0:c0 + m], xT[:, k, 0:n]) for k in range(nk)], w.tok, free, after)
                b.readers = [put(j, b.t[0:m, 0:n], t)]
            w.done(t)

        def lin2(xT, ws, tiles, put, *after):
            for i in tiles:
                for c in range(2):
                    b, free = P.bank()
                    t = P.mm(b.t[:, :], [(xT[:, k, i * 128:(i + 1) * 128], ws[k // 4].v[:, k % 4, c * 512:c * 512 + 512])
                                         for k in range(8)], ws[0].tok, ws[1].tok, free, after)
                    b.readers = [put(i, c, b.t[:, :], t)]
            for w in ws:
                w.done(t)

        pfree = [None] * NB
        tfree = [None] * NB
        sfree = [None] * 2

        def attend(units, other=iter(())):
            n = len(units)
            live = {}

            def scores(i):
                u = units[i]
                b, free = P.bank()
                P.wait("pe", [free, u["after"]])
                for col, w, l, r in u["qk"]:
                    t = P.mm(b.t[:, col:col + w], [(l, r)])
                live[i] = {"b": b, "t": t}

            def soft(i):
                u, L = units[i], live[i]
                x = L["b"].t[:, 0:u["nk"]]
                m = L["m"] = st[:, i % 4, :]
                P.wait("dve", [sfree[i % 2]])
                src, readers = u["peak"](x, bS[:, i % 2, 0:u["nk"]], m[:, 0:1], L["t"])
                sc = u["scale"]
                if u.get("sink") is not None:
                    P.ts(m[:, 1:2], m[:, 0:1], sc, u["sink"], ALU.mult, ALU.max)
                    t = P.ts(m[:, 1:2], m[:, 1:2], -1.0, None, ALU.mult, None)
                else:
                    t = P.ts(m[:, 1:2], m[:, 0:1], -sc, None, ALU.mult, None)
                p = bP[:, i % NB, 0:u["nk"]]
                te = P.act(p, src, ACT.Exp, t, pfree[i % NB], bias=m[:, 1:2], scale=sc, acc=m[:, 2:3])
                sfree[i % 2] = te
                L["b"].readers = readers + [te]
                if u.get("sink") is not None:
                    te = P.act(m[:, 3:4], u["sink"], ACT.Exp, bias=m[:, 1:2])
                L["p"] = te

            def turn(i):
                u, L = units[i], live[i]
                b, free = P.bank()
                nk = u["nk"]
                if u.get("ok") is not None:
                    p = bP[:, i % NB, 0:nk]
                    L["p"] = P.tt(p, p, u["ok"], ALU.mult, L["p"])
                P.wait("pe", [free, L["p"]])
                blocks = [(c, min(128, nk - c)) for c in range(0, nk, 128)]
                for j, (c, w) in enumerate(blocks):
                    t = P.tr(b.t[0:w, j * 128:(j + 1) * 128], bP[:, i % NB, c:c + w], ident, inc=j == len(blocks) - 1)
                pfree[i % NB] = t
                w = blocks[0][1]
                t = P.copy(bT[0:w, i % NB, 0:128 * len(blocks)], b.t[0:w, 0:128 * len(blocks)], t, tfree[i % NB],
                           eng="act")
                b.readers = [t]
                L["pt"] = t

            def mix(i):
                u, L = units[i], live.pop(i)
                b, free = P.bank()
                t = P.mm(b.t[:, 0:64], [(bT[0:v.shape[0], i % NB, j * 128:(j + 1) * 128], v) for j, v in enumerate(u["v"])],
                         free, L["pt"])
                tfree[i % NB] = t
                m = L["m"]
                tr = L["p"]
                if u.get("sink") is not None:
                    tr = P.tt(m[:, 2:3], m[:, 2:3], m[:, 3:4], ALU.add, tr)
                tr = P.recip(m[:, 4:5], m[:, 2:3], tr)
                b.readers = [u["put"](b.t[:, 0:64], m[:, 4:5], t, tr)]

            for s in range(n + 3):
                if s < n:
                    scores(s)
                next(other, None)
                if 0 <= s - 1 < n:
                    soft(s - 1)
                next(other, None)
                if 0 <= s - 2 < n:
                    turn(s - 2)
                if 0 <= s - 3 < n:
                    mix(s - 3)

        def own_half(dst, which, i, ps, t):
            for hp in range(2):
                o = slice(64 * hp, 64 * hp + 64)
                t = P.copy(dst[o, hp, which, i * 128:(i + 1) * 128], ps[o], t, eng="dve")
            return t

        def peak(x, s, m, t):
            return x, [P.red(m, x, ALU.max, t)]

        def peak_masked(mask):
            def f(x, s, m, t):
                t = P.ttr(s, x, mask, -3e38, ALU.add, ALU.max, m, t)
                return s, [t]
            return f

        def modulations():
            for l in range(2):
                for c in range(6):
                    w = W(d["w_ada"][l, c])
                    b, free = P.bank()
                    P.wait("pe", [w.tok, free, tsc])
                    for k in range(8):
                        o = slice(32 * (k % 4), 32 * (k % 4) + 32)
                        t = P.mm(b.t[o, :], [(scT[:, k, :], w.v[:, k, :])], start=k < 4, stop=k > 3)
                    w.done(t)
                    yield
                    part = rt[:, 2 * (c % 2):2 * (c % 2) + 2, :].rearrange("p a b -> p (a b)")
                    t = P.act(part, b.t[:, :], ACT.Copy, t)
                    b.readers = [t]
                    yield
                    b, free = P.bank()
                    P.wait("pe", [free, t])
                    for j in range(4):
                        t = P.mm(b.t[:, 2 * j:2 * j + 2], [(part[:, j * 128:(j + 1) * 128], C("pick"))])
                    yield
                    b.readers = [P.tt(mod[:, l, 4 * c:4 * c + 4, :], b.t[:, 0:8].rearrange("p (c w) -> p c w", w=2),
                                      bc(S("adab")[:, 24 * l + 4 * c:24 * l + 4 * c + 4], 2, 2), ALU.add, t)]
                    yield
                for wh in range(2):
                    P.stt(Amod[:, l, wh, :], mod[:, l, 8:16, wh], 1.0, S("ng0" if l == 0 else "ng1"), ALU.add, ALU.mult)

        P.op("pool", lambda e: e.memset(scT[:, :, :], 0.0))
        tsc = P.act(scT[:, :, 0:2], S("cc").rearrange("p (k w) -> p k w", w=2), ACT.Silu, P.last("pool"))

        with ExitStack() as sc:
            uT = P.sb(sc, "uT", [128, 8, 256])
            tu = norm_T([h[:, 0, :], h[:, 1, :]], uT, lambda i: S("gmix"))

            ang = P.sb(sc, "ang", [128, 3, 32])
            rr = P.sb(sc, "rr", [128, 3, 32])
            cos = P.sb(sc, "cos", [128, 3, 32])
            sin = P.sb(sc, "sin", [128, 3, 32])
            posf = P.sb(sc, "posf", [128, 3])
            P.op("dve", lambda e: e.tensor_copy(posf[:, :], post[:, :]))
            P.tt(ang[:, :, :], bc(C("inv"), 1, 3), bc(posf[:, :], 2, 32), ALU.mult)
            twopi = 2.0 * np.pi
            hi = float(np.float32(np.round(twopi * 128) / 128))
            mid = float(np.float32(np.round((twopi - hi) * 2.0 ** 19) / 2.0 ** 19))
            lo = float(np.float32(twopi - hi - mid))
            magic = 12582912.0
            P.ts(rr[:, :, :], ang[:, :, :], 1.0 / twopi, magic, ALU.mult, ALU.add)
            P.ts(rr[:, :, :], rr[:, :, :], -magic, None, ALU.add, None)
            for c in (hi, mid, lo):
                P.stt(ang[:, :, :], rr[:, :, :], -c, ang[:, :, :], ALU.mult, ALU.add)
            t = P.ts(ang[:, :, :], ang[:, :, :], 3.1415925, -3.1415925, ALU.min, ALU.max)
            P.act(sin[:, :, :], ang[:, :, :], ACT.Sin, t)
            t = P.act(rr[:, :, :], ang[:, :, :], ACT.Sin, scale=0.5)
            P.tt(rr[:, :, :], rr[:, :, :], rr[:, :, :], ALU.mult, t)
            P.ts(cos[:, :, :], rr[:, :, :], -2.0, 1.0, ALU.mult, ALU.add)

            qk = P.sb(sc, "qk", [128, 4, 256])
            w = W(d["w_gqk"])

            def put(j, ps, t):
                return P.ts(qk[:, j, :], ps, 0.125 if j < 2 else 1.0, None, ALU.mult, None, t)
            linT(uT, w, [(j * 128, 128) for j in range(4)], 256, put, tu)

            gate = P.sb(sc, "gate", [128, 2, 24])
            alow = P.sb(sc, "alow", [16, 256])
            w = W(d["w_sm"])
            for i in range(2):
                b, free = P.bank()
                t = P.mm(b.t[:, 0:24], [(uT[:, k, i * 128:(i + 1) * 128], w.v[:, k, 0:24]) for k in range(8)], w.tok, free)
                b.readers = [P.act(gate[:, i, :], b.t[:, 0:24], ACT.Sigmoid, t)]
            linT(uT, w, [(24, 16)], 256, lambda j, ps, t: P.copy(alow[:, :], ps, t))
            ta = P.last("act"), P.last("dve")
            gv = P.sb(sc, "gv", [128, 2, 512])
            lin(uT, W(d["w_gv"]), 512, range(2), lambda i, ps, t: P.copy(gv[:, i, :], ps, t))

            q = P.sb(sc, "q", [128, 2, 512])
            kv = P.sb(sc, "kv", [128, 2, 512])
            lin(uT, W(d["w_q"]), 512, range(2), lambda i, ps, t: P.copy(q[:, i, :], ps, t, eng="act"))
            lin(uT, W(d["w_kv"]), 512, range(2), lambda i, ps, t: P.copy(kv[:, i, :], ps, t, eng="act"))

            Bt = P.sb(sc, "Bt", [128, 2, 16, 30])
            hid = P.sb(sc, "hid", [128, 2, 2, 30])
            kcr = P.sb(sc, "kcr", [16, 2, 2, 64])
            kcT = P.sb(sc, "kcT", [128, 2, 16])
            vc = P.sb(sc, "vc", [16, 2, 64])
            w = W(d["w_kvc"])

            def put(j, ps, t):
                m, g = j // 2, j % 2
                for jp in range(2):
                    p0 = 64 * jp
                    src = ps[p0:p0 + 64, :].rearrange("p (n s) -> p s n", s=16)
                    pos = S("posk" if m == 0 else "posv")
                    for half in range(2):
                        t = P.tt(Bt[p0:p0 + 64, m, 8 * half:8 * half + 8, 15 * g:15 * g + 15],
                                 src[:, jp:16:2, half:half + 15],
                                 bc(pos[p0:p0 + 64, 8 * half:8 * half + 8], 2, 15), ALU.add, t)
                return t
            linT(uT, w, [(j * 128, 128) for j in range(4)], 256, put)
            gr = P.sb(sc, "gr", [128, 2, 512])
            lin(uT, W(d["w_gr"]), 512, range(2), lambda i, ps, t: P.act(gr[:, i, :], ps, ACT.Silu, t))

            la = P.sb(sc, "la", [128, 2, 256])
            cum = P.sb(sc, "cum", [128, 2, 256])
            tmp = P.sb(sc, "tmp", [128, 2, 256])
            ones = P.sb(sc, "ones", [128, 256])
            tones = P.op("pool", lambda e: e.memset(ones[:, :], 1.0))
            b, free = P.bank()
            P.wait("pe", [ta, free])
            for j in range(2):
                tla = P.mm(b.t[:, j * 256:(j + 1) * 256], [(S("wa2")[0:16, j * 128:(j + 1) * 128], alow[:, :])])
            bla = b
            tb = P.last("dve")
            for m in range(2):
                w = W(d["w1k" if m == 0 else "w1v"])
                b1 = S("b1k" if m == 0 else "b1v")
                for c in range(2):
                    b, free = P.bank()
                    t = P.mm(b.t[:, 0:30], [(w.v[:, j, c * 128:(c + 1) * 128], Bt[:, m, j, :]) for j in range(16)],
                             w.tok, free, tb)
                    b.readers = [P.act(hid[:, m, c, :], b.t[:, 0:30], ACT.Gelu_apprx_tanh, t, bias=b1[:, c:c + 1])]
                w.done(t)
            th = P.last("act")
            for j in range(2):
                t = P.ts(la[:, j, :], bla.t[:, j * 256:(j + 1) * 256], S("glaba")[:, j:j + 1], None, ALU.add, None, tla)
            bla.readers = [t]
            t = P.stt(tmp[:, :, :], la[:, :, :], -1.0, la[:, :, :], ALU.mult, ALU.max)
            P.act(tmp[:, :, :], tmp[:, :, :], ACT.Exp, t, scale=-1.0)
            t = P.act(tmp[:, :, :], tmp[:, :, :], ACT.Ln, tones, bias=ones[:, 0:1])
            P.stt(la[:, :, :], la[:, :, :], 0.0, tmp[:, :, :], ALU.min, ALU.subtract, t)
            P.ts(la[:, :, :], la[:, :, :], 1.0 / 16.0, None, ALU.mult, None)
            for j in range(2):
                P.op("dve", lambda e, j=j: e.tensor_tensor_scan(cum[:, j, :], ones[:, :], la[:, j, :], 0.0, ALU.mult, ALU.add),
                     tones)

            def rope_half(dst1, dst2, x1, x2, co, si, tmps):
                a, b_, c_, d_ = tmps
                P.tt(a, x1, co, ALU.mult)
                P.tt(b_, x2, si, ALU.mult)
                P.tt(c_, x2, co, ALU.mult)
                P.tt(d_, x1, si, ALU.mult)
                P.tt(dst1, a, b_, ALU.subtract)
                return P.tt(dst2, c_, d_, ALU.add)

            kr = P.sb(sc, "kr", [128, 2, 4, 2, 64])
            for i in range(2):
                qv = q[:, i, :].rearrange("p (h a r) -> p h a r", h=8, a=2)
                tm = [rt[:, n, :].rearrange("p (h r) -> p h r", h=8) for n in range(4)]
                P.wait("dve", [P.last("act")])
                rope_half(qv[:, :, 0, :], qv[:, :, 1, :], qv[:, :, 0, :], qv[:, :, 1, :],
                          bc(cos[:, i, :], 1, 8), bc(sin[:, i, :], 1, 8), tm)
                kw = kv[:, i, 0:256].rearrange("p (h a r) -> p h a r", h=4, a=2)
                tm = [rt[:, n, 0:128].rearrange("p (h r) -> p h r", h=4) for n in range(4)]
                ko = kr[:, i, :, 0, :].rearrange("p h (a r) -> p h a r", a=2)
                rope_half(ko[:, :, 0, :], ko[:, :, 1, :], kw[:, :, 0, :], kw[:, :, 1, :],
                          bc(cos[:, i, :], 1, 4), bc(sin[:, i, :], 1, 4), tm)
                tk = P.op("dve", lambda e, i=i: e.tensor_copy(kr[:, i, :, 1, :], kr[:, i, :, 0, :]))
            qT = P.sb(sc, "qT", [128, 4, 256])
            kT = P.sb(sc, "kT", [128, 2, 4, 256])
            for hp in range(2):
                tz = P.op("pool", lambda e, hp=hp: e.memset(kT[64 - 64 * hp:128 - 64 * hp, hp, :, :], 0.0))
            for i in range(2):
                to_T(lambda k: q[:, i, k * 128:(k + 1) * 128], 4,
                     lambda k0, n, ps, t: P.copy(qT[:, :, i * 128:(i + 1) * 128], ps, t), tk)
                to_T(lambda k: kr[:, i, k, :, :].rearrange("p a r -> p (a r)"), 4,
                     lambda k0, n, ps, t: own_half(kT, slice(0, 4), i, ps, t), tk)

            for m in range(2):
                w2 = S("w2k" if m == 0 else "w2v").rearrange("p (c n) -> p c n", c=2)
                b2 = S("b2k" if m == 0 else "b2v")[0:15, :]
                b, free = P.bank()
                P.wait("pe", [free, th])
                for g in range(2):
                    t = P.mm(b.t[0:15, g * 64:g * 64 + 64],
                             [(hid[:, m, c, 15 * g:15 * g + 15], w2[:, c, :]) for c in range(2)])
                ps = b.t[0:15, 0:128].rearrange("p (g n) -> p g n", g=2)
                if m == 1:
                    b.readers = [P.tt(vc[0:15, :, :], ps, bc(b2, 1, 2), ALU.add, t)]
                    continue
                t = P.tt(kcr[0:15, :, 0, :], ps, bc(b2, 1, 2), ALU.add, t)
                b.readers = [t]
                kk = kcr[0:15, :, 0, :].rearrange("p g (a r) -> p g a r", a=2)
                tm = [rt[0:15, n, 0:64].rearrange("p (h r) -> p h r", h=2) for n in range(4)]
                rope_half(kk[:, :, 0, :], kk[:, :, 1, :], kk[:, :, 0, :], kk[:, :, 1, :],
                          bc(cos[0:15, 2, :], 1, 2), bc(sin[0:15, 2, :], 1, 2), tm)
                t = P.op("dve", lambda e: e.tensor_copy(kcr[0:15, :, 1, :], kcr[0:15, :, 0, :]))
                b, free = P.bank()
                for g in range(2):
                    t = P.tr(b.t[:, g * 16:g * 16 + 15], kcr[0:15, g, :, :].rearrange("p a r -> p (a r)"),
                             ident[0:15, 0:15], free, t)
                for g in range(2):
                    t = P.copy(kcT[:, g, 0:15], b.t[:, g * 16:g * 16 + 15], t, eng="dve")
                b.readers = [t]

            yn = P.sb(sc, "yn", [128, 2, 512])
            cf = P.sb(sc, "cf", [128, 4])
            cfn = [0]

            def nsa_put(kind, hh, i):
                def f(ps, r, t, tr):
                    cfn[0] += 1
                    c = cf[:, cfn[0] % 4:cfn[0] % 4 + 1]
                    P.tt(c, r, gate[:, i, 3 * hh + kind:3 * hh + kind + 1], ALU.mult, tr)
                    o = yn[:, i, hh * 64:hh * 64 + 64]
                    if kind == 0:
                        return P.ts(o, ps, c, None, ALU.mult, None, t)
                    return P.stt(o, ps, c, o, ALU.mult, ALU.add, t)
                return f

            Am = P.sb(sc, "Am", [128, 4, 3, 128])
            Q = P.sb(sc, "Q", [128, 2, 256])
            K = P.sb(sc, "K", [128, 2, 256])
            E = tmp
            P.op("pool", lambda e: e.memset(Am[:, :, :, :], 0.0))
            P.op("pool", lambda e: e.memset(Q[:, :, :], 0.0))
            P.op("pool", lambda e: e.memset(K[:, :, :], 0.0))
            tzero = P.last("pool")
            tcum = P.last("dve")
            go = q

            def place(hp, ps, li, *after):
                a0 = const_o["lev"][0] + 128 * li
                mk = bc(bc(cst[:, a0:a0 + 128].bitcast(U32), 1, 2), 1, 2)
                return P.op("dve", lambda e: e.copy_predicated(Am[:, hp:4:2, 0:2, :], mk, ps), *after)

            def decayed():
                tq = None
                for m in (128,) + LEVELS:
                    nb = 128 // m
                    for j in range(2):
                        v = cum[:, j, :].rearrange("p (n a m) -> p n a m", a=2, m=m)
                        ev = E[:, j, :].rearrange("p (n a m) -> p n a m", a=2, m=m)
                        mid_ = v[:, :, 0, m - 1:m].to_broadcast([128, nb, m])
                        P.tt(ev[:, :, 1, :], v[:, :, 1, :], mid_, ALU.subtract, tcum, eng="pool")
                        t = P.tt(ev[:, :, 0, :], mid_, v[:, :, 0, :], ALU.subtract, tcum, eng="pool")
                    yield
                    t = P.act(E[:, :, :], E[:, :, :], ACT.Exp, t)
                    yield
                    for j in range(2):
                        def part(x, a):
                            return x.rearrange("p (n a m) -> p n a m", a=2, m=m)[:, :, a, :]
                        P.tt(part(Q[:, j, :], 1), part(qk[:, j, :], 1), part(E[:, j, :], 1), ALU.mult, t, tq, eng="pool")
                        tk_ = P.tt(part(K[:, j, :], 0), part(qk[:, 2 + j, :], 0), part(E[:, j, :], 0), ALU.mult, t, tq, eng="pool")
                    yield
                    held = []
                    for hp in range(2):
                        p0 = 64 * hp
                        b, free = P.bank()
                        P.wait("pe", [tk_, free])
                        for pr in range(2):
                            for bl in range(1 if m == 128 else 2):
                                ks = K[p0:p0 + 64, pr, bl * 128:bl * 128 + 128]
                                qs = Q[p0:p0 + 64, pr, 128:256] if m == 128 else Q[p0:p0 + 64, pr, bl * 128:bl * 128 + 128]
                                tq = P.mm(b.t[:, (2 * pr + bl) * 128:(2 * pr + bl) * 128 + 128], [(ks, qs)])
                        held.append((b, tq))
                    yield
                    for hp, (b, t) in enumerate(held):
                        ps = b.t[:, :].rearrange("p (h b t) -> p h b t", h=2, b=2)
                        if m == 128:
                            b.readers = [P.copy(Am[:, hp:4:2, 2, :], ps[:, :, 0, :], t, tzero, eng="dve")]
                        else:
                            b.readers = [place(hp, ps, LEVELS.index(m), t, tzero)]
                    yield
                for hp in range(2):
                    p0 = 64 * hp
                    b, free = P.bank()
                    P.wait("pe", [free])
                    for pr in range(2):
                        for bl in range(2):
                            tq = P.mm(b.t[:, (2 * pr + bl) * 128:(2 * pr + bl) * 128 + 128],
                                      [(qk[p0:p0 + 64, 2 + pr, bl * 128:bl * 128 + 128], qk[p0:p0 + 64, pr, bl * 128:bl * 128 + 128])])
                    ps = b.t[:, :].rearrange("p (h b t) -> p h b t", h=2, b=2)
                    b.readers = [place(hp, ps, len(LEVELS), tq)]
                tA = P.last("dve")
                yield
                for i in range(2):
                    b, free = P.bank()
                    P.wait("pe", [free, tA])
                    for hh in range(4):
                        pairs = [(Am[:, hh, i, :], gv[:, i, hh * 128:hh * 128 + 128])]
                        if i == 1:
                            pairs.insert(0, (Am[:, hh, 2, :], gv[:, 0, hh * 128:hh * 128 + 128]))
                        t = P.mm(b.t[:, hh * 128:hh * 128 + 128], pairs)
                    b.readers = [P.copy(go[:, i, :], b.t[:, :], t, eng="dve")]
                    P.tt(xs[:, 0, 0:512], go[:, i, :], go[:, i, :], ALU.mult)
                    P.red(ss[:, 4 * i:4 * i + 4], xs[:, 0, 0:512].rearrange("p (h e) -> p h e", h=4), ALU.add)
                t = P.ts(ss[:, :], ss[:, :], 1.0 / 128, EPS, ALU.mult, ALU.add)
                t = P.tt(rs[:, :], ss[:, :], C("nhalf")[:, 0:8], ALU.pow, t, eng="pool")
                for i in range(2):
                    gov = go[:, i, :].rearrange("p (h e) -> p h e", h=4)
                    P.tt(gov, gov, bc(rs[:, 4 * i:4 * i + 4], 2, 128), ALU.mult, t)
                    P.tt(go[:, i, :], go[:, i, :], gr[:, i, :], ALU.mult)

            units = []
            te = [P.last("act"), P.last("dve"), tz]
            for kind in range(3):
                for i in range(2):
                    for hh in range(8):
                        g, p0 = hh // 4, 64 * (hh % 2)
                        ql = qT[p0:p0 + 64, hh // 2, i * 128:(i + 1) * 128]
                        u = {"after": te, "scale": 0.125, "put": nsa_put(kind, hh, i)}
                        if kind == 0:
                            u.update(nk=15, qk=[(0, 15, ql, kcT[p0:p0 + 64, g, 0:15])],
                                     peak=peak_masked(C("cmpadd")[:, 15 * i:15 * i + 15]),
                                     ok=C("cmpok")[:, 15 * i:15 * i + 15], v=[vc[0:15, g, :]])
                        else:
                            n = 128 * (i + 1)
                            c = 256 + (kind - 1) * 128 + g * 64
                            u.update(nk=n, qk=[(0, n, qT[:, hh // 2, i * 128:(i + 1) * 128], kT[:, hh % 2, 2 * (kind - 1) + g, 0:n])],
                                     peak=peak_masked(C("causal")[:, 256 - n:]), v=[kv[:, j, c:c + 64] for j in range(i + 1)])
                        units.append(u)
            def others():
                works = [modulations(), decayed()]
                while works:
                    for g in list(works):
                        if next(g, works) is works:
                            works.remove(g)
                        else:
                            yield

            rest = others()
            attend(units, rest)
            for _ in rest:
                pass
            tg = P.last("dve")



            ynT, ogT = qT, kT[:, 0]
            for i in range(2):
                to_T(lambda k: yn[:, i, :].rearrange("p (d k) -> p k d", k=4)[:, k, :], 4,
                     lambda k0, n, ps, t: P.copy(ynT[:, :, i * 128:(i + 1) * 128], ps, t), tg)
                to_T(lambda k: go[:, i, :].rearrange("p (d k) -> p k d", k=4)[:, k, :], 4,
                     lambda k0, n, ps, t: P.tt(ogT[:, :, i * 128:(i + 1) * 128], ps, bc(S("glang"), 2, 128), ALU.mult, t))
            te = [P.last("act"), P.last("dve")]
            mx = grow
            sm = xs[:, :, :].rearrange("p i (m n) -> p i m n", m=2)
            for c in range(2):
                for m in range(2):
                    lin(uT, W(d["w_m"][2 * m + c]), 512, range(2),
                        lambda i, ps, t: P.act(sm[:, i, m, :], ps, ACT.Sigmoid, t, P.last("dve")))
                wa, wb = (W(d[n].rearrange("(p k) n -> p k n", k=4)[:, :, c * 512:c * 512 + 512])
                          for n in ("w_proj_nsa", "w_proj_gla"))
                for i in range(2):
                    o = mx[:, i, c * 512:c * 512 + 512]
                    b, free = P.bank()
                    t = P.mm(b.t[:, :], [(ynT[:, k, i * 128:(i + 1) * 128], wa.v[:, k, :]) for k in range(4)],
                             wa.tok, free, te)
                    b.readers = [P.tt(o, b.t[:, :], sm[:, i, 0, :], ALU.mult, t, P.last("act"))]
                    b, free = P.bank()
                    t = P.mm(b.t[:, :], [(ogT[:, k, i * 128:(i + 1) * 128], wb.v[:, k, :]) for k in range(4)],
                             wb.tok, free)
                    b.readers = [P.tt(bS[:, 0, :], b.t[:, :], sm[:, i, 1, :], ALU.mult, t)]
                    tm_ = P.tt(o, o, bS[:, 0, :], ALU.add)
                wa.done(t)
                wb.done(t)
            mxT = uT
            for i in range(2):
                to_T(lambda k: mx[:, i, :].rearrange("p (d k) -> p k d", k=8)[:, k, :], 8,
                     lambda k0, n, ps, t: P.copy(mxT[:, k0:k0 + n, i * 128:(i + 1) * 128], ps, t), tm_)
            te = [P.last("act"), P.last("dve")]
            wo = d["w_out"].rearrange("(p k) n -> p k n", k=8)

            def put(i, c, ps, t):
                o = h[:, i, c * 512:c * 512 + 512]
                return P.tt(o, o, ps, ALU.add, t)
            lin2(mxT, [W(wo[:, 0:4, :]), W(wo[:, 4:8, :])], range(2), put, te)
            P.barrier()

        T2 = [P.last(e) for e in ("pe", "act", "dve", "pool")]
        with ExitStack() as sc:
            vT = P.sb(sc, "vT", [128, 8, 256])
            tv = norm_T([h[:, 0, :], h[:, 1, :]], vT, lambda i: S("gffn"))
            lg = P.sb(sc, "lg", [128, 2, 36])
            wr = S("wr").rearrange("p (k n) -> p k n", k=8)
            for i in range(2):
                b, free = P.bank()
                t = P.mm(b.t[:, 0:36], [(vT[:, k, i * 128:(i + 1) * 128], wr[:, k, :]) for k in range(8)], free, tv)
                b.readers = [P.tt(lg[:, i, :], b.t[:, 0:36], S("brout"), ALU.add, t)]
            R = P.sb(sc, "R", [128, 2, 128])
            comb = P.sb(sc, "comb", [128, 2, 32])
            g4, e32 = lg[:, :, 0:4], lg[:, :, 4:36].rearrange("p i (g e) -> p i g e", g=4)
            m1, eg, sg, oh4 = R[:, :, 0:1], R[:, :, 1:5], R[:, :, 5:6], R[:, :, 6:10]
            w4, in8, oh8, oh8b, t8 = R[:, :, 10:14], R[:, :, 16:24], R[:, :, 24:32], R[:, :, 32:40], R[:, :, 40:48]
            ma, mb, e2, dn, c1, c2 = (R[:, :, 48 + n:49 + n] for n in range(6))
            tb_ = R[:, :, 64:96]

            def first(oh, x, mx_, n):
                P.tt(oh, x, mx_.to_broadcast([128, 2, n]), ALU.is_equal)
                P.tt(oh, oh, bc(C("desc")[:, 8 - n:8], 1, 2), ALU.mult)
                P.red(dn[:, :, 0], oh, ALU.max)
                return P.tt(oh, oh, dn.to_broadcast([128, 2, n]), ALU.is_equal)

            P.red(m1[:, :, 0], g4, ALU.max)
            t = P.tt(eg, g4, m1.to_broadcast([128, 2, 4]), ALU.subtract)
            t = P.act(eg, eg, ACT.Exp, t)
            P.red(sg[:, :, 0], eg, ALU.add, t)
            first(oh4, g4, m1, 4)
            pe_ = tb_.rearrange("p i (g e) -> p i g e", g=4)
            for i in range(2):
                P.tt(pe_[:, i], e32[:, i], bc(oh4[:, i], 2, 8), ALU.mult)
                P.red(in8[:, i], pe_[:, i].rearrange("p g e -> p e g"), ALU.add)
            P.red(ma[:, :, 0], in8, ALU.max)
            first(oh8, in8, ma, 8)
            P.stt(t8, oh8, NEG, in8, ALU.mult, ALU.add)
            P.red(mb[:, :, 0], t8, ALU.max)
            first(oh8b, t8, mb, 8)
            t = P.tt(e2, mb, ma, ALU.subtract)
            t = P.act(e2, e2, ACT.Exp, t)
            P.ts(dn, e2, 1.0, None, ALU.add, None, t)
            P.tt(dn, dn, sg, ALU.mult)
            P.recip(c1, dn)
            P.tt(c2, c1, e2, ALU.mult)
            A = P.sb(sc, "A", [128, 2, 32])
            P.tt(t8, oh8, oh8b, ALU.add)
            av = A[:, :, :].rearrange("p i (g e) -> p i g e", g=4)
            for i in range(2):
                tA = P.tt(av[:, i], bc(t8[:, i], 1, 4), bc(oh4[:, i], 2, 8), ALU.mult)
            P.tt(oh8, oh8, c1.to_broadcast([128, 2, 8]), ALU.mult)
            P.tt(oh8b, oh8b, c2.to_broadcast([128, 2, 8]), ALU.mult)
            P.tt(oh8, oh8, oh8b, ALU.add)
            cv = comb[:, :, :].rearrange("p i (g e) -> p i g e", g=4)
            for i in range(2):
                t = P.tt(cv[:, i], bc(oh8[:, i], 1, 4), bc(oh4[:, i], 2, 8), ALU.mult)

            key = P.sb(sc, "key", [128, 2, 32])
            cnt = P.sb(sc, "cnt", [128, 1])
            flag = P.sb(sc, "flag", [1, 1], I32)
            b, free = P.bank()
            P.wait("pe", [free, tA])
            P.mm(b.t[:, 0:32], [(C("before"), A[:, 0, :])])
            P.mm(b.t[:, 32:64], [(C("ones"), A[:, 0, :]), (C("before"), A[:, 1, :])])
            t = P.mm(b.t[:, 64:96], [(C("ones"), A[:, 0, :]), (C("ones"), A[:, 1, :])])
            P.stt(key[:, :, :], b.t[:, 0:64].rearrange("p (i e) -> p i e", i=2), 1.0, A[:, :, :], ALU.add, ALU.mult, t)
            b.readers = [P.red(cnt[:, :], b.t[:, 64:96], ALU.max)]
            tflag = P.op("dve", lambda e: e.tensor_copy(flag[:, :], cnt[0:1, :]))

            big = P.sb(sc, "big", [128, 2, 32, 64])
            xring = P.sb(sc, "xring", [128, XSLOT, SLOT])
            for n in range(XSLOT):
                views[NSLOT + n] = xring[:, n, :]
                slot_reader[NSLOT + n] = T2
            order = []
            for p in range(17):
                order += [(n, e) for n in "gu" for e in (2 * p, 2 * p + 1)] if p < 16 else []
                order += [("d", 2 * p - 2), ("d", 2 * p - 1)] if p > 0 else []
            ahead = NSLOT

            def source(kind, e):
                if kind == "d":
                    return d["w_down"][e].rearrange("(j p) n -> p j n", p=128)
                return d["w_gate" if kind == "g" else "w_up"][e].rearrange("(p k) f -> p k f", k=8)

            got = {}
            slots[:] = slots[at[0] % NSLOT:] + slots[:at[0] % NSLOT] + list(range(NSLOT, NSLOT + XSLOT))
            at[0] = 0
            for key_ in order[:ahead]:
                got[key_] = W(source(*key_))

            def stream():
                have, left = dict(got), order[ahead:]

                def tile(kind, e):
                    while (kind, e) not in have:
                        key_ = left.pop(0)
                        have[key_] = W(source(*key_))
                    return have.pop((kind, e))
                return tile

            Y = P.banks[0:4]

            def finish(ty):
                for i in range(2):
                    for c in range(2):
                        o = h[:, i, c * 512:c * 512 + 512]
                        t = P.tt(o, o, Y[2 * i + c].t[:, :], ALU.add, ty)
                P.barrier()

            def dense():
                tile = stream()
                combT = big[0:32, 0, 0:4, :].rearrange("p a b -> p (a b)")
                cb = big[:, 0, 4:12, :].rearrange("p (a b) c -> p a (b c)", a=2)
                sl = big[:, 0, 12:20, :].rearrange("p (a b) c -> p a (b c)", a=2)
                hT = big[:, 1, :, :].rearrange("p (a f b) c -> p a f (b c)", a=2, f=4)
                b, free = P.bank()
                for i in range(2):
                    t = P.tr(b.t[0:32, i * 128:(i + 1) * 128], comb[:, i, :], ident)
                tc = P.copy(combT, b.t[0:32, 0:256], t)
                b.readers = [tc]
                hfree = [None, None]
                hready = [None, None]

                def up(e):
                    wg, wu = tile("g", e), tile("u", e)
                    b, free = P.bank()
                    t = P.mm(b.t[:, 0:256], [(ident[0:32, e:e + 1].to_broadcast([32, 128]), combT)], free, tc)
                    tcb = P.copy(cb[:, e % 2, :], b.t[:, 0:256], t, P.last("dve"), eng="act")
                    b.readers = [tcb]
                    for f in range(4):
                        b, free = P.bank()
                        P.mm(b.t[:, 0:256], [(wg.v[:, k, f * 128:(f + 1) * 128], vT[:, k, :]) for k in range(8)], free, wg.tok)
                        t2 = P.mm(b.t[:, 256:512], [(wu.v[:, k, f * 128:(f + 1) * 128], vT[:, k, :]) for k in range(8)], wu.tok)
                        t = P.act(sl[:, f % 2, :], b.t[:, 0:256], ACT.Silu, t2, P.last("dve"))
                        o = hT[:, e % 2, f, :]
                        t3 = P.tt(o, b.t[:, 256:512], cb[:, e % 2, :], ALU.mult, tcb, t, hfree[e % 2])
                        b.readers = [t, t3]
                        hready[e % 2] = P.tt(o, o, sl[:, f % 2, :], ALU.mult, t)
                    wg.done(t2)
                    wu.done(t2)

                def down(e):
                    wd = tile("d", e)
                    P.wait("pe", [wd.tok, hready[e % 2]])
                    for i in range(2):
                        for c in range(2):
                            t = P.mm(Y[2 * i + c].t[:, :],
                                     [(hT[:, e % 2, f, i * 128:(i + 1) * 128], wd.v[:, f, c * 512:c * 512 + 512]) for f in range(4)],
                                     start=e == 0, stop=e == 31)
                    hfree[e % 2] = t
                    wd.done(t)
                    return t

                for e in range(33):
                    if e < 32:
                        up(e)
                    if e > 0:
                        ty = down(e - 1)
                finish(ty)

            def sparse():
                tile = stream()
                for e in range(0, 32, 8):
                    for i in range(2):
                        tG = P.tt(big[:, i, e:e + 8, :], bc(C("iota"), 1, 8), bc(key[:, i, e:e + 8], 2, 64), ALU.is_equal)
                L = {}

                def gather(p):
                    for k0 in (0, 4):
                        b, free = P.bank()
                        P.wait("pe", [free, tG])
                        for k in range(4):
                            t = P.mm(b.t[:, k * 128:(k + 1) * 128],
                                     [(xs[:, i, (k0 + k) * 128:(k0 + k + 1) * 128],
                                       big[:, i, 2 * p:2 * p + 2, :].rearrange("p e j -> p (e j)")) for i in range(2)])
                        b.readers = [P.tt(ve[:, p % 2, k0:k0 + 4, :], b.t[:, :].rearrange("p (k j) -> p k j", k=4),
                                          bc(S("gffn")[:, k0:k0 + 4], 2, 128), ALU.mult, t, L.get(("up", p - 2)))]
                    L["v", p] = b.readers

                def up(p):
                    P.wait("pe", [L["v", p]])
                    bs_ = []
                    for n in "gu":
                        b, free = P.bank()
                        w = [tile(n, 2 * p + a) for a in range(2)]
                        P.wait("pe", [free, w[0].tok, w[1].tok])
                        for k in range(8):
                            for a in range(2):
                                o = slice(64 * a, 64 * a + 64)
                                t = P.mm(b.t[o, :], [(ve[:, p % 2, k, o], w[a].v[:, k, :])], start=k == 0, stop=k == 7)
                        w[0].done(t)
                        w[1].done(t)
                        bs_.append((b, t))
                    (g, tg_), (u, tu_) = bs_
                    L["up", p] = tu_
                    t = P.act(sl, g.t[:, :], ACT.Silu, tg_, L.get(("h", p - 1)))
                    g.readers = [t]
                    L["h", p] = P.tt(hp[p % 2], u.t[:, :], sl, ALU.mult, tu_, t, L.get(("turned", p - 2)))
                    u.readers = [L["h", p]]

                def turn(p):
                    b, free = P.bank()
                    P.wait("pe", [free, L["h", p]])
                    for f in range(4):
                        t = P.tr(b.t[:, f * 128:(f + 1) * 128], hp[p % 2][:, f * 128:(f + 1) * 128], ident, inc=f == 3)
                    L["turned", p] = t
                    L["hT", p] = P.copy(hT[:, p % 2, :], b.t[:, :], t, L.get(("down", p - 2)), eng="act")
                    b.readers = [L["hT", p]]

                def down(p):
                    w = [tile("d", 2 * p + a) for a in range(2)]
                    P.wait("pe", [L["hT", p], w[0].tok, w[1].tok])
                    for c in range(2):
                        b, free = P.bank()
                        P.wait("pe", [free])
                        for f in range(4):
                            for a in range(2):
                                o = slice(64 * a, 64 * a + 64)
                                t = P.mm(b.t[o, :], [(hT[:, p % 2, f * 128 + 64 * a:f * 128 + 64 * a + 64],
                                                      w[a].v[:, f, c * 512:c * 512 + 512])], start=f == 0, stop=f == 3)
                        b.readers = [P.copy(yk[:, p % 2, c * 512:c * 512 + 512], b.t[:, :], t, L.get(("put", p - 2)),
                                            eng="act")]
                    w[0].done(t)
                    w[1].done(t)
                    L["down", p] = t
                    L["y", p] = b.readers

                def weights(p):
                    gw = gwt[:, p % 2]
                    t = P.tt(gw, big[:, :, 2 * p:2 * p + 2, :], bc(comb[:, :, 2 * p:2 * p + 2], 3, 64), ALU.mult, tG,
                             L.get(("wturned", p - 2)), eng="pool")
                    b, free = P.bank()
                    P.wait("pe", [free, t])
                    for i in range(2):
                        t = P.tr(b.t[:, i * 128:(i + 1) * 128], gw[:, i].rearrange("p e j -> p (e j)"), ident)
                    L["wturned", p] = t
                    t = P.copy(sw[:, p % 2, :], b.t[:, 0:256], t, L.get(("put", p - 2)), eng="dve")
                    b.readers = [t]
                    L["sw", p] = t

                def put_back(p):
                    P.wait("pe", [L["sw", p], L["y", p]])
                    for i in range(2):
                        for c in range(2):
                            t = P.mm(Y[2 * i + c].t[:, :],
                                     [(sw[:, p % 2, i * 128:(i + 1) * 128], yk[:, p % 2, c * 512:c * 512 + 512])],
                                     start=p == 0, stop=p == 15)
                    L["put", p] = t
                    return t

                gather(0)
                for p in range(18):
                    if p < 15:
                        gather(p + 1)
                    if p < 16:
                        up(p)
                    if p >= 2:
                        ty = put_back(p - 2)
                    if p < 16:
                        weights(p)
                    if 1 <= p <= 16:
                        down(p - 1)
                    if p < 16:
                        turn(p)
                finish(ty)

            ve = P.sb(sc, "ve", [128, 2, 8, 128])
            gwt = bP[:, 0, :].rearrange("p (a i e j) -> p a i e j", a=2, i=2, e=2)
            sw = bP[:, 1, :].rearrange("p (a t) -> p a t", a=2)
            sl, hp, hT = bS[:, 0, :], (bS[:, 1, :], bP[:, 2, :]), bT[:, 0:2, :]
            yk = grow
            P.barrier()
            P.ring = P.banks[4:8]
            start = (list(slots), at[0], list(slot_n), list(slot_reader))
            ends_ = []

            def side(f):
                def g():
                    slots[:], at[0], slot_n[:], slot_reader[:] = list(start[0]), start[1], list(start[2]), list(start[3])
                    P.at = 0
                    for b in P.ring:
                        b.readers = []
                    f()
                    ends_.append((at[0], list(slot_n)))
                return g

            P.branch(flag[:, :], CAP, side(dense), side(sparse), tflag)
            assert ends_[0] == ends_[1]
            slot_reader[:] = [[P.last(e) for e in ("pe", "act", "dve", "pool")]] * (NSLOT + XSLOT)
            cut = at[0] % len(slots)
            slots[:] = [n for n in slots[cut:] + slots[:cut] if n < NSLOT]
            at[0] = 0
            P.ring = P.banks
            P.at = 0
            for b in P.banks:
                b.readers = []
            P.barrier()

        def row_bcast(dst, col, *after):
            dv = dst.rearrange("p (n k) -> p k n", k=8)
            for k0 in (0, 4):
                b, free = P.bank()
                P.wait("pe", [free, after])
                for k in range(4):
                    t = P.mm(b.t[:, k * 128:(k + 1) * 128], [(col(k0 + k).to_broadcast([128, 128]), ident)])
                b.readers = [P.copy(dv[:, k0:k0 + 4, :], b.t[:, :].rearrange("p (k n) -> p k n", k=4), t, eng="dve")]

        def final_norm(g, dst):
            row_bcast(grow[:, 0, :], lambda k: S(g)[:, k:k + 1])
            t = rstd([h[:, 0, :], h[:, 1, :]], 1024, 2)
            for i in range(2):
                t = P.stt(dst(i), h[:, i, :], rs[:, i:i + 1], grow[:, 0, :], ALU.mult, ALU.mult, t)
            return t

        final_norm("gfin", lambda i: h[:, i, :])

        def modulated(UT, l):
            return norm_T([h[:, i, :] for i in range(4)], UT, lambda i: Amod[:, l, i // 2, :],
                          lambda i: mod[:, l, 0:8, i // 2])

        def residual(i, c, ps, t):
            o = h[:, i, c * 512:c * 512 + 512]
            t = P.tt(bS[:, 0, :], ps, grow[:, i // 2, c * 512:c * 512 + 512], ALU.mult, t)
            P.tt(o, o, bS[:, 0, :], ALU.add)
            return t

        with ExitStack() as sc:
            UT = P.sb(sc, "UT", [128, 8, 512])
            tu = modulated(UT, 0)
            for wh in range(2):
                row_bcast(grow[:, wh, :], lambda k: mod[:, 0, 16 + k, wh:wh + 1], P.last("dve"))
            ZO = P.sb(sc, "ZO", [128, 4, 1024])
            va = P.sb(sc, "va", [128, 4, 128])
            with ExitStack() as sa:
                cq = P.sb(sa, "cq", [128, 4, 416])
                vb = P.sb(sa, "vb", [128, 4, 8, 64])
                vbf = vb[:, :, :, :].rearrange("p i h r -> p (i h r)")
                ck = vbf[:, 0:1024].rearrange("p (i n) -> p i n", i=4)
                kaT = xs[:, :, :].rearrange("p hp (g t) -> p hp g t", g=2)
                for hp in range(2):
                    tz = P.op("pool", lambda e, hp=hp: e.memset(kaT[64 - 64 * hp:128 - 64 * hp, hp, :, :], 0.0),
                              P.last("pe"))
                qq = P.sb(sa, "qq", [128, 8, 512])
                qa, qaT, kbT = qq[:, 0:4, :], qq[:, 4:8, :], qq
                ka = P.sb(sa, "ka", [128, 4, 128])
                kd = P.sb(sa, "kd", [128, 2, 2, 64])
                T4 = range(4)
                lin(UT, W(d["w_qa"]), 512, T4, lambda i, ps, t: P.copy(qa[:, i, :], ps, t), tu)

                def put(i, ps, t):
                    P.copy(ka[:, i, :], ps[:, 0:128], t, eng="dve")
                    P.copy(va[:, i, :], ps[:, 128:256], t, eng="dve")
                    return P.copy(ck[:, i, :], ps[:, 256:512], t, eng="dve")
                lin(UT, W(d["w_kva"]), 512, T4, put)
                lin(UT, W(d["w_za"]), 512, T4, lambda i, ps, t: P.act(ZO[:, i, 0:512], ps, ACT.Silu, t))
                lin(UT, W(d["w_zb"]), 512, T4, lambda i, ps, t: P.act(ZO[:, i, 512:1024], ps, ACT.Silu, t))
                lin(UT, W(d["w_cq"]), 416, T4, lambda i, ps, t: P.copy(cq[:, i, :], ps, t))
                P.wait("dve", [P.last("act")])

                def rope_pairs(x1, x2, i, ca, sa_, n, r, dst1=None, dst2=None):
                    co = bc(C(ca).rearrange("p (i r) -> p i r", i=4)[:, i, :], 1, n)
                    si = bc(C(sa_).rearrange("p (i r) -> p i r", i=4)[:, i, :], 1, n)
                    tm = [rt[:, m_, 0:n * r].rearrange("p (h r) -> p h r", h=n) for m_ in range(4)]
                    P.tt(tm[0], x1, co, ALU.mult)
                    P.tt(tm[1], x2, si, ALU.mult)
                    P.tt(tm[2], x1, si, ALU.mult)
                    P.tt(tm[3], x2, co, ALU.mult)
                    P.tt(x1 if dst1 is None else dst1, tm[0], tm[1], ALU.subtract)
                    return P.tt(x2 if dst2 is None else dst2, tm[2], tm[3], ALU.add)

                tkd = None
                for i in range(4):
                    v = qa[:, i, :].rearrange("p (h r a) -> p h r a", h=8, a=2)
                    rope_pairs(v[:, :, :, 0], v[:, :, :, 1], i, "cosa", "sina", 8, 32)
                    v = ka[:, i, :].rearrange("p (h r a) -> p h r a", h=2, a=2)
                    rope_pairs(v[:, :, :, 0], v[:, :, :, 1], i, "cosa", "sina", 2, 32)
                    for a in range(2):
                        t = P.op("dve", lambda e, a=a, i=i: e.tensor_copy(
                            kd[:, :, a, :], ka[:, i, :].rearrange("p (g r) -> p g r", g=2)), tkd)
                    to_T(lambda k: qa[:, i, k * 128:(k + 1) * 128], 4,
                         lambda k0, n, ps, t: P.copy(qaT[:, :, i * 128:(i + 1) * 128], ps, t), t)
                    tkd = to_T(lambda k: kd[:, k, :, :].rearrange("p a r -> p (a r)"), 2,
                               lambda k0, n, ps, t: own_half(kaT, slice(0, 2), i, ps, t), t)
                te = [P.last("act"), P.last("dve"), tz]

                def gated(i, c0):
                    def f(ps, r, t, tr):
                        o = ZO[:, i, c0:c0 + 64]
                        return P.stt(o, ps, r, o, ALU.mult, ALU.mult, t, tr)
                    return f

                units = []
                for i in range(4):
                    for hh in range(8):
                        g = hh // 4
                        k0, nk = (0, 512) if i < 2 else (256, 256)
                        units.append({
                            "after": te, "scale": 0.125, "put": gated(i, hh * 64), "nk": nk,
                            "qk": [(0, nk, qaT[:, hh // 2, i * 128:(i + 1) * 128], kaT[:, hh % 2, g, k0:k0 + nk])], "sink": S("sink")[:, hh:hh + 1],
                            "peak": peak_masked(C("amask")[:, i * 512:(i + 1) * 512]) if i < 2 else peak,
                            "v": [va[:, j, g * 64:g * 64 + 64] for j in range(k0 // 128, 4)]})
                attend(units)

                cqT = xs[:, :, :].rearrange("p a b -> p (a b)")[:, 0:1536].rearrange("p (k t) -> p k t", k=3)
                ckT = P.sb(sa, "ckT", [128, 2, 512])
                rstd([cq[:, i, 0:384] for i in range(4)], 384, 4, P.last("pe"))
                t = rstd([ck[:, i, :] for i in range(4)], 256, 4, P.last("pe"), c0=4)
                for i in range(4):
                    t = P.ts(cq[:, i, 0:384], cq[:, i, 0:384], rs[:, i:i + 1], None, ALU.mult, None, t)
                    to_T(lambda k: cq[:, i, 0:384].rearrange("p (d k) -> p k d", k=3)[:, k, :], 3,
                         lambda k0, n, ps, t: P.tt(cqT[:, :, i * 128:(i + 1) * 128], ps, bc(S("qng"), 2, 128), ALU.mult, t), t)
                for i in range(4):
                    t = P.ts(ck[:, i, :], ck[:, i, :], rs[:, 4 + i:5 + i], None, ALU.mult, None, t)
                    to_T(lambda k: ck[:, i, :].rearrange("p (d k) -> p k d", k=2)[:, k, :], 2,
                         lambda k0, n, ps, t: P.tt(ckT[:, :, i * 128:(i + 1) * 128], ps, bc(S("kvng"), 2, 128), ALU.mult, t), t)
                krp = P.sb(sa, "krp", [128, 4, 32])
                P.op("dve", lambda e: e.tensor_copy(krp[:, :, :], cq[:, :, 384:416]))
                rows = cq[:, :, :].rearrange("p i n -> p (i n)")[:, 0:1536].rearrange("p (i h r) -> p i h r", i=4, h=4)
                qbT = UT
                tz = [P.op("pool", lambda e, x=x: e.memset(x[96:128, :, :], 0.0), P.last("pe")) for x in (UT, qq)]

                def head_T(dst, c, *after):
                    for hh in range(4):
                        b, free = P.bank()
                        P.wait("pe", [free, after])
                        for i in range(4):
                            t = P.tr(b.t[0:96, i * 128:(i + 1) * 128], rows[:, i, hh, :], ident, inc=i == 3)
                        b.readers = [P.copy(dst[0:96, 4 * c + hh, :], b.t[0:96, :], t)]
                    return t

                P.wait("pe", [P.last("dve")])
                w = W(d["b_w_uq"].rearrange("(p k) n -> p k n", k=3))
                trow = None
                for c in range(2):
                    for i in range(4):
                        b, free = P.bank()
                        t = P.mm(b.t[:, 0:384], [(cqT[:, k, i * 128:(i + 1) * 128], w.v[:, k, c * 384:c * 384 + 384]) for k in range(3)],
                                 w.tok, free)
                        b.readers = [P.copy(rows[:, i, :, :], b.t[:, 0:384].rearrange("p (h r) -> p h r", h=4), t, trow, eng="dve")]
                        v = rows[:, i, :, 64:96].rearrange("p h (r a) -> p h r a", a=2)
                        tr_ = rope_pairs(v[:, :, :, 0], v[:, :, :, 1], i, "cosb", "sinb", 4, 16)
                    trow = head_T(qbT, c, tr_)
                w.done(t)
                w = W(d["b_w_ukv"].rearrange("(p k) n -> p k n", k=2))
                for i in range(4):
                    v = krp[:, i:i + 1, :].rearrange("p h (r a) -> p h r a", a=2)
                    rope_pairs(v[:, :, :, 0], v[:, :, :, 1], i, "cosb", "sinb", 1, 16)
                for c in range(2):
                    for i in range(4):
                        b, free = P.bank()
                        t = P.mm(b.t[:, :], [(ckT[:, k, i * 128:(i + 1) * 128], w.v[:, k, c * 512:c * 512 + 512]) for k in range(2)],
                                 w.tok, free)
                        ps = b.t[:, :].rearrange("p (h a r) -> p h a r", h=4, a=2)
                        P.copy(rows[:, i, :, 0:64], ps[:, :, 0, :], t, trow, eng="dve")
                        b.readers = [P.copy(vb[:, i, 4 * c:4 * c + 4, :], ps[:, :, 1, :], t, eng="dve")]
                        tr_ = P.op("dve", lambda e, i=i: e.tensor_copy(rows[:, i, :, 64:96], bc(krp[:, i, :], 1, 4)))
                    trow = head_T(kbT, c, tr_)
                w.done(t)
                te = [P.last("act"), P.last("dve"), tz]
                units = []
                for i in range(4):
                    for hh in range(8):
                        k0, nk = (0, 512) if i < 2 else (256, 256)
                        units.append({
                            "after": te, "scale": 96.0 ** -0.5, "put": gated(i, 512 + hh * 64), "nk": nk,
                            "qk": [(0, nk, qbT[:, hh, i * 128:(i + 1) * 128], kbT[:, hh, k0:k0 + nk])],
                            "peak": peak, "v": [vb[:, j, hh, :] for j in range(k0 // 128, 4)]})
                attend(units)
                P.barrier()

            def rows_T(dst, n, *after):
                for i in range(n):
                    to_T(lambda k: ZO[:, i, :].rearrange("p (d k) -> p k d", k=8)[:, k, :], 8,
                         lambda k0, m, ps, t: P.copy(dst[:, k0:k0 + m, i * 128:(i + 1) * 128], ps, t), *after)
                return [P.last("act"), P.last("dve")]
            te = rows_T(UT, 4, P.last("dve"))
            wo = d["ab_out_w"].rearrange("(p k) n -> p k n", k=8)
            lin2(UT, [W(wo[:, 0:4, :]), W(wo[:, 4:8, :])], range(4), residual, te)
            P.barrier()

        with ExitStack() as sc:
            UT = P.sb(sc, "UT1", [128, 8, 512])
            tu = modulated(UT, 1)
            row_bcast(grow[:, 0, :], lambda k: mod[:, 1, 16 + k, 0:1], P.last("dve"))
            qcT = P.sb(sc, "qcT", [128, 2, 8, 256])
            for hp in range(2):
                tz = P.op("pool", lambda e, hp=hp: e.memset(qcT[64 - 64 * hp:128 - 64 * hp, hp, :, :], 0.0))
            kcT2 = P.sb(sc, "kcT2", [128, 8, 512])
            vcr = P.sb(sc, "vcr", [128, 4, 1024])
            ZO = P.sb(sc, "ZO1", [128, 2, 1024])
            M4 = [(j * 128, 128) for j in range(4)]

            def own(j, ps, t):
                for hp in range(2):
                    o = slice(64 * hp, 64 * hp + 64)
                    t = P.copy(qcT[o, hp, j, :], ps[o], t, eng="dve")
                return t
            for c in range(2):
                linT(UT, W(d["w_c"][c]), M4, 256, lambda j, ps, t: own(4 * c + j, ps, t), tu)
            for c in range(2):
                linT(UT, W(d["w_c"][2 + c]), M4, 512, lambda j, ps, t: P.copy(kcT2[:, 4 * c + j, :], ps, t))
            for c in range(2):
                lin(UT, W(d["w_c"][4 + c]), 512, range(4), lambda i, ps, t: P.copy(vcr[:, i, c * 512:c * 512 + 512], ps, t))
            for c in range(2):
                lin(UT, W(d["w_c"][6 + c]), 512, range(2), lambda i, ps, t: P.act(ZO[:, i, c * 512:c * 512 + 512], ps, ACT.Silu, t))
            te = [P.last("act"), P.last("dve"), tz]

            def gated(i, c0):
                def f(ps, r, t, tr):
                    o = ZO[:, i, c0:c0 + 64]
                    return P.stt(o, ps, r, o, ALU.mult, ALU.mult, t, tr)
                return f

            def peak_biased(bias, tb):
                def f(x, s, m, t):
                    P.stt(s[:, 0:256], x[:, 0:256], 0.125, bias, ALU.mult, ALU.add, t, tb)
                    t = P.ts(s[:, 256:512], x[:, 256:512], 0.125, None, ALU.mult, None)
                    P.red(m, s, ALU.max)
                    return s, [t]
                return f

            for c in range(2):
                w = W(d["bias"][c])
                v = w.v.rearrange("p h (r k) -> p (h r) k", k=64)
                tb = P.tt(v, v, bc(C("colmask"), 1, 64), ALU.add, w.tok, eng="pool")
                units = []
                for hh in range(8 * c, 8 * c + 8):
                    for i in range(2):
                        units.append({
                            "after": te, "scale": 1.0, "put": gated(i, hh * 64), "nk": 512,
                            "qk": [(0, 512, qcT[:, hh % 2, hh // 2, i * 128:(i + 1) * 128], kcT2[:, hh // 2, :])],
                            "peak": peak_biased(w.v[:, hh % 8, i * 256:(i + 1) * 256], tb),
                            "v": [vcr[:, j, hh * 64:hh * 64 + 64] for j in range(4)]})
                attend(units)
                w.done(P.last("dve"))
            for i in range(2):
                to_T(lambda k: ZO[:, i, :].rearrange("p (d k) -> p k d", k=8)[:, k, :], 8,
                     lambda k0, n, ps, t: P.copy(qcT[:, 0, k0:k0 + n, i * 128:(i + 1) * 128], ps, t), P.last("dve"))
            te = [P.last("act"), P.last("dve")]
            wo = d["c_out_w"].rearrange("(p k) n -> p k n", k=8)
            lin2(qcT[:, 0], [W(wo[:, 0:4, :]), W(wo[:, 4:8, :])], range(2), residual, te)
            t = final_norm("fin2", lambda i: xs[:, i, :])
            o = out.rearrange("o (t p) d -> p (o t) d", p=128)
            tf = P.dma("sp", o, xs[:, :, :], "out", s_out, 16, t)
            P.wait("sp", [tf])
            P.barrier()

        block = ctx.enter_context(nc.Block())

        @block.tensor
        def _(e):
            P.emit(e, P.q["pe"])

        @block.scalar
        def _(e):
            P.emit(e, P.q["act"])

        @block.vector
        def _(e):
            P.emit(e, P.q["dve"])

        @block.gpsimd
        def _(e):
            P.emit(e, P.q["pool"])

        @block.sync
        def _(e):
            P.emit(e, P.q["sp"])


def constants():
    f = np.float32
    p = np.arange(128)
    o = {"ident": np.eye(128)}
    o["inv"] = np.tile((f(1.0) / (f(10000.0) ** (np.arange(32, dtype=f) / f(32)))).astype(f), (128, 1))
    o["causal"] = np.concatenate([np.zeros((128, 128)), np.where(p[None, :] <= p[:, None], 0.0, NEG)], 1)
    t = p[:, None, None] + 128 * np.arange(2)[None, :, None]
    ok = (16 * np.arange(15) + 31)[None, None, :] <= t
    o["cmpadd"] = np.where(ok, 0.0, NEG)
    o["cmpok"] = ok * 1.0
    k = np.arange(512)[None, None, :]
    o["amask"] = np.where((np.abs(k - t) <= 128) | (k >= 256), 0.0, NEG)
    lev = []
    s, q = p[:, None], p[None, :]
    for m in LEVELS:
        lev.append((s // (2 * m) == q // (2 * m)) & (s // m % 2 == 0) & (q // m % 2 == 1))
    lev.append(s == q)
    o["lev"] = np.stack(lev, 1) * 1.0
    qc, kc = (p % 64)[:, None], np.arange(64)[None, :]
    cs = np.clip(qc - 8, 0, 48)
    o["colmask"] = np.where((kc >= cs) & (kc < cs + 16), 0.0, NEG)
    tok = p[:, None] + 128 * np.arange(2)[None, :]
    for name, d in (("a", 64), ("b", 32)):
        n = d // 4
        inv = (f(10000.0) ** (-np.arange(n, dtype=f) / f(n))).astype(f)
        row, col = (tok // 64).astype(f), (tok % 64).astype(f)
        ang = np.concatenate([row[..., None] * inv, col[..., None] * inv], -1).astype(f)
        one = np.zeros((128, 2, 2 * n), f)
        o["cos" + name] = np.concatenate([np.cos(ang), one + 1], 1)
        o["sin" + name] = np.concatenate([np.sin(ang), one], 1)
    o["desc"] = np.tile(np.arange(8, 0, -1), (128, 1))
    o["before"] = (s < q) * 1.0
    o["ones"] = np.ones((128, 128))
    o["iota"] = np.tile(np.arange(1, 65), (128, 1))
    o["pick"] = (p[:, None] % 32 == np.arange(2)[None, :]) * 1.0
    o["nhalf"] = np.full((128, 16), -0.5)
    return np.concatenate([np.asarray(o[n], f).reshape(128, w) for n, w in CONST], 1)


def tiles(w, k, *cols):
    w = w.reshape(128, k, w.shape[1])
    return np.ascontiguousarray(np.concatenate([w[:, :, c] for c in cols], 2))


def kernel(**inputs):
    import concourse.bacc as _bacc
    from concourse import mybir as _mybir
    from concourse.bass_utils import run_bass_kernel_spmd as _run

    a = {k: np.asarray(v) for k, v in inputs.items()}
    f = np.float32
    w_in = a["w_in"][0]
    c = np.cumsum([0, 512, 128, 128, 128, 128, 128, 128, 24, 256, 256, 512, 16, 512, 1024, 1024])
    col = [slice(c[i], c[i + 1]) for i in range(15)]
    ab = a["ab_in_w_2"][0]
    cin = a["c_in_w_2"][0]

    def kmaj(v, k):
        return v.reshape(128, k)

    def tmaj(v, k):
        return v.reshape(k, 128).T

    def rep(v):
        return np.broadcast_to(v.reshape(1, -1), (128, v.size))

    def pairs(pos):
        return pos.reshape(16, 128).T

    def half(s, n):
        return slice(s.start + n * 64, s.start + n * 64 + 64)

    wr = np.concatenate([a["w_grp"][0], a["w_exp"][0]], 1).reshape(128, 288)
    wa2 = np.zeros((128, 256), f)
    wa2[0:16] = a["gla_w_a2"][0]
    small = {
        "gmix": kmaj(a["g_mix"][0], 8), "gffn": kmaj(a["g_ffn"][0], 8), "gfin": kmaj(a["g_final"], 8),
        "ng0": kmaj(a["norm_g_2"][0], 8), "ng1": kmaj(a["norm_g_2"][1], 8), "fin2": kmaj(a["final_g_2"], 8),
        "qng": kmaj(a["b_q_norm_g_2"][0], 3), "kvng": kmaj(a["b_kv_norm_g_2"][0], 2),
        "glang": kmaj(a["gla_norm_g"][0], 4), "b1k": tmaj(a["cmp_b1_k"][0], 2), "b1v": tmaj(a["cmp_b1_v"][0], 2),
        "glaba": tmaj(a["gla_b_a"][0], 2),
        "cc": np.stack([kmaj(a["c_2"][0], 8), kmaj(a["c_ctx_2"], 8)], 2).reshape(128, 16),
        "adab": a["ada_b_2"].reshape(2, 3, 128, 8).transpose(2, 0, 1, 3).reshape(128, 48),
        "posk": pairs(a["cmp_pos_k"][0]), "posv": pairs(a["cmp_pos_v"][0]),
        "w2k": a["cmp_w2_k"][0].reshape(2, 128, 64).transpose(1, 0, 2).reshape(128, 128),
        "w2v": a["cmp_w2_v"][0].reshape(2, 128, 64).transpose(1, 0, 2).reshape(128, 128),
        "wr": wr, "wa2": wa2, "b2k": rep(a["cmp_b2_k"][0]), "b2v": rep(a["cmp_b2_v"][0]),
        "brout": np.concatenate([rep(a["b_grp"][0]), rep(a["b_exp"][0])], 1), "sink": rep(a["a_sink_2"][0]),
    }
    pos = a["positions"][0]
    ends = np.zeros(128, np.int64)
    ends[0:15] = 16 * np.arange(15) + 31
    t = np.arange(256)
    dr = t[None, :] // 64 - t[:, None] // 64 + 7
    dc = np.clip(t[None, :] % 64 - t[:, None] % 64 + 15, 0, 30)
    bias = a["c_rpb_2"][0][:, dr, dc].reshape(2, 8, 2, 128, 256).transpose(0, 3, 1, 2, 4).reshape(2, 128, 8, 512)

    def pos_tile(w):
        return np.ascontiguousarray(w.reshape(16, 128, 256).transpose(1, 0, 2))

    ada = a["ada_w_2"].reshape(2, 128, 8, 3, 128, 8).transpose(0, 3, 5, 1, 2, 4)
    ada = ada.reshape(2, 6, 4, 128, 8, 128).transpose(0, 1, 3, 4, 2, 5).reshape(2, 6, 128, 8, 512)
    send = {
        "const": constants(),
        "small": np.concatenate([np.asarray(small[n]).reshape(128, w) for n, w in SMALL], 1),
        "pos": np.stack([pos[0:128], pos[128:256], pos[ends]], 1),
        "x": a["x"], "ctx": a["ctx_2"],
        "w_gqk": tiles(w_in, 8, col[8], col[9]), "w_sm": tiles(w_in, 8, col[7], col[11]),
        "w_gv": tiles(w_in, 8, col[10]), "w_q": tiles(w_in, 8, col[0]),
        "w_kv": tiles(w_in, 8, col[3], col[5], col[4], col[6]),
        "w_kvc": tiles(w_in, 8, *[half(col[m], g) for m in (1, 2) for g in (0, 0, 1, 1)]),
        "w1k": pos_tile(a["cmp_w1_k"][0]), "w1v": pos_tile(a["cmp_w1_v"][0]),
        "w_gr": tiles(w_in, 8, col[12]),
        "w_m": np.stack([tiles(w_in, 8, slice(c[13] + 512 * j, c[13] + 512 * j + 512)) for j in range(4)]),
        "w_proj_nsa": a["w_proj_nsa"][0], "w_proj_gla": a["w_proj_gla"][0], "w_out": a["w_out"][0],
        "w_gate": a["w_gate"][0], "w_up": a["w_up"][0], "w_down": a["w_down"][0],
        "w_ada": np.ascontiguousarray(ada),
        "w_qa": tiles(ab, 8, slice(0, 512)),
        "w_kva": tiles(ab, 8, slice(512, 768), slice(1664, 1920)),
        "w_za": tiles(ab, 8, slice(768, 1280)), "w_zb": tiles(ab, 8, slice(1952, 2464)),
        "w_cq": tiles(ab, 8, slice(1280, 1664), slice(1920, 1952)),
        "b_w_uq": a["b_w_uq_2"][0], "b_w_ukv": a["b_w_ukv_2"][0], "ab_out_w": a["ab_out_w_2"][0],
        "w_c": np.stack([tiles(cin, 8, slice(512 * j, 512 * j + 512)) for j in range(8)]),
        "bias": np.ascontiguousarray(bias), "c_out_w": a["c_out_w_2"][0],
    }
    nc = _bacc.Bacc("TRN2", target_bir_lowering=False, num_devices=1)
    arrays, d = {}, {}
    for name, v in send.items():
        v = np.ascontiguousarray(v)
        arrays[f"in_{name}"] = v
        d[name] = nc.dram_tensor(f"in_{name}", v.shape, _mybir.dt.from_np(v.dtype), kind="ExternalInput").ap()
    out = nc.dram_tensor("out_0", (1, 256, 1024), _mybir.dt.float32, kind="ExternalOutput").ap()
    build(nc, d, out)
    r = _run(nc, [arrays], core_ids=[0])
    return r.results[0]["out_0"]
```

```python
from collections import namedtuple
from contextlib import ExitStack

import numpy as np

import concourse.bass as bass
from concourse import mybir
from concourse.alu_op_type import AluOpType as ALU

F32 = mybir.dt.float32
F32R = mybir.dt.float32r
I32 = mybir.dt.int32
U32 = mybir.dt.uint32
ACT = mybir.ActivationFunctionType
X = mybir.AxisListType.X
EPS = 1e-6
NEG = -1e30
NSLOT = 4
XSLOT = 10
CAP = 64
SLOT = 2048
LEVELS = (64, 32, 16, 8, 4, 2, 1)

SMALL = [("gmix", 8), ("gffn", 8), ("gfin", 8), ("ng0", 8), ("ng1", 8), ("fin2", 8), ("qng", 3),
         ("kvng", 2), ("glang", 4), ("b1k", 2), ("b1v", 2), ("glaba", 2), ("cc", 16), ("adab", 48),
         ("posk", 16), ("posv", 16), ("w2k", 128), ("w2v", 128), ("wr", 288), ("wa2", 256),
         ("b2k", 64), ("b2v", 64), ("brout", 36), ("sink", 8)]
CONST = [("ident", 128), ("inv", 32), ("nhalf", 16), ("desc", 8), ("iota", 64), ("pick", 2), ("minus", 1), ("sel", 120), ("bd", 8), ("fold", 30), ("causal", 256),
         ("cmpadd", 30), ("cmpok", 30), ("before", 128), ("ones", 128), ("amask", 1024),
         ("lev", 128 * (len(LEVELS) + 1)), ("colmask", 64), ("cosa", 128), ("sina", 128), ("cosb", 64), ("sinb", 64)]


Tile = namedtuple("Tile", "slot v tok")
Parts = namedtuple("Parts", "a b tok")


def offsets(fields):
    out, at = {}, 0
    for name, w in fields:
        out[name] = (at, w)
        at += w
    return out, at


class Bank:
    def __init__(self, t):
        self.t = t
        self.freed = []


class Ring:
    def __init__(self, banks):
        self.banks, self.at = banks, 0


class Prog:

    ENGINES = ("pe", "act", "dve", "pool", "sp")

    def __init__(self, nc, ctx):
        self.nc = nc
        self.ctx = ctx
        self.q = {e: [] for e in self.ENGINES}
        self.sem = {e: ctx.enter_context(nc.semaphore("s_" + e)) for e in self.ENGINES}
        self.n = {e: 0 for e in self.ENGINES}
        self.seen = {e: {} for e in self.ENGINES}
        self.flip = 0
        self.banks = [Bank(ctx.enter_context(nc.psum_tensor(f"ps{i}", [128, 512], F32))) for i in range(8)]
        self.ring = Ring(self.banks)

    def wait(self, eng, toks):
        for t in toks:
            if t is None:
                continue
            if isinstance(t, (list, tuple)) and not (t and isinstance(t[0], str)):
                self.wait(eng, t)
                continue
            key, sem, v = t
            if self.seen[eng].get(key, 0) < v:
                self.seen[eng][key] = v
                self.q[eng].append(lambda e, s=sem, v=v: e.wait_ge(s, v))

    def last(self, eng):
        return (eng, self.sem[eng], self.n[eng]) if self.n[eng] else None

    def op(self, eng, fn, *after, inc=True):
        if eng != "pe":
            self.wait(eng, [self.last(eng)])
        self.wait(eng, after)
        if not inc:
            self.q[eng].append(fn)
            return None
        self.n[eng] += 1
        self.q[eng].append(lambda e, s=self.sem[eng]: fn(e).then_inc(s, 1))
        return (eng, self.sem[eng], self.n[eng])

    def dma(self, eng, out, in_, name, sem, count, *after):
        self.wait(eng, after)
        self.q[eng].append(lambda e: e.dma_start(out, in_).then_inc(sem, 16))
        return (name, sem, count)

    def barrier(self):
        for e in ("pe", "act", "dve", "pool"):
            self.wait(e, [self.last(o) for o in ("pe", "act", "dve", "pool") if o != e])

    def branch(self, flag, least, many, few, *after):
        for e in self.ENGINES:
            self.wait(e, after)
        outer, n0 = self.q, dict(self.n)
        seen0 = {e: dict(v) for e, v in self.seen.items()}
        sides = []
        for f in (many, few):
            self.q = {e: [] for e in self.ENGINES}
            self.n = dict(n0)
            self.seen = {e: dict(v) for e, v in seen0.items()}
            f()
            sides.append((self.q, self.n))
        self.n = {e: max(n[e] for _, n in sides) for e in self.ENGINES}
        for q, n in sides:
            for e in self.ENGINES:
                if n[e] < self.n[e]:
                    q[e].append(lambda g, s=self.sem[e], k=self.n[e] - n[e]: g.drain().then_inc(s, k))
        self.q = outer
        self.seen = seen0
        for e in self.ENGINES:
            self.q[e].append((flag, least, sides[0][0][e], sides[1][0][e]))

    def emit(self, eng, items):
        for f in items:
            if not isinstance(f, tuple):
                f(eng)
                continue
            flag, least, many, few = f
            v = eng.value_load(flag)
            with eng.If(v > least):
                self.emit(eng, many)
            with eng.Else():
                self.emit(eng, few)

    def bank(self, ring=None):
        if ring is None:
            ring = self.ring
        b = ring.banks[ring.at % len(ring.banks)]
        ring.at += 1
        assert b.freed is not None
        r, b.freed = b.freed, None
        return b, r

    def mm(self, out, pairs, *after, start=True, stop=True, skip=False):
        self.wait("pe", after)
        for i, (l, r) in enumerate(pairs):
            t = self.op("pe", lambda e, l=l, r=r, i=i: e.matmul(
                out, l, r, start=start and i == 0, stop=stop and i == len(pairs) - 1, skip_group_check=skip),
                inc=i == len(pairs) - 1)
        return t

    def tr(self, out, in_, ident, *after, inc=True):
        return self.op("pe", lambda e: e.transpose(out, in_, ident), *after, inc=inc)

    def tt(self, out, a, b, op, *after, eng="dve"):
        return self.op(eng, lambda e: e.tensor_tensor(out, a, b, op), *after)

    def ts(self, out, a, s1, s2, op0, op1, *after, eng="dve"):
        if op1 is None:
            return self.op(eng, lambda e: e.tensor_scalar(out, a, s1, None, op0), *after)
        return self.op(eng, lambda e: e.tensor_scalar(out, a, s1, s2, op0, op1), *after)

    def stt(self, out, a, s, b, op0, op1, *after):
        return self.op("dve", lambda e: e.scalar_tensor_tensor(out=out, in0=a, scalar=s, in1=b, op0=op0, op1=op1),
                       *after)

    def red(self, out, a, op, *after):
        return self.op("dve", lambda e: e.tensor_reduce(out, a, X, op), *after)

    def ttr(self, out, a, b, init, op0, op1, acc, *after):
        return self.op("dve", lambda e: e.tensor_tensor_reduce(out, a, b, 1.0, init, op0, op1, acc), *after)

    def recip(self, out, a, *after):
        return self.op("dve", lambda e: e.reciprocal(out, a), *after)

    def act(self, out, in_, f, *after, bias=None, scale=1.0, acc=None):
        kw = {"scale": scale}
        if bias is not None:
            kw["bias"] = bias
        if acc is not None:
            kw["accum_out"] = acc
        return self.op("act", lambda e: e.activation(out, in_, f, **kw), *after)

    def copy(self, out, in_, *after, eng=None):
        if eng is None:
            self.flip ^= 1
            eng = "act" if self.flip else "dve"
        if eng == "act":
            return self.act(out, in_, ACT.Copy, *after)
        return self.op("dve", lambda e: e.tensor_copy(out, in_), *after)

    def sb(self, scope, name, shape, dt=F32):
        return scope.enter_context(self.nc.sbuf_tensor(name, shape, dt))


def bc(ap, axis, n):
    a = ap.unsqueeze(axis)
    shape = list(a.shape)
    shape[axis] = n
    return a.to_broadcast(shape)


def build(nc, d, out):
    with ExitStack() as ctx:
        P = Prog(nc, ctx)
        s_load = [ctx.enter_context(nc.semaphore(f"s_load{i}")) for i in range(2)]
        s_out = ctx.enter_context(nc.semaphore("s_out"))
        ring = P.sb(ctx, "wring", [128, NSLOT, SLOT])
        s_w = [ctx.enter_context(nc.semaphore(f"s_w{i}")) for i in range(NSLOT + XSLOT)]
        slots = list(range(NSLOT))
        views = [ring[:, i, :] for i in range(NSLOT)] + [None] * XSLOT
        slot_n = [0] * (NSLOT + XSLOT)
        released = [None] * (NSLOT + XSLOT)
        at = [0]
        def shaped(v, shape):
            n = 1
            for x in shape[1:]:
                n *= x
            v = v[0:shape[0], 0:n]
            if len(shape) == 3:
                v = v.rearrange("p (a b) -> p a b", a=shape[1])
            return v

        def fetch(src):
            i = slots[at[0] % len(slots)]
            at[0] += 1
            slot_n[i] += 16
            v = shaped(views[i], src.shape)
            return Tile(i, v, P.dma("sp", v, src, f"w{i}", s_w[i], slot_n[i], released[i]))

        def release(tiles, *toks):
            for w in tiles:
                released[w.slot] = list(toks)

        def fetch_all(src):
            k = 2048 // src.shape[2]
            return [fetch(src[:, n:min(n + k, src.shape[1]), :]) for n in range(0, src.shape[1], k)]

        def at_k(tiles, k):
            n = tiles[0].v.shape[1]
            return tiles[k // n].v[:, k % n, :]

        def loaded(tiles):
            return [w.tok for w in tiles]

        def split(w, a, b, eng, *after):
            a, b = shaped(a, w.v.shape), shaped(b, w.v.shape)
            ta = P.act(a, w.v, ACT.Copy, w.tok, *after)
            tb = P.tt(b, w.v, a.bitcast(F32), ALU.subtract, ta, eng=eng)
            release([w], ta, tb)
            return Parts(a, b, [ta, tb])

        class Stream:

            def __init__(self, entries, ab, eng="dve"):
                self.entries, self.ab, self.eng = entries, ab, eng
                self.parts, self.products = [], []

            def ahead(self, eng, n=1):
                while len(self.parts) < min(len(self.products) + n, len(self.entries)):
                    j = len(self.parts)
                    w = fetch(self.entries[j][1])
                    self.parts.append(split(w, self.ab[:, j % 2, 0, :], self.ab[:, j % 2, 1, :], eng,
                                            self.products[j - 2] if j > 1 else None))

            def take(self, name):
                self.ahead(self.eng, 2)
                j = len(self.products)
                assert self.entries[j][0] == name, (self.entries[j][0], name)
                return self.parts[j]

        def tiles_of(name, src):
            return [(f"{name}.{c}", src[:, 4 * c:4 * c + 4, :]) for c in range(2)]

        def square(name, w):
            w = w.rearrange("(p k) n -> p k n", k=8)
            return [x for c in range(2) for x in tiles_of(f"{name}{c}", w[:, :, 512 * c:512 * c + 512])]

        const_o, const_n = offsets(CONST)
        small_o, small_n = offsets(SMALL)
        cst = P.sb(ctx, "cst", [128, const_n])
        sml = P.sb(ctx, "sml", [128, small_n])
        post = P.sb(ctx, "post", [128, 3], I32)
        h = P.sb(ctx, "h", [128, 4, 1024])
        ld = [0, 0]

        def load(o, i, late=0):
            ld[late] += 16
            P.dma("sp", o, i, f"load{late}", s_load[late], ld[late])

        late_n = const_o["amask"][0]
        load(h[:, 0:2, :], d["x"].rearrange("o (t p) d -> p (o t) d", p=128))
        load(cst[:, 0:late_n], d["const"][:, 0:late_n])
        load(sml[:, :], d["small"])
        T0 = ("load0", s_load[0], ld[0])
        for e in ("pe", "act", "dve", "pool"):
            P.wait(e, [T0])

        def C(name, k=None):
            a, w = const_o[name]
            return cst[:, a:a + w]

        def S(name):
            a, w = small_o[name]
            return sml[:, a:a + w]

        ident = C("ident")
        NB = 3
        bS = P.sb(ctx, "bS", [128, 2, 512])
        bP = P.sb(ctx, "bP", [128, NB, 512])
        bT = P.sb(ctx, "bT", [128, NB, 512])
        st = P.sb(ctx, "st", [128, 4, 8])
        ss = P.sb(ctx, "ss", [128, 8])
        rs = P.sb(ctx, "rs", [128, 8])
        xs = P.sb(ctx, "xs", [128, 2, 1024])
        grow = P.sb(ctx, "grow", [128, 2, 1024])
        rt = P.sb(ctx, "rt", [128, 4, 256])
        mod = P.sb(ctx, "mod", [128, 2, 24, 2])
        Amod = P.sb(ctx, "Amod", [128, 2, 2, 8])

        def rstd(rows, width, n, *after, c0=0):
            for i, r in enumerate(rows):
                P.ttr(xs[:, 0, 0:width], r, r, 0.0, ALU.mult, ALU.add, ss[:, c0 + i:c0 + i + 1], *after)
            s = ss[:, c0:c0 + n]
            t = P.ts(s, s, 1.0 / width, EPS, ALU.mult, ALU.add)
            return P.tt(rs[:, c0:c0 + n], s, C("nhalf")[:, 0:n], ALU.pow, t, eng="pool")

        def to_T(cols, nk, put, *after):
            for k0 in range(0, nk, 4):
                n = min(4, nk - k0)
                b, free = P.bank()
                P.wait("pe", [after, free])
                for k in range(n):
                    t = P.tr(b.t[:, k * 128:k * 128 + 128], cols(k0 + k), ident, inc=k == n - 1)
                b.freed = [put(k0, n, b.t[:, 0:n * 128].rearrange("p (k t) -> p k t", k=n), t)]
            return t

        def halves(ps, A, B, t):
            ta = P.act(A, ps, ACT.Copy, t)
            return P.tt(B, ps, A.bitcast(F32), ALU.subtract, ta)

        def squares(rows, c0, *after):
            for i, r in enumerate(rows):
                t = P.act(junk, r, ACT.Square, *after, scale=1.0 / 32.0, acc=ss[:, c0 + i:c0 + i + 1])
            return t

        def rsqrt(c0, n, t):
            t = P.ts(ss[:, c0:c0 + n], ss[:, c0:c0 + n], EPS, None, ALU.add, None, t, eng="pool")
            return P.tt(rs[:, c0:c0 + n], ss[:, c0:c0 + n], C("nhalf")[:, 0:n], ALU.pow, eng="pool")

        mfree, mq = [None] * 3, [0]

        def diag(i, c, t0):
            return P.ts(bP[:, 2, i * 128:(i + 1) * 128], ident, rs[:, c:c + 1], None, ALU.mult, None, t0)

        def norm_T(tiles, A, B, scale, shift):
            for i, r, td in tiles:
                D = bP[:, 2, i * 128:(i + 1) * 128]
                a, b2 = scale(i), (shift(i) if shift else None)
                rv = r.rearrange("p (d k) -> p k d", k=8)
                for k0 in (0, 4):
                    b, free = P.bank()
                    P.wait("pe", [free, td])
                    for k in range(4):
                        t = P.mm(b.t[:, k * 128:(k + 1) * 128], [(rv[:, k0 + k, :], D)])
                    ps = b.t[:, :].rearrange("p (k t) -> p k t", k=4)
                    q = mq[0] % 3
                    mq[0] += 1
                    m = bT[:, q, :].rearrange("p (k t) -> p k t", k=4)
                    t = P.tt(m, ps, bc(a[:, k0:k0 + 4], 2, 128), ALU.mult, t, mfree[q])
                    b.freed = [t]
                    if b2 is not None:
                        t = P.tt(m, m, bc(b2[:, k0:k0 + 4], 2, 128), ALU.add)
                    oa, ob = (o[:, k0:k0 + 4, i * 128:(i + 1) * 128] for o in (A, B))
                    t = P.act(oa, m, ACT.Copy, t)
                    mfree[q] = P.tt(ob, m, oa.bitcast(F32), ALU.subtract, t, eng="pool")
            return [P.last("act"), P.last("pool")]

        def three(out, l, r, first, last, *after):
            P.wait("pe", after)
            for n, (x, y) in enumerate(((0, 0), (0, 1), (1, 0))):
                t = P.op("pe", lambda e, x=x, y=y, n=n: e.matmul(out, l[x], r[y], start=first and n == 0, stop=last and n == 2),
                         inc=n == 2)
            return t

        def lin(stream, name, A, B, cols, tiles, put, *after):
            open_ = {i: P.bank() for i in tiles}
            for c in range(2):
                w = stream.take(f"{name}.{c}")
                P.wait("pe", [w.tok, after])
                for i in tiles:
                    b, free = open_[i]
                    for k in range(4):
                        q = 4 * c + k
                        ts_ = slice(i * 128, (i + 1) * 128)
                        t = three(b.t[:, 0:cols], (A[:, q, ts_], B[:, q, ts_]), (w.a[:, k, 0:cols], w.b[:, k, 0:cols]),
                                  q == 0, q == 7, free)
                    if c == 1:
                        b.freed = [put(i, b.t[:, 0:cols], t)]
                stream.products.append(t)

        def lin_by(stream, name, A, B, cols, parts, put):
            stream.ahead("pool", 2)
            ws = stream.parts[len(stream.products):][:2]
            for tiles, after in parts:
                P.wait("pe", after)
                for i in tiles:
                    b, free = P.bank()
                    for q in range(8):
                        w, k = ws[q // 4], q % 4
                        if k == 0:
                            P.wait("pe", w.tok)
                        ts_ = slice(i * 128, (i + 1) * 128)
                        t = three(b.t[:, 0:cols], (A[:, q, ts_], B[:, q, ts_]), (w.a[:, k, 0:cols], w.b[:, k, 0:cols]),
                                  q == 0, q == 7, free)
                    b.freed = [put(i, b.t[:, 0:cols], t)]
            stream.products += [t, t]

        def linT(stream, name, A, B, n, put, *after):
            open_ = {j: P.bank() for j in range(4)}
            for c in range(2):
                w = stream.take(f"{name}.{c}")
                P.wait("pe", [w.tok, after])
                for j in range(4):
                    b, free = open_[j]
                    for k in range(4):
                        q = 4 * c + k
                        cs = slice(j * 128, (j + 1) * 128)
                        t = three(b.t[:, 0:n], (w.a[:, k, cs], w.b[:, k, cs]), (A[:, q, 0:n], B[:, q, 0:n]),
                                  q == 0, q == 7, free)
                    if c == 1:
                        b.freed = [put(j, b.t[:, 0:n], t)]
                stream.products.append(t)

        junk = bS[:, :, :].rearrange("p a n -> p (a n)")
        pfree = [None] * NB
        tfree = [None] * NB
        sfree = [None] * 2

        def attend(units, other=iter(())):
            n = len(units)
            live = {}

            def scores(i):
                u = units[i]
                b, free = P.bank()
                P.wait("pe", [free, u["after"]])
                for col, w, l, r in u["qk"]:
                    t = P.mm(b.t[:, col:col + w], [(l, r)])
                live[i] = {"b": b, "t": t}

            def soft(i):
                u, L = units[i], live[i]
                x = L["b"].t[:, 0:u["nk"]]
                m = L["m"] = st[:, i % 4, :]
                P.wait("dve", [sfree[i % 2]])
                srcs, tm, seen_ = u["peak"](x, bS[:, i % 2, 0:u["nk"]], m, L["t"])
                sc = u["scale"]
                if u.get("sink") is not None:
                    t = P.ts(m[:, 1:2], m[:, 0:1], -sc, u["nsink"], ALU.mult, ALU.min, tm)
                elif len(srcs) == 2:
                    t = P.ts(m[:, 1:2], m[:, 0:1], m[:, 4:5], -sc, ALU.max, ALU.mult, tm)
                else:
                    t = P.ts(m[:, 1:2], m[:, 0:1], -sc, None, ALU.mult, None, tm)
                c = 0
                for n_, src in enumerate(srcs):
                    w = src.shape[-1]
                    te = P.act(bP[:, i % NB, c:c + w], src, ACT.Exp, t, pfree[i % NB], bias=m[:, 1:2], scale=sc,
                               acc=m[:, 2 + n_:3 + n_])
                    c += w
                sfree[i % 2] = te
                L["b"].freed = seen_ + [te]
                L["two"] = len(srcs) == 2
                if u.get("sink") is not None:
                    te = P.act(m[:, 3:4], u["sink"], ACT.Exp, bias=m[:, 1:2])
                    L["two"] = True
                L["p"] = te

            def turn(i):
                u, L = units[i], live[i]
                b, free = P.bank()
                nk = u["nk"]
                P.wait("pe", [free, L["p"]])
                m, tr = L["m"], L["p"]
                if L["two"]:
                    tr = P.tt(m[:, 2:3], m[:, 2:3], m[:, 3:4], ALU.add, tr, eng="pool")
                L["r"] = P.tt(m[:, 4:5], m[:, 2:3], C("minus"), ALU.pow, tr, eng="pool")
                if u.get("gate") is not None:
                    L["r"] = P.tt(m[:, 4:5], m[:, 4:5], u["gate"], ALU.mult, eng="pool")
                blocks = [(c, min(128, nk - c)) for c in range(0, nk, 128)]
                for j, (c, w) in enumerate(blocks):
                    t = P.tr(b.t[0:w, j * 128:(j + 1) * 128], bP[:, i % NB, c:c + w], ident, inc=j == len(blocks) - 1)
                pfree[i % NB] = t
                w = blocks[0][1]
                t = P.copy(bT[0:w, i % NB, 0:128 * len(blocks)], b.t[0:w, 0:128 * len(blocks)], t, tfree[i % NB],
                           eng="act")
                b.freed = [t]
                L["pt"] = t

            def mix(i):
                u, L = units[i], live.pop(i)
                b, free = P.bank()
                t = P.mm(b.t[:, 0:64], [(bT[0:v.shape[0], i % NB, j * 128:(j + 1) * 128], v) for j, v in enumerate(u["v"])],
                         free, L["pt"])
                tfree[i % NB] = t
                m = L["m"]
                b.freed = [u["put"](b.t[:, 0:64], m[:, 4:5], t, L["r"])]

            for s in range(n + 4):
                if s < n:
                    scores(s)
                next(other, None)
                if 0 <= s - 1 < n:
                    soft(s - 1)
                next(other, None)
                if 0 <= s - 2 < n:
                    turn(s - 2)
                next(other, None)
                if 0 <= s - 4 < n:
                    mix(s - 4)

        def own_half(dst, which, i, ps, t):
            for hp in range(2):
                o = slice(64 * hp, 64 * hp + 64)
                t = P.copy(dst[o, hp, which, i * 128:(i + 1) * 128], ps[o], t, eng="dve")
            return t

        def peak(x, s, m, t):
            t = P.red(m[:, 0:1], x, ALU.max, t)
            return [x], t, [t]

        def peak_masked(mask):
            def f(x, s, m, t):
                t = P.ttr(s, x, mask, -3e38, ALU.add, ALU.max, m[:, 0:1], t)
                return [s], t, [t]
            return f

        def modulations(ring):
            for l in range(2):
                for c in range(6):
                    w = fetch_all(d["w_ada"][l, c])
                    b, free = P.bank(ring)
                    P.wait("pe", [loaded(w), free, tsc])
                    for k in range(8):
                        o = slice(32 * (k % 4), 32 * (k % 4) + 32)
                        t = P.mm(b.t[o, :], [(scT[:, k, :], at_k(w, k))], start=k < 4, stop=k > 3)
                    release(w, t)
                    yield
                    part = rt[:, 2 * (c % 2):2 * (c % 2) + 2, :].rearrange("p a b -> p (a b)")
                    t = P.act(part, b.t[:, :], ACT.Copy, t)
                    b.freed = [t]
                    yield
                    b, free = P.bank(ring)
                    P.wait("pe", [free, t])
                    for j in range(4):
                        t = P.mm(b.t[:, 2 * j:2 * j + 2], [(part[:, j * 128:(j + 1) * 128], C("pick"))])
                    yield
                    b.freed = [P.tt(mod[:, l, 4 * c:4 * c + 4, :], b.t[:, 0:8].rearrange("p (c w) -> p c w", w=2),
                                      bc(S("adab")[:, 24 * l + 4 * c:24 * l + 4 * c + 4], 2, 2), ALU.add, t)]
                    yield
                for wh in range(2):
                    P.stt(Amod[:, l, wh, :], mod[:, l, 8:16, wh], 1.0, S("ng0" if l == 0 else "ng1"), ALU.add, ALU.mult)

        with ExitStack() as sc:
            ab = P.sb(sc, "ab0", [128, 2, 2, SLOT], F32R)
            scT = P.sb(sc, "scT", [128, 8, 32])
            P.op("pool", lambda e: e.memset(scT[:, :, :], 0.0))
            tsc = P.act(scT[:, :, 0:2], S("cc").rearrange("p (k w) -> p k w", w=2), ACT.Silu, P.last("pool"))
            uA, uB = (P.sb(sc, n, [128, 8, 256], F32R) for n in ("uA", "uB"))
            entries = [("sm", d["w_sm"])]
            for n in ("gqk", "gv", "q", "kv", "kvc", "gr"):
                entries += tiles_of(n, d["w_" + n])
            for c in range(2):
                for m in range(2):
                    entries += tiles_of(f"m{m}{c}", d["w_m"][2 * m + c])
            stream = Stream(entries + square("out", d["w_out"]), ab)
            hx = [(i, h[:, i, :]) for i in range(2)]
            grows = grow[:, :, :].rearrange("p i (m n) -> p i m n", m=2)

            def mix_gate(m):
                lin(stream, f"m{m}0", uA, uB, 512, range(2), lambda i, ps, t: P.copy(grows[:, i, m, :], ps, t, eng="act"))

            t = rsqrt(0, 2, squares([h[:, 0, :], h[:, 1, :]], 0))
            norm_T([(*hx[0], diag(0, 0, t))], uA, uB, lambda i: S("gmix"), None)
            stream.ahead("pool")
            load(post[:, :], d["pos"], 1)
            load(cst[:, late_n:], d["const"][:, late_n:], 1)
            load(h[:, 2:4, :], d["ctx"].rearrange("o (t p) d -> p (o t) d", p=128), 1)
            T1 = ("load1", s_load[1], ld[1])
            tu = norm_T([(*hx[1], diag(1, 1, t))], uA, uB, lambda i: S("gmix"), None)
            ang = P.sb(sc, "ang", [128, 3, 32])
            rr = P.sb(sc, "rr", [128, 3, 32])
            cos = P.sb(sc, "cos", [128, 3, 32])
            sin = P.sb(sc, "sin", [128, 3, 32])
            posf = P.sb(sc, "posf", [128, 3])
            P.op("dve", lambda e: e.tensor_copy(posf[:, :], post[:, :]), T1)
            P.wait("act", [T1])
            P.wait("pe", [T1])
            P.wait("pool", [T1])
            P.tt(ang[:, :, :], bc(C("inv"), 1, 3), bc(posf[:, :], 2, 32), ALU.mult)
            twopi = 2.0 * np.pi
            hi = float(np.float32(np.round(twopi * 128) / 128))
            mid = float(np.float32(np.round((twopi - hi) * 2.0 ** 19) / 2.0 ** 19))
            lo = float(np.float32(twopi - hi - mid))
            magic = 12582912.0
            P.ts(rr[:, :, :], ang[:, :, :], 1.0 / twopi, magic, ALU.mult, ALU.add)
            P.ts(rr[:, :, :], rr[:, :, :], -magic, None, ALU.add, None)
            for c in (hi, mid, lo):
                P.stt(ang[:, :, :], rr[:, :, :], -c, ang[:, :, :], ALU.mult, ALU.add)
            t = P.ts(ang[:, :, :], ang[:, :, :], 3.1415925, -3.1415925, ALU.min, ALU.max)
            P.act(sin[:, :, :], ang[:, :, :], ACT.Sin, t)
            t = P.act(rr[:, :, :], ang[:, :, :], ACT.Sin, scale=0.5)
            P.tt(rr[:, :, :], rr[:, :, :], rr[:, :, :], ALU.mult, t)
            P.ts(cos[:, :, :], rr[:, :, :], -2.0, 1.0, ALU.mult, ALU.add)

            gate = P.sb(sc, "gate", [128, 2, 24])
            alow = P.sb(sc, "alow", [16, 256])
            low = P.sb(sc, "low", [128, 2, 16])
            w = stream.take("sm")
            for i in range(2):
                b, free = P.bank()
                P.wait("pe", [w.tok, free, tu])
                for k in range(8):
                    ts_ = slice(i * 128, (i + 1) * 128)
                    t = three(b.t[:, 0:40], (uA[:, k, ts_], uB[:, k, ts_]), (w.a[:, k, :], w.b[:, k, :]), k == 0, k == 7)
                P.act(gate[:, i, :], b.t[:, 0:24], ACT.Sigmoid, t)
                tlow = P.act(low[:, i, :], b.t[:, 24:40], ACT.Copy)
                b.freed = [tlow]
            stream.products.append(t)

            qk = P.sb(sc, "qk", [128, 4, 256])

            def put(j, ps, t):
                return P.ts(qk[:, j, :], ps, 0.125 if j < 2 else 1.0, None, ALU.mult, None, t)
            linT(stream, "gqk", uA, uB, 256, put)
            b, free = P.bank()
            P.wait("pe", [free, tlow])
            for i in range(2):
                t = P.tr(b.t[0:16, i * 128:(i + 1) * 128], low[:, i, :], ident)
            ta = P.copy(alow[:, :], b.t[0:16, 0:256], t)
            b.freed = [ta]


            gv = P.sb(sc, "gv", [128, 2, 512])
            lin(stream, "gv", uA, uB, 512, range(2), lambda i, ps, t: P.copy(gv[:, i, :], ps, t))

            q = P.sb(sc, "q", [128, 2, 512])
            kv = P.sb(sc, "kv", [128, 2, 512])
            lin(stream, "q", uA, uB, 512, range(2), lambda i, ps, t: P.copy(q[:, i, :], ps, t, eng="act"))
            lin(stream, "kv", uA, uB, 512, range(2), lambda i, ps, t: P.copy(kv[:, i, :], ps, t, eng="act"))

            yn = P.sb(sc, "yn", [128, 2, 512])
            Bt = yn[:, :, :].rearrange("p a b -> p (a b)").rearrange("p (m s n) -> p m s n", m=2, s=16)
            tzb = P.op("pool", lambda e: e.memset(yn[:, :, :], 0.0))
            hid = P.sb(sc, "hid", [128, 2, 2, 30])
            kcr = P.sb(sc, "kcr", [16, 2, 2, 64])
            kcT = P.sb(sc, "kcT", [128, 2, 2, 16])
            for hp in range(2):
                tzc = P.op("pool", lambda e, hp=hp: e.memset(kcT[64 - 64 * hp:128 - 64 * hp, hp, :, :], 0.0))
            vc = P.sb(sc, "vc", [16, 2, 64])

            def put(j, ps, t):
                m, g = j // 2, j % 2
                for jp in range(2):
                    p0 = 64 * jp
                    src = ps[p0:p0 + 64, :].rearrange("p (n s) -> p s n", s=16)
                    pos = S("posk" if m == 0 else "posv")
                    for half in range(2):
                        t = P.tt(Bt[p0:p0 + 64, m, 8 * half:8 * half + 8, 15 * g:15 * g + 15],
                                 src[:, jp:16:2, half:half + 15],
                                 bc(pos[p0:p0 + 64, 8 * half:8 * half + 8], 2, 15), ALU.add, t, tzb)
                return t
            linT(stream, "kvc", uA, uB, 256, put)
            tb = P.last("dve")
            gr = P.sb(sc, "gr", [128, 2, 512])
            lin(stream, "gr", uA, uB, 512, range(2), lambda i, ps, t: P.act(gr[:, i, :], ps, ACT.Silu, t))

            stream.eng = "pool"
            stream.ahead("dve", 2)
            la = P.sb(sc, "la", [128, 2, 256])
            cum = P.sb(sc, "cum", [128, 2, 256])
            tmp = P.sb(sc, "tmp", [128, 2, 256])
            ones = P.sb(sc, "ones", [128, 256])
            tones = P.op("pool", lambda e: e.memset(ones[:, :], 1.0))
            b, free = P.bank()
            P.wait("pe", [ta, free])
            for j in range(2):
                tla = P.mm(b.t[:, j * 256:(j + 1) * 256], [(S("wa2")[0:16, j * 128:(j + 1) * 128], alow[:, :])])
            bla = b
            for j in range(2):
                t = P.ts(la[:, j, :], bla.t[:, j * 256:(j + 1) * 256], S("glaba")[:, j:j + 1], None, ALU.add, None, tla)
            bla.freed = [t]
            t = P.stt(tmp[:, :, :], la[:, :, :], -1.0, la[:, :, :], ALU.mult, ALU.max)
            P.act(tmp[:, :, :], tmp[:, :, :], ACT.Exp, t, scale=-1.0)
            t = P.act(tmp[:, :, :], tmp[:, :, :], ACT.Ln, tones, bias=ones[:, 0:1])
            P.stt(la[:, :, :], la[:, :, :], 0.0, tmp[:, :, :], ALU.min, ALU.subtract, t)
            P.ts(la[:, :, :], la[:, :, :], 1.0 / 16.0, None, ALU.mult, None)
            for j in range(2):
                P.op("dve", lambda e, j=j: e.tensor_tensor_scan(cum[:, j, :], ones[:, :], la[:, j, :], 0.0, ALU.mult, ALU.add),
                     tones)

            def rope_half(dst1, dst2, x1, x2, co, si, tmps):
                a, b_, c_, d_ = tmps
                P.tt(a, x1, co, ALU.mult)
                P.tt(b_, x2, si, ALU.mult)
                P.tt(c_, x2, co, ALU.mult)
                P.tt(d_, x1, si, ALU.mult)
                P.tt(dst1, a, b_, ALU.subtract)
                return P.tt(dst2, c_, d_, ALU.add)

            Am = P.sb(sc, "Am", [128, 4, 3, 128])
            kr = Am[:, :, :, :].rearrange("p h b t -> p (h b t)")[:, 0:1024].rearrange("p (i n a r) -> p i n a r", i=2, n=4, a=2)
            for i in range(2):
                qv = q[:, i, :].rearrange("p (h a r) -> p h a r", h=8, a=2)
                tm = [rt[:, n, :].rearrange("p (h r) -> p h r", h=8) for n in range(4)]
                P.wait("dve", [P.last("act")])
                rope_half(qv[:, :, 0, :], qv[:, :, 1, :], qv[:, :, 0, :], qv[:, :, 1, :],
                          bc(cos[:, i, :], 1, 8), bc(sin[:, i, :], 1, 8), tm)
                kw = kv[:, i, 0:256].rearrange("p (h a r) -> p h a r", h=4, a=2)
                tm = [rt[:, n, 0:128].rearrange("p (h r) -> p h r", h=4) for n in range(4)]
                ko = kr[:, i, :, 0, :].rearrange("p h (a r) -> p h a r", a=2)
                rope_half(ko[:, :, 0, :], ko[:, :, 1, :], kw[:, :, 0, :], kw[:, :, 1, :],
                          bc(cos[:, i, :], 1, 4), bc(sin[:, i, :], 1, 4), tm)
                tk = P.op("dve", lambda e, i=i: e.tensor_copy(kr[:, i, :, 1, :], kr[:, i, :, 0, :]))
            mix_gate(0)
            hsum = bT[:, 0, :]
            b, free = P.bank()
            for m in range(2):
                w = fetch_all(d["w1k" if m == 0 else "w1v"])
                P.wait("pe", [loaded(w), free, tb])
                for j in range(16):
                    o = slice(32 * (j % 4), 32 * (j % 4) + 32)
                    t = P.mm(b.t[o, m * 256:(m + 1) * 256], [(Bt[:, m, j, :], at_k(w, j))], start=j < 4, stop=j > 11)
                release(w, t)
            th = P.act(hsum, b.t[:, :], ACT.Copy, t, P.last("pool"))
            b.freed = [th]
            qT = P.sb(sc, "qT", [128, 4, 256])
            kT = P.sb(sc, "kT", [128, 2, 4, 256])
            for hp in range(2):
                tz = P.op("pool", lambda e, hp=hp: e.memset(kT[64 - 64 * hp:128 - 64 * hp, hp, :, :], 0.0))
            for i in range(2):
                to_T(lambda k: q[:, i, k * 128:(k + 1) * 128], 4,
                     lambda k0, n, ps, t: P.copy(qT[:, :, i * 128:(i + 1) * 128], ps, t), tk)
                to_T(lambda k: kr[:, i, k, :, :].rearrange("p a r -> p (a r)"), 4,
                     lambda k0, n, ps, t: own_half(kT, slice(0, 4), i, ps, t), tk)

            b, free = P.bank()
            P.wait("pe", [free, th])
            for m in range(2):
                for c in range(2):
                    o = (2 * m + c) * 30
                    t = P.mm(b.t[:, o:o + 30], [(hsum[:, m * 256 + c * 128:m * 256 + (c + 1) * 128], C("fold"))])
            for m in range(2):
                for c in range(2):
                    o = (2 * m + c) * 30
                    th = P.act(hid[:, m, c, :], b.t[:, o:o + 30], ACT.Gelu_apprx_tanh, t,
                               bias=S("b1k" if m == 0 else "b1v")[:, c:c + 1])
            b.freed = [th]
            for m in range(2):
                w2 = S("w2k" if m == 0 else "w2v").rearrange("p (c n) -> p c n", c=2)
                b2 = S("b2k" if m == 0 else "b2v")[0:15, :]
                b, free = P.bank()
                P.wait("pe", [free, th])
                for g in range(2):
                    t = P.mm(b.t[0:15, g * 64:g * 64 + 64],
                             [(hid[:, m, c, 15 * g:15 * g + 15], w2[:, c, :]) for c in range(2)])
                ps = b.t[0:15, 0:128].rearrange("p (g n) -> p g n", g=2)
                if m == 1:
                    b.freed = [P.tt(vc[0:15, :, :], ps, bc(b2, 1, 2), ALU.add, t)]
                    continue
                t = P.tt(kcr[0:15, :, 0, :], ps, bc(b2, 1, 2), ALU.add, t)
                b.freed = [t]
                kk = kcr[0:15, :, 0, :].rearrange("p g (a r) -> p g a r", a=2)
                tm = [rt[0:15, n, 0:64].rearrange("p (h r) -> p h r", h=2) for n in range(4)]
                rope_half(kk[:, :, 0, :], kk[:, :, 1, :], kk[:, :, 0, :], kk[:, :, 1, :],
                          bc(cos[0:15, 2, :], 1, 2), bc(sin[0:15, 2, :], 1, 2), tm)
                t = P.op("dve", lambda e: e.tensor_copy(kcr[0:15, :, 1, :], kcr[0:15, :, 0, :]))
                b, free = P.bank()
                for g in range(2):
                    t = P.tr(b.t[:, g * 16:g * 16 + 15], kcr[0:15, g, :, :].rearrange("p a r -> p (a r)"),
                             ident[0:15, 0:15], free, t)
                for g in range(2):
                    for hp in range(2):
                        o = slice(64 * hp, 64 * hp + 64)
                        t = P.copy(kcT[o, hp, g, 0:15], b.t[o, g * 16:g * 16 + 15], t, eng="dve")
                b.freed = [t]

            mix_gate(1)

            def nsa_put(kind, hh, i):
                def f(ps, r, t, tr):
                    o = yn[:, i, hh * 64:hh * 64 + 64]
                    return P.stt(o, ps, r, o, ALU.mult, ALU.add, t, tr, tyn)
                return f

            Q = la
            K = P.sb(sc, "K", [128, 2, 256])
            E = tmp
            P.op("pool", lambda e: e.memset(Am[:, :, :, :], 0.0), P.last("pe"))
            P.op("pool", lambda e: e.memset(Q[:, :, :], 0.0), P.last("dve"))
            P.op("pool", lambda e: e.memset(K[:, :, :], 0.0))
            tzero = P.last("pool")
            tcum = P.last("dve")
            go = q

            def place(hp, ps, li, *after):
                a0 = const_o["lev"][0] + 128 * li
                mk = bc(bc(cst[:, a0:a0 + 128].bitcast(U32), 1, 2), 1, 2)
                return P.op("dve", lambda e: e.copy_predicated(Am[:, hp:4:2, 0:2, :], mk, ps), *after)

            def decayed(ring):
                tq = None
                for m in (128,) + LEVELS:
                    nb = 128 // m
                    for j in range(2):
                        v = cum[:, j, :].rearrange("p (n a m) -> p n a m", a=2, m=m)
                        ev = E[:, j, :].rearrange("p (n a m) -> p n a m", a=2, m=m)
                        mid_ = v[:, :, 0, m - 1:m].to_broadcast([128, nb, m])
                        P.tt(ev[:, :, 1, :], v[:, :, 1, :], mid_, ALU.subtract, tcum, eng="pool")
                        t = P.tt(ev[:, :, 0, :], mid_, v[:, :, 0, :], ALU.subtract, tcum, eng="pool")
                    yield
                    t = P.act(E[:, :, :], E[:, :, :], ACT.Exp, t)
                    yield
                    for j in range(2):
                        def part(x, a):
                            return x.rearrange("p (n a m) -> p n a m", a=2, m=m)[:, :, a, :]
                        P.tt(part(Q[:, j, :], 1), part(qk[:, j, :], 1), part(E[:, j, :], 1), ALU.mult, t, tq, eng="pool")
                        tk_ = P.tt(part(K[:, j, :], 0), part(qk[:, 2 + j, :], 0), part(E[:, j, :], 0), ALU.mult, t, tq, eng="pool")
                    yield
                    held = []
                    for hp in range(2):
                        p0 = 64 * hp
                        b, free = P.bank(ring)
                        P.wait("pe", [tk_, free])
                        for pr in range(2):
                            for bl in range(1 if m == 128 else 2):
                                ks = K[p0:p0 + 64, pr, bl * 128:bl * 128 + 128]
                                qs = Q[p0:p0 + 64, pr, 128:256] if m == 128 else Q[p0:p0 + 64, pr, bl * 128:bl * 128 + 128]
                                tq = P.mm(b.t[:, (2 * pr + bl) * 128:(2 * pr + bl) * 128 + 128], [(ks, qs)])
                        held.append((b, tq))
                    yield
                    for hp, (b, t) in enumerate(held):
                        ps = b.t[:, :].rearrange("p (h b t) -> p h b t", h=2, b=2)
                        if m == 128:
                            b.freed = [P.copy(Am[:, hp:4:2, 2, :], ps[:, :, 0, :], t, tzero, eng="dve")]
                        else:
                            b.freed = [place(hp, ps, LEVELS.index(m), t, tzero)]
                    yield
                for hp in range(2):
                    p0 = 64 * hp
                    b, free = P.bank(ring)
                    P.wait("pe", [free])
                    for pr in range(2):
                        for bl in range(2):
                            tq = P.mm(b.t[:, (2 * pr + bl) * 128:(2 * pr + bl) * 128 + 128],
                                      [(qk[p0:p0 + 64, 2 + pr, bl * 128:bl * 128 + 128], qk[p0:p0 + 64, pr, bl * 128:bl * 128 + 128])])
                    ps = b.t[:, :].rearrange("p (h b t) -> p h b t", h=2, b=2)
                    b.freed = [place(hp, ps, len(LEVELS), tq)]
                tA = P.last("dve")
                yield
                for i in range(2):
                    b, free = P.bank(ring)
                    P.wait("pe", [free, tA])
                    for hh in range(4):
                        pairs = [(Am[:, hh, i, :], gv[:, i, hh * 128:hh * 128 + 128])]
                        if i == 1:
                            pairs.insert(0, (Am[:, hh, 2, :], gv[:, 0, hh * 128:hh * 128 + 128]))
                        t = P.mm(b.t[:, hh * 128:hh * 128 + 128], pairs)
                    b.freed = [P.copy(go[:, i, :], b.t[:, :], t, eng="dve")]
                    P.tt(xs[:, 0, 0:512], go[:, i, :], go[:, i, :], ALU.mult)
                    P.red(ss[:, 4 * i:4 * i + 4], xs[:, 0, 0:512].rearrange("p (h e) -> p h e", h=4), ALU.add)
                t = P.ts(ss[:, :], ss[:, :], 1.0 / 128, EPS, ALU.mult, ALU.add)
                t = P.tt(rs[:, :], ss[:, :], C("nhalf")[:, 0:8], ALU.pow, t, eng="pool")
                for i in range(2):
                    gov = go[:, i, :].rearrange("p (h e) -> p h e", h=4)
                    P.tt(gov, gov, bc(rs[:, 4 * i:4 * i + 4], 2, 128), ALU.mult, t)
                    P.tt(go[:, i, :], go[:, i, :], gr[:, i, :], ALU.mult)

            vcd = xs[0:120, 0, 0:512]
            b, free = P.bank()
            t = P.mm(b.t[0:120, 0:128], [(C("sel")[0:15, :], vc[0:15, :, :].rearrange("p g d -> p (g d)"))], free,
                     P.last("dve"))
            tvd = P.tt(vcd.rearrange("p (g h d) -> p g h d", g=2, h=4),
                       bc(b.t[0:120, 0:128].rearrange("p (g d) -> p g d", g=2), 2, 4),
                       bc(C("bd")[0:120, :].rearrange("p (g h) -> p g h", g=2), 3, 64), ALU.mult, t)
            b.freed = [tvd]
            held = []
            for i in range(2):
                b, free = P.bank()
                P.wait("pe", [free, tzc, P.last("act"), P.last("dve")])
                for hh in range(8):
                    t = P.mm(b.t[:, hh * 15:hh * 15 + 15],
                             [(qT[:, hh // 2, i * 128:(i + 1) * 128], kcT[:, hh % 2, hh // 4, 0:15])])
                held.append((b, t))
            pc = [rt[:, i, 0:120].rearrange("p (h n) -> p h n", h=8) for i in range(2)]
            te, tr = [None] * 2, [None] * 2
            for i, (b, t) in enumerate(held):
                P.tt(pc[i], b.t[:, 0:120].rearrange("p (h n) -> p h n", h=8), bc(C("cmpadd")[:, 15 * i:15 * i + 15], 1, 8),
                     ALU.add, t)
                b.freed = [P.last("dve")]
                P.red(st[:, i, :], pc[i], ALU.max)
                t = P.tt(pc[i], pc[i], bc(st[:, i, :], 2, 15), ALU.subtract)
                te[i] = P.act(pc[i], pc[i], ACT.Exp, t, scale=0.125)
            for i in range(2):
                t = P.red(st[:, 2 + i, :], pc[i], ALU.add, te[i])
                P.tt(st[:, 2 + i, :], st[:, 2 + i, :], C("minus").to_broadcast([128, 8]), ALU.pow, t, eng="pool")
                tr[i] = P.tt(st[:, 2 + i, :], st[:, 2 + i, :], gate[:, i, 0:24:3], ALU.mult, eng="pool")
                P.tt(pc[i], pc[i], bc(C("cmpok")[:, 15 * i:15 * i + 15], 1, 8), ALU.mult)
            for i in range(2):
                t = P.tt(pc[i], pc[i], bc(st[:, 2 + i, :], 2, 15), ALU.mult, tr[i])
                b, free = P.bank()
                t = P.tr(b.t[0:120, 0:128], rt[:, i, 0:120], ident, free, t)
                t = P.copy(rt[0:120, 2 + i, 0:128], b.t[0:120, 0:128], t, eng="act")
                b.freed = [t]
                b, free = P.bank()
                t = P.mm(b.t[:, :], [(rt[0:120, 2 + i, 0:128], vcd)], free, t, tvd)
                b.freed = [P.copy(yn[:, i, :], b.t[:, :], t, eng="act")]
            tyn = P.last("act")

            units = []
            te = [P.last("act"), P.last("dve"), tz]
            for kind in (1, 2):
                for i in range(2):
                    for hh in range(8):
                        g = hh // 4
                        u = {"after": te, "scale": 0.125, "put": nsa_put(kind, hh, i), "gate": gate[:, i, 3 * hh + kind:3 * hh + kind + 1]}
                        n = 128 * (i + 1)
                        c = 256 + (kind - 1) * 128 + g * 64
                        u.update(nk=n, qk=[(0, n, qT[:, hh // 2, i * 128:(i + 1) * 128], kT[:, hh % 2, 2 * (kind - 1) + g, 0:n])],
                                 peak=peak_masked(C("causal")[:, 256 - n:]), v=[kv[:, j, c:c + 64] for j in range(i + 1)])
                        units.append(u)
            def others():
                works = [modulations(Ring(P.banks[5:6])), decayed(Ring(P.banks[6:8]))]
                while works:
                    for g in list(works):
                        if next(g, works) is works:
                            works.remove(g)
                        else:
                            yield

            P.ring = Ring(P.banks[0:5])
            rest = others()
            attend(units, rest)
            for _ in rest:
                pass
            P.ring = Ring(P.banks)
            tg = P.last("dve")



            ynT, ogT = qT, kT[:, 0]
            for i in range(2):
                to_T(lambda k: yn[:, i, :].rearrange("p (d k) -> p k d", k=4)[:, k, :], 4,
                     lambda k0, n, ps, t: P.copy(ynT[:, :, i * 128:(i + 1) * 128], ps, t), tg)
                to_T(lambda k: go[:, i, :].rearrange("p (d k) -> p k d", k=4)[:, k, :], 4,
                     lambda k0, n, ps, t: P.tt(ogT[:, :, i * 128:(i + 1) * 128], ps, bc(S("glang"), 2, 128), ALU.mult, t))
            te = [P.last("act"), P.last("dve")]
            mx = grow
            stream.eng = "dve"
            for c in range(2):
                if c == 0:
                    sm = grows
                    for i in range(2):
                        P.act(grow[:, i, :], grow[:, i, :], ACT.Sigmoid)
                else:
                    sm = xs[:, :, :].rearrange("p i (m n) -> p i m n", m=2)
                    for m in range(2):
                        lin(stream, f"m{m}1", uA, uB, 512, range(2),
                            lambda i, ps, t: P.act(sm[:, i, m, :], ps, ACT.Sigmoid, t, P.last("dve")))
                wa, wb = (fetch(d[n].rearrange("(p k) n -> p k n", k=4)[:, :, c * 512:c * 512 + 512])
                          for n in ("w_proj_nsa", "w_proj_gla"))
                for i in range(2):
                    o = mx[:, i, c * 512:c * 512 + 512]
                    b, free = P.bank()
                    t = P.mm(b.t[:, :], [(ynT[:, k, i * 128:(i + 1) * 128], wa.v[:, k, :]) for k in range(4)],
                             wa.tok, free, te)
                    b.freed = [P.tt(o, b.t[:, :], sm[:, i, 0, :], ALU.mult, t, P.last("act"))]
                    b, free = P.bank()
                    t = P.mm(b.t[:, :], [(ogT[:, k, i * 128:(i + 1) * 128], wb.v[:, k, :]) for k in range(4)],
                             wb.tok, free)
                    b.freed = [P.tt(bS[:, 0, :], b.t[:, :], sm[:, i, 1, :], ALU.mult, t)]
                    tm_ = P.tt(o, o, bS[:, 0, :], ALU.add)
                release([wa, wb], t)
            for i in range(2):
                to_T(lambda k: mx[:, i, :].rearrange("p (d k) -> p k d", k=8)[:, k, :], 8,
                     lambda k0, n, ps, t: halves(ps, *(o[:, k0:k0 + n, i * 128:(i + 1) * 128] for o in (uA, uB)), t), tm_)
            te = [P.last("act"), P.last("dve")]
            for c in range(2):
                def put(i, ps, t):
                    o = h[:, i, c * 512:c * 512 + 512]
                    return P.tt(o, o, ps, ALU.add, t)
                lin(stream, f"out{c}", uA, uB, 512, range(2), put, te)
            P.barrier()

        T2 = [P.last(e) for e in ("pe", "act", "dve", "pool")]
        with ExitStack() as sc:
            vT = P.sb(sc, "vT", [128, 8, 256])
            t = rsqrt(0, 2, squares([h[:, 0, :], h[:, 1, :]], 0, P.last("dve")))
            for i in range(2):
                xv = xs[:, i, :].rearrange("p (k d) -> p k d", k=8)
                t = P.act(xv, h[:, i, :].rearrange("p (d k) -> p k d", k=8), ACT.Copy, t, scale=rs[:, i:i + 1])
                to_T(lambda k: xv[:, k, :], 8, lambda k0, n, ps, t: P.tt(
                    vT[:, k0:k0 + n, i * 128:(i + 1) * 128], ps, bc(S("gffn")[:, k0:k0 + n], 2, 128), ALU.mult, t), t)
            tv = P.last("dve")
            tctx = rsqrt(2, 2, squares([h[:, 2, :], h[:, 3, :]], 2))
            lg = bT[:, 2, 256:328].rearrange("p (i n) -> p i n", i=2)
            wr = S("wr").rearrange("p (k n) -> p k n", k=8)
            for i in range(2):
                b, free = P.bank()
                t = P.mm(b.t[:, 0:36], [(vT[:, k, i * 128:(i + 1) * 128], wr[:, k, :]) for k in range(8)], free, tv)
                b.freed = [P.tt(lg[:, i, :], b.t[:, 0:36], S("brout"), ALU.add, t)]
            R = bT[:, 2, 0:256].rearrange("p (i n) -> p i n", i=2)
            comb = P.sb(sc, "comb", [128, 2, 32])
            g4, e32 = lg[:, :, 0:4], lg[:, :, 4:36].rearrange("p i (g e) -> p i g e", g=4)
            m1, eg, sg, oh4 = R[:, :, 0:1], R[:, :, 1:5], R[:, :, 5:6], R[:, :, 6:10]
            w4, in8, oh8, oh8b, t8 = R[:, :, 10:14], R[:, :, 16:24], R[:, :, 24:32], R[:, :, 32:40], R[:, :, 40:48]
            ma, mb, e2, dn, c1, c2 = (R[:, :, 48 + n:49 + n] for n in range(6))
            tb_ = R[:, :, 64:96]

            def first(oh, x, mx_, n):
                P.tt(oh, x, mx_.to_broadcast([128, 2, n]), ALU.is_equal)
                P.tt(oh, oh, bc(C("desc")[:, 8 - n:8], 1, 2), ALU.mult)
                P.red(dn[:, :, 0], oh, ALU.max)
                return P.tt(oh, oh, dn.to_broadcast([128, 2, n]), ALU.is_equal)

            P.red(m1[:, :, 0], g4, ALU.max)
            t = P.tt(eg, g4, m1.to_broadcast([128, 2, 4]), ALU.subtract)
            t = P.act(eg, eg, ACT.Exp, t)
            P.red(sg[:, :, 0], eg, ALU.add, t)
            first(oh4, g4, m1, 4)
            pe_ = tb_.rearrange("p i (g e) -> p i g e", g=4)
            for i in range(2):
                P.tt(pe_[:, i], e32[:, i], bc(oh4[:, i], 2, 8), ALU.mult)
                P.red(in8[:, i], pe_[:, i].rearrange("p g e -> p e g"), ALU.add)
            P.red(ma[:, :, 0], in8, ALU.max)
            first(oh8, in8, ma, 8)
            P.stt(t8, oh8, NEG, in8, ALU.mult, ALU.add)
            P.red(mb[:, :, 0], t8, ALU.max)
            first(oh8b, t8, mb, 8)
            t = P.tt(e2, mb, ma, ALU.subtract)
            t = P.act(e2, e2, ACT.Exp, t)
            P.ts(dn, e2, 1.0, None, ALU.add, None, t)
            P.tt(dn, dn, sg, ALU.mult)
            P.recip(c1, dn)
            P.tt(c2, c1, e2, ALU.mult)
            A = bT[:, 2, 328:392].rearrange("p (i n) -> p i n", i=2)
            P.tt(t8, oh8, oh8b, ALU.add)
            av = A[:, :, :].rearrange("p i (g e) -> p i g e", g=4)
            for i in range(2):
                tA = P.tt(av[:, i], bc(t8[:, i], 1, 4), bc(oh4[:, i], 2, 8), ALU.mult)
            P.tt(oh8, oh8, c1.to_broadcast([128, 2, 8]), ALU.mult)
            P.tt(oh8b, oh8b, c2.to_broadcast([128, 2, 8]), ALU.mult)
            P.tt(oh8, oh8, oh8b, ALU.add)
            cv = comb[:, :, :].rearrange("p i (g e) -> p i g e", g=4)
            for i in range(2):
                t = P.tt(cv[:, i], bc(oh8[:, i], 1, 4), bc(oh4[:, i], 2, 8), ALU.mult)

            key = P.sb(sc, "key", [128, 2, 32])
            cnt = P.sb(sc, "cnt", [128, 1])
            flag = P.sb(sc, "flag", [1, 1], I32)
            b, free = P.bank()
            P.wait("pe", [free, tA])
            P.mm(b.t[:, 0:32], [(C("before"), A[:, 0, :])])
            P.mm(b.t[:, 32:64], [(C("ones"), A[:, 0, :]), (C("before"), A[:, 1, :])])
            t = P.mm(b.t[:, 64:96], [(C("ones"), A[:, 0, :]), (C("ones"), A[:, 1, :])])
            P.stt(key[:, :, :], b.t[:, 0:64].rearrange("p (i e) -> p i e", i=2), 1.0, A[:, :, :], ALU.add, ALU.mult, t)
            b.freed = [P.red(cnt[:, :], b.t[:, 64:96], ALU.max)]
            tflag = P.op("dve", lambda e: e.tensor_copy(flag[:, :], cnt[0:1, :]))

            big = P.sb(sc, "big", [128, 2, 32, 64])
            xring = P.sb(sc, "xring", [128, XSLOT, SLOT])
            for n in range(XSLOT):
                views[NSLOT + n] = xring[:, n, :]
                released[NSLOT + n] = T2
            order = []
            for p in range(17):
                order += [(n, e) for n in "gu" for e in (2 * p, 2 * p + 1)] if p < 16 else []
                order += [("d", 2 * p - 2), ("d", 2 * p - 1)] if p > 0 else []
            ahead = (NSLOT + XSLOT) // 2

            def source(kind, e):
                if kind == "d":
                    return d["w_down"][e].rearrange("(j p) n -> p j n", p=128)
                return d["w_gate" if kind == "g" else "w_up"][e].rearrange("(p k) f -> p k f", k=8)

            got = {}
            slots[:] = slots[at[0] % NSLOT:] + slots[:at[0] % NSLOT] + list(range(NSLOT, NSLOT + XSLOT))
            at[0] = 0
            for key_ in order[:ahead]:
                got[key_] = fetch_all(source(*key_))

            def stream():
                have, left = dict(got), order[ahead:]

                def tile(kind, e):
                    while (kind, e) not in have:
                        key_ = left.pop(0)
                        have[key_] = fetch_all(source(*key_))
                    return have.pop((kind, e))
                return tile

            Y = P.banks[0:4]

            def finish(ty):
                for i in range(2):
                    for c in range(2):
                        o = h[:, i, c * 512:c * 512 + 512]
                        t = P.tt(o, o, Y[2 * i + c].t[:, :], ALU.add, ty)
                P.barrier()

            def dense():
                tile = stream()
                combT = big[0:32, 0, 0:4, :].rearrange("p a b -> p (a b)")
                cb = big[:, 0, 4:12, :].rearrange("p (a b) c -> p a (b c)", a=2)
                sl = big[:, 0, 12:20, :].rearrange("p (a b) c -> p a (b c)", a=2)
                hT = big[:, 1, :, :].rearrange("p (a f b) c -> p a f (b c)", a=2, f=4)
                b, free = P.bank()
                for i in range(2):
                    t = P.tr(b.t[0:32, i * 128:(i + 1) * 128], comb[:, i, :], ident)
                tc = P.copy(combT, b.t[0:32, 0:256], t)
                b.freed = [tc]
                hfree = [None, None]
                hready = [None, None]

                def up(e):
                    wg, wu = tile("g", e), tile("u", e)
                    b, free = P.bank()
                    t = P.mm(b.t[:, 0:256], [(ident[0:32, e:e + 1].to_broadcast([32, 128]), combT)], free, tc)
                    tcb = P.copy(cb[:, e % 2, :], b.t[:, 0:256], t, P.last("dve"), eng="act")
                    b.freed = [tcb]
                    for f in range(4):
                        b, free = P.bank()
                        P.mm(b.t[:, 0:256], [(at_k(wg, k)[:, f * 128:(f + 1) * 128], vT[:, k, :]) for k in range(8)], free, loaded(wg))
                        t2 = P.mm(b.t[:, 256:512], [(at_k(wu, k)[:, f * 128:(f + 1) * 128], vT[:, k, :]) for k in range(8)], loaded(wu))
                        t = P.act(sl[:, f % 2, :], b.t[:, 0:256], ACT.Silu, t2, P.last("dve"))
                        o = hT[:, e % 2, f, :]
                        t3 = P.tt(o, b.t[:, 256:512], cb[:, e % 2, :], ALU.mult, tcb, t, hfree[e % 2])
                        b.freed = [t, t3]
                        hready[e % 2] = P.tt(o, o, sl[:, f % 2, :], ALU.mult, t)
                    release(wg + wu, t2)

                def down(e):
                    wd = tile("d", e)
                    P.wait("pe", [loaded(wd), hready[e % 2]])
                    for i in range(2):
                        for c in range(2):
                            t = P.mm(Y[2 * i + c].t[:, :],
                                     [(hT[:, e % 2, f, i * 128:(i + 1) * 128], at_k(wd, f)[:, c * 512:c * 512 + 512]) for f in range(4)],
                                     start=e == 0, stop=e == 31)
                    hfree[e % 2] = t
                    release(wd, t)
                    return t

                for e in range(33):
                    if e < 32:
                        up(e)
                    if e > 0:
                        ty = down(e - 1)
                finish(ty)

            def sparse():
                tile = stream()
                tG = []
                for e in range(0, 32, 8):
                    for i in range(2):
                        tg8 = P.tt(big[:, i, e:e + 8, :], bc(C("iota"), 1, 8), bc(key[:, i, e:e + 8], 2, 64), ALU.is_equal)
                    tG.append(tg8)
                L = {}

                def gather(p):
                    for k0 in (0, 4):
                        b, free = P.bank()
                        P.wait("pe", [free, tG[p // 4]])
                        for k in range(4):
                            t = P.mm(b.t[:, k * 128:(k + 1) * 128],
                                     [(xs[:, i, (k0 + k) * 128:(k0 + k + 1) * 128],
                                       big[:, i, 2 * p:2 * p + 2, :].rearrange("p e j -> p (e j)")) for i in range(2)])
                        b.freed = [P.tt(ve[:, p % 2, k0:k0 + 4, :], b.t[:, :].rearrange("p (k j) -> p k j", k=4),
                                          bc(S("gffn")[:, k0:k0 + 4], 2, 128), ALU.mult, t, L.get(("up", p - 2)))]
                    L["v", p] = b.freed

                def up(p):
                    P.wait("pe", [L["v", p]])
                    bs_ = []
                    for n in "gu":
                        b, free = P.bank()
                        w = [tile(n, 2 * p + a) for a in range(2)]
                        P.wait("pe", [free, loaded(w[0] + w[1])])
                        for k in range(8):
                            for a in range(2):
                                o = slice(64 * a, 64 * a + 64)
                                t = P.mm(b.t[o, :], [(ve[:, p % 2, k, o], at_k(w[a], k))], start=k == 0, stop=k == 7)
                        release(w[0] + w[1], t)
                        bs_.append((b, t))
                    (g, tg_), (u, tu_) = bs_
                    L["up", p] = tu_
                    t = P.act(sl, g.t[:, :], ACT.Silu, tg_, L.get(("h", p - 1)))
                    g.freed = [t]
                    L["h", p] = P.tt(hp[p % 2], u.t[:, :], sl, ALU.mult, tu_, t, L.get(("turned", p - 2)))
                    u.freed = [L["h", p]]

                def turn(p):
                    b, free = P.bank()
                    P.wait("pe", [free, L["h", p]])
                    for f in range(4):
                        t = P.tr(b.t[:, f * 128:(f + 1) * 128], hp[p % 2][:, f * 128:(f + 1) * 128], ident, inc=f == 3)
                    L["turned", p] = t
                    L["hT", p] = P.copy(hT[:, p % 2, :], b.t[:, :], t, L.get(("down", p - 2)), eng="act")
                    b.freed = [L["hT", p]]

                def down(p):
                    w = [tile("d", 2 * p + a) for a in range(2)]
                    P.wait("pe", [L["hT", p], loaded(w[0] + w[1])])
                    for c in range(2):
                        b, free = P.bank()
                        P.wait("pe", [free])
                        for f in range(4):
                            for a in range(2):
                                o = slice(64 * a, 64 * a + 64)
                                t = P.mm(b.t[o, :], [(hT[:, p % 2, f * 128 + 64 * a:f * 128 + 64 * a + 64],
                                                      at_k(w[a], f)[:, c * 512:c * 512 + 512])], start=f == 0, stop=f == 3)
                        b.freed = [P.copy(yk[:, p % 2, c * 512:c * 512 + 512], b.t[:, :], t, L.get(("put", p - 2)),
                                            eng="act")]
                    release(w[0] + w[1], t)
                    L["down", p] = t
                    L["y", p] = b.freed

                def weights(p):
                    gw = gwt[:, p % 2]
                    t = P.tt(gw, big[:, :, 2 * p:2 * p + 2, :], bc(comb[:, :, 2 * p:2 * p + 2], 3, 64), ALU.mult, tG[p // 4],
                             L.get(("wturned", p - 2)), eng="pool")
                    b, free = P.bank()
                    P.wait("pe", [free, t])
                    for i in range(2):
                        t = P.tr(b.t[:, i * 128:(i + 1) * 128], gw[:, i].rearrange("p e j -> p (e j)"), ident)
                    L["wturned", p] = t
                    t = P.copy(sw[:, p % 2, :], b.t[:, 0:256], t, L.get(("put", p - 2)), eng="dve")
                    b.freed = [t]
                    L["sw", p] = t

                def put_back(p):
                    P.wait("pe", [L["sw", p], L["y", p]])
                    for i in range(2):
                        for c in range(2):
                            t = P.mm(Y[2 * i + c].t[:, :],
                                     [(sw[:, p % 2, i * 128:(i + 1) * 128], yk[:, p % 2, c * 512:c * 512 + 512])],
                                     start=p == 0, stop=p == 15)
                    L["put", p] = t
                    return t

                gather(0)
                for p in range(18):
                    if p < 15:
                        gather(p + 1)
                    if p < 16:
                        up(p)
                    if p >= 2:
                        ty = put_back(p - 2)
                    if p < 16:
                        weights(p)
                    if 1 <= p <= 16:
                        down(p - 1)
                    if p < 16:
                        turn(p)
                finish(ty)

            ve = vT[:, :, :].rearrange("p k t -> p (k t)").rearrange("p (a k j) -> p a k j", a=2, k=8)
            gwt = bP[:, 0, :].rearrange("p (a i e j) -> p a i e j", a=2, i=2, e=2)
            sw = bP[:, 1, :].rearrange("p (a t) -> p a t", a=2)
            sl, hp, hT = bS[:, 0, :], (bS[:, 1, :], bP[:, 2, :]), bT[:, 0:2, :]
            yk = grow
            P.barrier()
            P.ring = Ring(P.banks[4:8])
            start = (list(slots), at[0], list(slot_n), list(released))
            ends_ = []

            def side(f):
                def g():
                    slots[:], at[0], slot_n[:], released[:] = list(start[0]), start[1], list(start[2]), list(start[3])
                    P.ring.at = 0
                    for b in P.ring.banks:
                        b.freed = []
                    f()
                    ends_.append((at[0], list(slot_n)))
                return g

            P.branch(flag[:, :], CAP, side(dense), side(sparse), tflag)
            assert ends_[0] == ends_[1]
            released[:] = [[P.last(e) for e in ("pe", "act", "dve", "pool")]] * (NSLOT + XSLOT)
            cut = at[0] % len(slots)
            slots[:] = [n for n in slots[cut:] + slots[:cut] if n < NSLOT]
            at[0] = 0
            P.ring = Ring(P.banks)
            for b in P.banks:
                b.freed = []
            P.barrier()

        def row_bcast(dst, col, *after, eng="act"):
            dv = dst.rearrange("p (n k) -> p k n", k=8)
            for k0 in (0, 4):
                b, free = P.bank()
                P.wait("pe", [free, after])
                for k in range(4):
                    t = P.mm(b.t[:, k * 128:(k + 1) * 128], [(col(k0 + k).to_broadcast([128, 128]), ident)])
                b.freed = [P.copy(dv[:, k0:k0 + 4, :], b.t[:, :].rearrange("p (k n) -> p k n", k=4), t, eng=eng)]
            return b.freed

        grown = bP[:, 0:2, :].rearrange("p a n -> p (a n)")

        def final_norm(g, dst, tg_, t):
            for i in range(2):
                t = P.stt(dst(i), h[:, i, :], rs[:, i:i + 1], grown, ALU.mult, ALU.mult, t, tg_)
            return t

        t = rsqrt(0, 2, squares([h[:, 0, :], h[:, 1, :]], 0, P.last("dve")))
        td = {i: diag(i, i, tctx) for i in (2, 3)}
        tg_ = row_bcast(grown, lambda k: S("gfin")[:, k:k + 1], P.last("dve"), eng="dve")

        def modulated(A, B, l, which, td):
            return norm_T([(i, h[:, i, :], td[i]) for i in which], A, B, lambda i: Amod[:, l, i // 2, :],
                          lambda i: mod[:, l, 0:8, i // 2])

        def gated_by(ZO):
            def gated(i, c0):
                def f(ps, r, t, tr):
                    o = ZO[:, i, c0:c0 + 64]
                    return P.stt(o, ps, r, o, ALU.mult, ALU.mult, t, tr)
                return f
            return gated

        tsq = {}

        def residual(i, c, ps, t):
            o = h[:, i, c * 512:c * 512 + 512]
            t = P.tt(bS[:, 0, :], ps, grow[:, i // 2, c * 512:c * 512 + 512], ALU.mult, t)
            th = P.tt(o, o, bS[:, 0, :], ALU.add)
            if c == 1:
                tsq[i] = P.act(xs[:, 0, :], h[:, i, :], ACT.Square, th, scale=1.0 / 32.0, acc=ss[:, i:i + 1])
            return t

        ab = P.sb(ctx, "ab1", [128, 2, 2, SLOT], F32R)
        entries = []
        for n in ("cq", "kva", "qa", "za", "zb"):
            entries += tiles_of(n, d["w_" + n])
        entries += square("out", d["ab_out_w"])
        for j in range(8):
            entries += tiles_of(f"c{j}", d["w_c"][j])
        stream = Stream(entries + square("cout", d["c_out_w"]), ab, "pool")

        with ExitStack() as sc:
            ZO = P.sb(sc, "ZO", [128, 4, 1024])
            with ExitStack() as sa:
                cq = P.sb(sa, "cq", [128, 4, 416])
                vb = P.sb(sa, "vb", [128, 4, 8, 64])
                vbf = vb[:, :, :, :].rearrange("p i h r -> p (i h r)")
                ck = vbf[:, 0:1024].rearrange("p (i n) -> p i n", i=4)
                ka, va = (vbf[:, n:n + 512].rearrange("p (i n) -> p i n", i=4) for n in (1024, 1536))
                qa = P.sb(sa, "qa", [128, 4, 512])
                kd = bS[:, 0, 0:256].rearrange("p (g a r) -> p g a r", g=2, a=2)
                krp = P.sb(sa, "krp", [128, 4, 32])
                U = ExitStack()
                UA, UB = (P.sb(U, n, [128, 8, 512], F32R) for n in ("UA", "UB"))
                stream.ahead("pool")
                t = final_norm("gfin", lambda i: h[:, i, :], tg_, t)
                stream.ahead("dve", 2)
                tlat = rsqrt(4, 2, squares([h[:, 0, :], h[:, 1, :]], 4, t))
                modulated(UA, UB, 0, (2,), td)
                td.update({i: diag(i, 4 + i, tlat) for i in (0, 1)})
                tuc = modulated(UA, UB, 0, (3,), td)
                tu = modulated(UA, UB, 0, (0, 1), td)
                T4 = (2, 3, 0, 1)

                lin_by(stream, "cq", UA, UB, 416, (((2, 3), tuc), ((0, 1), tu)),
                       lambda i, ps, t: P.copy(cq[:, i, :], ps, t, eng="act"))
                def put(i, ps, t):
                    P.copy(ka[:, i, :], ps[:, 0:128], t, eng="dve")
                    P.copy(va[:, i, :], ps[:, 128:256], t, eng="dve")
                    return P.copy(ck[:, i, :], ps[:, 256:512], t, eng="dve")
                lin(stream, "kva", UA, UB, 512, T4, put)
                lin(stream, "qa", UA, UB, 512, T4, lambda i, ps, t: P.copy(qa[:, i, :], ps, t))

                def rope_pairs(x1, x2, i, ca, sa_, n, r, dst1=None, dst2=None):
                    co = bc(C(ca).rearrange("p (i r) -> p i r", i=4)[:, i, :], 1, n)
                    si = bc(C(sa_).rearrange("p (i r) -> p i r", i=4)[:, i, :], 1, n)
                    tm = [rt[:, m_, 0:n * r].rearrange("p (h r) -> p h r", h=n) for m_ in range(4)]
                    P.tt(tm[0], x1, co, ALU.mult)
                    P.tt(tm[1], x2, si, ALU.mult)
                    P.tt(tm[2], x1, si, ALU.mult)
                    P.tt(tm[3], x2, co, ALU.mult)
                    P.tt(x1 if dst1 is None else dst1, tm[0], tm[1], ALU.subtract)
                    return P.tt(x2 if dst2 is None else dst2, tm[2], tm[3], ALU.add)

                P.wait("dve", [P.last("act")])
                P.op("dve", lambda e: e.tensor_copy(krp[:, :, :], cq[:, :, 384:416]))
                rstd([cq[:, i, 0:384] for i in range(4)], 384, 4)
                t = rstd([ck[:, i, :] for i in range(4)], 256, 4, c0=4)
                for i in range(4):
                    P.ts(cq[:, i, 0:384], cq[:, i, 0:384], rs[:, i:i + 1], None, ALU.mult, None, t)
                    P.ts(ck[:, i, :], ck[:, i, :], rs[:, 4 + i:5 + i], None, ALU.mult, None, t)
                    v = krp[:, i:i + 1, :].rearrange("p h (r a) -> p h r a", a=2)
                    rope_pairs(v[:, :, :, 0], v[:, :, :, 1], i, "cosb", "sinb", 1, 16)
                for i in range(4):
                    v = qa[:, i, :].rearrange("p (h r a) -> p h r a", h=8, a=2)
                    rope_pairs(v[:, :, :, 0], v[:, :, :, 1], i, "cosa", "sina", 8, 32)
                    v = ka[:, i, :].rearrange("p (h r a) -> p h r a", h=2, a=2)
                    rope_pairs(v[:, :, :, 0], v[:, :, :, 1], i, "cosa", "sina", 2, 32)
                for wh in range(2):
                    row_bcast(grow[:, wh, :], lambda k: mod[:, 0, 16 + k, wh:wh + 1])
                lin(stream, "za", UA, UB, 512, T4, lambda i, ps, t: P.act(ZO[:, i, 0:512], ps, ACT.Silu, t))
                lin(stream, "zb", UA, UB, 512, T4, lambda i, ps, t: P.act(ZO[:, i, 512:1024], ps, ACT.Silu, t))
                P.barrier()
                U.close()
                kaT = xs[:, :, :].rearrange("p hp (g t) -> p hp g t", g=2)
                for hp in range(2):
                    tz = P.op("pool", lambda e, hp=hp: e.memset(kaT[64 - 64 * hp:128 - 64 * hp, hp, :, :], 0.0),
                              P.last("dve"))
                qaT = P.sb(sa, "qaT", [128, 4, 512])
                qbT = P.sb(sa, "qbT", [128, 8, 512])
                tzq = P.op("pool", lambda e: e.memset(qbT[96:128, :, :], 0.0))

                def kbT(hh):
                    return (qa if hh < 4 else qaT)[:, hh % 4, :]

                tkd = None
                for i in range(4):
                    for a in range(2):
                        t = P.op("dve", lambda e, a=a, i=i: e.tensor_copy(
                            kd[:, :, a, :], ka[:, i, :].rearrange("p (g r) -> p g r", g=2)), tkd)
                    to_T(lambda k: qa[:, i, k * 128:(k + 1) * 128], 4,
                         lambda k0, n, ps, t: P.copy(qaT[:, :, i * 128:(i + 1) * 128], ps, t), t)
                    tkd = to_T(lambda k: kd[:, k, :, :].rearrange("p a r -> p (a r)"), 2,
                               lambda k0, n, ps, t: own_half(kaT, slice(0, 2), i, ps, t), t)
                cqT = P.sb(sa, "cqT", [128, 3, 512])
                ckT = P.sb(sa, "ckT", [128, 2, 512])
                for i in range(4):
                    to_T(lambda k: cq[:, i, 0:384].rearrange("p (d k) -> p k d", k=3)[:, k, :], 3,
                         lambda k0, n, ps, t: P.tt(cqT[:, :, i * 128:(i + 1) * 128], ps, bc(S("qng"), 2, 128), ALU.mult, t))
                    tck = to_T(lambda k: ck[:, i, :].rearrange("p (d k) -> p k d", k=2)[:, k, :], 2,
                               lambda k0, n, ps, t: P.tt(ckT[:, :, i * 128:(i + 1) * 128], ps, bc(S("kvng"), 2, 128), ALU.mult, t))
                tcq = P.last("dve")
                te = [P.last("act"), P.last("dve"), tz]
                nsink = rs
                P.ts(nsink[:, :], S("sink"), -1.0, None, ALU.mult, None)

                rows = cq[:, :, :].rearrange("p i n -> p (i n)")[:, 0:1536].rearrange("p (i h r) -> p i h r", i=4, h=4)

                def head_T(dst, hh, *after):
                    b, free = P.bank()
                    P.wait("pe", [free, after])
                    for i in range(4):
                        t = P.tr(b.t[0:96, i * 128:(i + 1) * 128], rows[:, i, hh, :], ident, inc=i == 3)
                    b.freed = [P.copy(dst[0:96, :], b.t[0:96, :], t, eng="dve")]
                    return t

                trow_ = [None]

                def low_rank_queries():
                    w = fetch_all(d["b_w_uq"].rearrange("(p k) n -> p k n", k=3))
                    for c in range(2):
                        for i in range(4):
                            b, free = P.bank()
                            t = P.mm(b.t[:, 0:384], [(cqT[:, k, i * 128:(i + 1) * 128], at_k(w, k)[:, c * 384:c * 384 + 384]) for k in range(3)],
                                     loaded(w), free, tcq)
                            yield
                            b.freed = [P.copy(rows[:, i, :, :], b.t[:, 0:384].rearrange("p (h r) -> p h r", h=4), t,
                                              trow_[0], tck, eng="dve")]
                            v = rows[:, i, :, 64:96].rearrange("p h (r a) -> p h r a", a=2)
                            tr_ = rope_pairs(v[:, :, :, 0], v[:, :, :, 1], i, "cosb", "sinb", 4, 16)
                            yield
                        for hh in range(4):
                            trow_[0] = head_T(qbT[:, 4 * c + hh, :], hh, tr_)
                            yield
                    release(w, t)

                units = []
                for i in range(4):
                    for hh in range(8):
                        g = hh // 4
                        k0, nk = (0, 512) if i < 2 else (256, 256)
                        units.append({
                            "after": te, "scale": 0.125, "put": gated_by(ZO)(i, hh * 64), "nk": nk,
                            "qk": [(0, nk, qaT[:, hh // 2, i * 128:(i + 1) * 128], kaT[:, hh % 2, g, k0:k0 + nk])], "sink": S("sink")[:, hh:hh + 1], "nsink": nsink[:, hh:hh + 1],
                            "peak": peak_masked(C("amask")[:, i * 512:(i + 1) * 512]) if i < 2 else peak,
                            "v": [va[:, j, g * 64:g * 64 + 64] for j in range(k0 // 128, 4)]})
                rest = low_rank_queries()
                attend(units, rest)
                for _ in rest:
                    pass

                tz = [tzq] + [P.op("pool", lambda e, x=x: e.memset(x[96:128, :, :], 0.0), P.last("pe")) for x in (qa, qaT)]
                trow = trow_[0]
                w = fetch_all(d["b_w_ukv"].rearrange("(p k) n -> p k n", k=2))
                for c in range(2):
                    for i in range(4):
                        b, free = P.bank()
                        t = P.mm(b.t[:, :], [(ckT[:, k, i * 128:(i + 1) * 128], at_k(w, k)[:, c * 512:c * 512 + 512]) for k in range(2)],
                                 loaded(w), free)
                        ps = b.t[:, :].rearrange("p (h a r) -> p h a r", h=4, a=2)
                        P.copy(rows[:, i, :, 0:64], ps[:, :, 0, :], t, trow, eng="dve")
                        b.freed = [P.copy(vb[:, i, 4 * c:4 * c + 4, :], ps[:, :, 1, :], t, eng="dve")]
                        tr_ = P.op("dve", lambda e, i=i: e.tensor_copy(rows[:, i, :, 64:96], bc(krp[:, i, :], 1, 4)))
                    trow = None
                    for hh in range(4):
                        trow = head_T(kbT(4 * c + hh), hh, tr_)
                release(w, t)
                te = [P.last("act"), P.last("dve"), tz]
                units = []
                for i in range(4):
                    for hh in range(8):
                        k0, nk = (0, 512) if i < 2 else (256, 256)
                        units.append({
                            "after": te, "scale": 96.0 ** -0.5, "put": gated_by(ZO)(i, 512 + hh * 64), "nk": nk,
                            "qk": [(0, nk, qbT[:, hh, i * 128:(i + 1) * 128], kbT(hh)[:, k0:k0 + nk])],
                            "peak": peak, "v": [vb[:, j, hh, :] for j in range(k0 // 128, 4)]})
                attend(units)
                P.barrier()

            mA, mB = (P.sb(sc, n, [128, 8, 512], F32R) for n in ("mA", "mB"))
            tz = P.last("dve")
            for i in range(4):
                to_T(lambda k: ZO[:, i, :].rearrange("p (d k) -> p k d", k=8)[:, k, :], 8,
                     lambda k0, n, ps, t: halves(ps, *(o[:, k0:k0 + n, i * 128:(i + 1) * 128] for o in (mA, mB)), t), tz)
            te = [P.last("act"), P.last("dve")]
            for c in range(2):
                lin(stream, f"out{c}", mA, mB, 512, range(4), lambda i, ps, t: residual(i, c, ps, t), te)
            t = rsqrt(0, 2, tsq[1])
            td = {i: diag(i, i, t) for i in (0, 1)}
            P.barrier()

        with ExitStack() as sc:
            stream.eng = "dve"
            UA, UB = (P.sb(sc, n, [128, 8, 512], F32R) for n in ("UA1", "UB1"))
            qcT = P.sb(sc, "qcT", [128, 2, 8, 256])
            t = rsqrt(2, 2, tsq[3])
            td.update({i: diag(i, i, t) for i in (2, 3)})
            tul = modulated(UA, UB, 1, (0, 1), td)
            stream.ahead("dve", 2)
            tu = modulated(UA, UB, 1, (2, 3), td)
            kcT2 = P.sb(sc, "kcT2", [128, 8, 512])
            vc2 = P.sb(sc, "vc2", [128, 2, 1024])
            vcr = [rt[:, :, :].rearrange("p a b -> p (a b)"), grow[:, 1, :], vc2[:, 0, :], vc2[:, 1, :]]
            ZO = xs

            def own(j, ps, t):
                for hp in range(2):
                    o = slice(64 * hp, 64 * hp + 64)
                    t = P.copy(qcT[o, hp, j, :], ps[o], t, eng="act")
                return t
            linT(stream, "c0", UA, UB, 256, lambda j, ps, t: own(j, ps, t), tul)
            linT(stream, "c1", UA, UB, 256, lambda j, ps, t: own(4 + j, ps, t))
            for hp in range(2):
                tz = P.op("pool", lambda e, hp=hp: e.memset(qcT[64 - 64 * hp:128 - 64 * hp, hp, :, :], 0.0))
            for c in range(2):
                linT(stream, f"c{2 + c}", UA, UB, 512, lambda j, ps, t: P.copy(kcT2[:, 4 * c + j, :], ps, t), tu)
            for c in range(2):
                lin(stream, f"c{4 + c}", UA, UB, 512, range(4), lambda i, ps, t: P.copy(vcr[i][:, c * 512:c * 512 + 512], ps, t))
            for c in range(2):
                lin(stream, f"c{6 + c}", UA, UB, 512, range(2), lambda i, ps, t: P.act(ZO[:, i, c * 512:c * 512 + 512], ps, ACT.Silu, t))
            row_bcast(grow[:, 0, :], lambda k: mod[:, 1, 16 + k, 0:1], P.last("dve"))
            te = [P.last("act"), P.last("dve"), tz]

            def peak_biased(bias, c):
                def f(x, s, m, t):
                    P.ttr(s[:, 0:256], x[:, 0:256], bias, -3e38, ALU.add, ALU.max, m[:, 0:1], t, tb[c])
                    t = P.red(m[:, 4:5], x[:, 256:512], ALU.max)
                    return [s[:, 0:256], x[:, 256:512]], t, [t]
                return f

            tiles_ = []
            for c in range(4):
                w = fetch(d["bias"][c // 2][:, 4 * (c % 2):4 * (c % 2) + 4, :])
                units = []
                for hh in range(4 * c, 4 * c + 4):
                    for i in range(2):
                        units.append({
                            "after": te, "scale": 0.125, "put": gated_by(ZO)(i, hh * 64), "nk": 512,
                            "qk": [(0, 512, qcT[:, hh % 2, hh // 2, i * 128:(i + 1) * 128], kcT2[:, hh // 2, :])],
                            "peak": peak_biased(w.v[:, hh % 4, i * 256:(i + 1) * 256], c),
                            "v": [vcr[j][:, hh * 64:hh * 64 + 64] for j in range(4)]})
                tiles_.append((w, units))
            tb = {}

            def biases():
                for c, (w, _) in enumerate(tiles_):
                    v = w.v.rearrange("p h (r k) -> p (h r) k", k=64)
                    tb[c] = P.stt(v, v, 8.0, bc(C("colmask"), 1, 32), ALU.mult, ALU.add, w.tok)
                    yield
                    yield

            work = biases()
            next(work)
            attend([u for _, us in tiles_ for u in us], work)
            for w, _ in tiles_:
                release([w], P.last("dve"))
            tz = P.last("dve")
            tg_ = row_bcast(grown, lambda k: S("fin2")[:, k:k + 1], tz)
            for i in range(2):
                to_T(lambda k: ZO[:, i, :].rearrange("p (d k) -> p k d", k=8)[:, k, :], 8,
                     lambda k0, n, ps, t: halves(ps, *(o[:, k0:k0 + n, i * 128:(i + 1) * 128] for o in (UA, UB)), t), tz)
            te = [P.last("act"), P.last("dve")]
            for c in range(2):
                lin(stream, f"cout{c}", UA, UB, 512, range(2), lambda i, ps, t: residual(i, c, ps, t), te)
            t = rsqrt(0, 2, tsq[1])
            t = final_norm("fin2", lambda i: xs[:, i, :], tg_, t)
            o = out.rearrange("o (t p) d -> p (o t) d", p=128)
            tf = P.dma("sp", o, xs[:, :, :], "out", s_out, 16, t)
            P.wait("sp", [tf])
            P.barrier()

        block = ctx.enter_context(nc.Block())

        @block.tensor
        def _(e):
            P.emit(e, P.q["pe"])

        @block.scalar
        def _(e):
            P.emit(e, P.q["act"])

        @block.vector
        def _(e):
            P.emit(e, P.q["dve"])

        @block.gpsimd
        def _(e):
            P.emit(e, P.q["pool"])

        @block.sync
        def _(e):
            P.emit(e, P.q["sp"])


def constants():
    f = np.float32
    p = np.arange(128)
    o = {"ident": np.eye(128)}
    o["inv"] = np.tile((f(1.0) / (f(10000.0) ** (np.arange(32, dtype=f) / f(32)))).astype(f), (128, 1))
    o["causal"] = np.concatenate([np.zeros((128, 128)), np.where(p[None, :] <= p[:, None], 0.0, NEG)], 1)
    t = p[:, None, None] + 128 * np.arange(2)[None, :, None]
    ok = (16 * np.arange(15) + 31)[None, None, :] <= t
    o["cmpadd"] = np.where(ok, 0.0, NEG)
    o["cmpok"] = ok * 1.0
    k = np.arange(512)[None, None, :]
    o["amask"] = np.where((np.abs(k - t) <= 128) | (k >= 256), 0.0, NEG)
    lev = []
    s, q = p[:, None], p[None, :]
    for m in LEVELS:
        lev.append((s // (2 * m) == q // (2 * m)) & (s // m % 2 == 0) & (q // m % 2 == 1))
    lev.append(s == q)
    o["lev"] = np.stack(lev, 1) * 1.0
    qc, kc = (p % 64)[:, None], np.arange(64)[None, :]
    cs = np.clip(qc - 8, 0, 48)
    o["colmask"] = np.where((kc >= cs) & (kc < cs + 16), 0.0, NEG)
    tok = p[:, None] + 128 * np.arange(2)[None, :]
    for name, d in (("a", 64), ("b", 32)):
        n = d // 4
        inv = (f(10000.0) ** (-np.arange(n, dtype=f) / f(n))).astype(f)
        row, col = (tok // 64).astype(f), (tok % 64).astype(f)
        ang = np.concatenate([row[..., None] * inv, col[..., None] * inv], -1).astype(f)
        one = np.zeros((128, 2, 2 * n), f)
        o["cos" + name] = np.concatenate([np.cos(ang), one + 1], 1)
        o["sin" + name] = np.concatenate([np.sin(ang), one], 1)
    o["desc"] = np.tile(np.arange(8, 0, -1), (128, 1))
    o["before"] = (s < q) * 1.0
    o["ones"] = np.ones((128, 128))
    o["iota"] = np.tile(np.arange(1, 65), (128, 1))
    o["pick"] = (p[:, None] % 32 == np.arange(2)[None, :]) * 1.0
    hn = np.arange(120)
    o["fold"] = (p[:, None] % 32 == np.arange(30)[None, :]) * 1.0
    o["sel"] = (p[:, None] == hn[None, :] % 15) * 1.0
    o["bd"] = (p[:, None] // 15 == np.arange(8)[None, :]) * 1.0
    o["minus"] = np.full((128, 1), -1.0)
    o["nhalf"] = np.full((128, 16), -0.5)
    return np.concatenate([np.asarray(o[n], f).reshape(128, w) for n, w in CONST], 1)


def tiles(w, k, *cols):
    w = w.reshape(128, k, w.shape[1])
    return np.ascontiguousarray(np.concatenate([w[:, :, c] for c in cols], 2))


def kernel(**inputs):
    import concourse.bacc as _bacc
    from concourse import mybir as _mybir
    from concourse.bass_utils import run_bass_kernel_spmd as _run

    a = {k: np.asarray(v) for k, v in inputs.items()}
    f = np.float32
    w_in = a["w_in"][0]
    c = np.cumsum([0, 512, 128, 128, 128, 128, 128, 128, 24, 256, 256, 512, 16, 512, 1024, 1024])
    col = [slice(c[i], c[i + 1]) for i in range(15)]
    ab = a["ab_in_w_2"][0]
    cin = a["c_in_w_2"][0]

    def kmaj(v, k):
        return v.reshape(128, k)

    def tmaj(v, k):
        return v.reshape(k, 128).T

    def rep(v):
        return np.broadcast_to(v.reshape(1, -1), (128, v.size))

    def pairs(pos):
        return pos.reshape(16, 128).T

    def half(s, n):
        return slice(s.start + n * 64, s.start + n * 64 + 64)

    wr = np.concatenate([a["w_grp"][0], a["w_exp"][0]], 1).reshape(128, 288)
    wa2 = np.zeros((128, 256), f)
    wa2[0:16] = a["gla_w_a2"][0]
    small = {
        "gmix": kmaj(a["g_mix"][0], 8), "gffn": kmaj(a["g_ffn"][0], 8), "gfin": kmaj(a["g_final"], 8),
        "ng0": kmaj(a["norm_g_2"][0], 8), "ng1": kmaj(a["norm_g_2"][1], 8), "fin2": kmaj(a["final_g_2"], 8),
        "qng": kmaj(a["b_q_norm_g_2"][0], 3), "kvng": kmaj(a["b_kv_norm_g_2"][0], 2),
        "glang": kmaj(a["gla_norm_g"][0], 4), "b1k": tmaj(a["cmp_b1_k"][0], 2), "b1v": tmaj(a["cmp_b1_v"][0], 2),
        "glaba": tmaj(a["gla_b_a"][0], 2),
        "cc": np.stack([kmaj(a["c_2"][0], 8), kmaj(a["c_ctx_2"], 8)], 2).reshape(128, 16),
        "adab": a["ada_b_2"].reshape(2, 3, 128, 8).transpose(2, 0, 1, 3).reshape(128, 48),
        "posk": pairs(a["cmp_pos_k"][0]), "posv": pairs(a["cmp_pos_v"][0]),
        "w2k": a["cmp_w2_k"][0].reshape(2, 128, 64).transpose(1, 0, 2).reshape(128, 128),
        "w2v": a["cmp_w2_v"][0].reshape(2, 128, 64).transpose(1, 0, 2).reshape(128, 128),
        "wr": wr, "wa2": wa2, "b2k": rep(a["cmp_b2_k"][0]), "b2v": rep(a["cmp_b2_v"][0]),
        "brout": np.concatenate([rep(a["b_grp"][0]), rep(a["b_exp"][0])], 1), "sink": rep(a["a_sink_2"][0]),
    }
    pos = a["positions"][0]
    ends = np.zeros(128, np.int64)
    ends[0:15] = 16 * np.arange(15) + 31
    t = np.arange(256)
    dr = t[None, :] // 64 - t[:, None] // 64 + 7
    dc = np.clip(t[None, :] % 64 - t[:, None] % 64 + 15, 0, 30)
    bias = a["c_rpb_2"][0][:, dr, dc].reshape(2, 8, 2, 128, 256).transpose(0, 3, 1, 2, 4).reshape(2, 128, 8, 512)

    def pos_tile(w):
        return np.ascontiguousarray(w.reshape(16, 128, 256).transpose(1, 0, 2))

    ada = a["ada_w_2"].reshape(2, 128, 8, 3, 128, 8).transpose(0, 3, 5, 1, 2, 4)
    ada = ada.reshape(2, 6, 4, 128, 8, 128).transpose(0, 1, 3, 4, 2, 5).reshape(2, 6, 128, 8, 512)
    send = {
        "const": constants(),
        "small": np.concatenate([np.asarray(small[n]).reshape(128, w) for n, w in SMALL], 1),
        "pos": np.stack([pos[0:128], pos[128:256], pos[ends]], 1),
        "x": a["x"], "ctx": a["ctx_2"],
        "w_gqk": tiles(w_in, 8, col[8], col[9]), "w_sm": tiles(w_in, 8, col[7], col[11]),
        "w_gv": tiles(w_in, 8, col[10]), "w_q": tiles(w_in, 8, col[0]),
        "w_kv": tiles(w_in, 8, col[3], col[5], col[4], col[6]),
        "w_kvc": tiles(w_in, 8, *[half(col[m], g) for m in (1, 2) for g in (0, 0, 1, 1)]),
        "w1k": pos_tile(a["cmp_w1_k"][0]), "w1v": pos_tile(a["cmp_w1_v"][0]),
        "w_gr": tiles(w_in, 8, col[12]),
        "w_m": np.stack([tiles(w_in, 8, slice(c[13] + 512 * j, c[13] + 512 * j + 512)) for j in range(4)]),
        "w_proj_nsa": a["w_proj_nsa"][0], "w_proj_gla": a["w_proj_gla"][0], "w_out": a["w_out"][0],
        "w_gate": a["w_gate"][0], "w_up": a["w_up"][0], "w_down": a["w_down"][0],
        "w_ada": np.ascontiguousarray(ada),
        "w_qa": tiles(ab, 8, slice(0, 512)),
        "w_kva": tiles(ab, 8, slice(512, 768), slice(1664, 1920)),
        "w_za": tiles(ab, 8, slice(768, 1280)), "w_zb": tiles(ab, 8, slice(1952, 2464)),
        "w_cq": tiles(ab, 8, slice(1280, 1664), slice(1920, 1952)),
        "b_w_uq": a["b_w_uq_2"][0], "b_w_ukv": a["b_w_ukv_2"][0], "ab_out_w": a["ab_out_w_2"][0],
        "w_c": np.stack([tiles(cin, 8, slice(512 * j, 512 * j + 512)) for j in range(8)]),
        "bias": np.ascontiguousarray(bias), "c_out_w": a["c_out_w_2"][0],
    }
    nc = _bacc.Bacc("TRN2", target_bir_lowering=False, num_devices=1)
    arrays, d = {}, {}
    for name, v in send.items():
        v = np.ascontiguousarray(v)
        arrays[f"in_{name}"] = v
        d[name] = nc.dram_tensor(f"in_{name}", v.shape, _mybir.dt.from_np(v.dtype), kind="ExternalInput").ap()
    out = nc.dram_tensor("out_0", (1, 256, 1024), _mybir.dt.float32, kind="ExternalOutput").ap()
    build(nc, d, out)
    r = _run(nc, [arrays], core_ids=[0])
    return r.results[0]["out_0"]
```
